# Optimizing a Trainium2 kernel written in Bass

```python
import jax, jax.numpy as jnp
from jax import lax
import numpy as np

D_MODEL = 1024
BATCH = 1
SEQ = 256
DEPTH = 1

HEAD_DIM = 64
DIL_GROUPS = ((128, 1), (512, 4), (2048, 16))
DIL_HEADS_PER_GROUP = 4
DIL_HEADS = DIL_HEADS_PER_GROUP * len(DIL_GROUPS)
DIL_OUT = DIL_HEADS_PER_GROUP * HEAD_DIM
SB_HEADS = 8
SB_OUT = SB_HEADS * HEAD_DIM
ROPE_THETA = 500000.0
ROPE_DIMS = HEAD_DIM // 4
Q_BLOCK = 128
N_EXPERTS = 32
TOP_K = 4
D_EXPERT = D_MODEL
SWIGLU_ALPHA = 1.702
SWIGLU_LIMIT = 7.0
MOE_BLOCK = 256
NORM_EPS = 1e-6
NEG_INF = -1e30
IN_COLS = 3 * DIL_HEADS * HEAD_DIM + 3 * SB_HEADS * HEAD_DIM + 2 * D_MODEL

kernel_name = "hybrid_dilated_stickbreaking_moe_layer"

def rms_norm(x, gain):
    xf = x.astype(jnp.float32)
    y = xf * lax.rsqrt(jnp.mean(xf * xf, axis=-1, keepdims=True) + NORM_EPS)
    return (y * gain.astype(jnp.float32)).astype(x.dtype)

def partial_rope(t, positions):
    half = ROPE_DIMS // 2
    inv_freq = ROPE_THETA ** (-(jnp.arange(half, dtype=jnp.float32) * 2.0 / ROPE_DIMS))
    ang = positions.astype(jnp.float32)[..., None] * inv_freq
    cos = jnp.cos(ang)[:, :, None, :]
    sin = jnp.sin(ang)[:, :, None, :]
    tr = t[..., :ROPE_DIMS].astype(jnp.float32)
    t1, t2 = tr[..., :half], tr[..., half:]
    rot = jnp.concatenate([t1 * cos - t2 * sin, t2 * cos + t1 * sin], axis=-1)
    return jnp.concatenate([rot.astype(t.dtype), t[..., ROPE_DIMS:]], axis=-1)

def dilated_group_attention(q, k, v, window, dilation):
    b, s, h, hd = q.shape
    r = dilation
    n_back = window // dilation
    length = s // r
    nb = -(-length // Q_BLOCK)
    lp = nb * Q_BLOCK

    def to_sub(t):
        t = t.reshape(b, length, r, h, hd).transpose(0, 2, 1, 3, 4)
        t = jnp.pad(t, ((0, 0), (0, 0), (0, lp - length), (0, 0), (0, 0)))
        return t.reshape(b, r, nb, Q_BLOCK, h, hd).astype(jnp.float32)

    def with_prev(t):
        prev = jnp.pad(t, ((0, 0), (0, 0), (1, 0), (0, 0), (0, 0), (0, 0)))[:, :, :-1]
        return jnp.concatenate([prev, t], axis=3)

    qs = to_sub(q)
    kc = with_prev(to_sub(k))
    vc = with_prev(to_sub(v))
    scores = jnp.einsum('brnqhd,brnkhd->brnhqk', qs, kc) * (hd ** -0.5)
    blk = jnp.arange(nb)[:, None, None]
    qi = jnp.arange(Q_BLOCK)[None, :, None] + Q_BLOCK
    ki = jnp.arange(2 * Q_BLOCK)[None, None, :]
    dist = qi - ki
    valid = (dist >= 0) & (dist <= n_back) & (blk * Q_BLOCK + ki - Q_BLOCK >= 0)
    scores = jnp.where(valid[None, None, :, None], scores, NEG_INF)
    m = jnp.max(scores, axis=-1, keepdims=True)
    p = jnp.exp(scores - m)
    den = jnp.sum(p, axis=-1)
    out = jnp.einsum('brnhqk,brnkhd->brnqhd', p, vc) / jnp.swapaxes(den, -1, -2)[..., None]
    lse = jnp.swapaxes(m[..., 0] + jnp.log(den), -1, -2)

    def from_sub(t):
        t = t.reshape((b, r, lp) + t.shape[4:])[:, :, :length]
        return jnp.swapaxes(t, 1, 2).reshape((b, s) + t.shape[3:])

    return from_sub(out), from_sub(lse)

def dilated_mixture(q, k, v):
    outs, lses = [], []
    for g, (window, dilation) in enumerate(DIL_GROUPS):
        sl = slice(g * DIL_HEADS_PER_GROUP, (g + 1) * DIL_HEADS_PER_GROUP)
        o, l = dilated_group_attention(q[:, :, sl], k[:, :, sl], v[:, :, sl], window, dilation)
        outs.append(o)
        lses.append(l)
    outs = jnp.stack(outs)
    alpha = jax.nn.softmax(jnp.stack(lses), axis=0)
    return jnp.sum(alpha[..., None] * outs, axis=0)

def stick_breaking_attention(q, k, v):
    b, s, h, hd = q.shape
    nb = s // Q_BLOCK
    qb = jnp.moveaxis(q.reshape(b, nb, Q_BLOCK, h, hd), 1, 0).astype(jnp.float32)
    kf = k.astype(jnp.float32)
    vf = v.astype(jnp.float32)
    key_idx = jnp.arange(s)

    def one_block(args):
        q_blk, i = args
        z = jnp.einsum('bqhd,bkhd->bhqk', q_blk, kf) * (hd ** -0.5)
        t = i * Q_BLOCK + jnp.arange(Q_BLOCK)
        causal = key_idx[None, :] < t[:, None]
        log_beta = jax.nn.log_sigmoid(z)
        log_not = jnp.where(causal, -jax.nn.softplus(z), 0.0)
        suffix = lax.cumsum(log_not, axis=3, reverse=True) - log_not
        weights = jnp.where(causal, jnp.exp(log_beta + suffix), 0.0)
        return jnp.einsum('bhqk,bkhd->bqhd', weights, vf)

    out = lax.map(one_block, (qb, jnp.arange(nb)))
    return jnp.moveaxis(out, 0, 1).reshape(b, s, h, hd)

def hybrid_mixer(h, positions, w_in, w_branch_a, w_branch_b, w_out):
    b, s, _ = h.shape
    widths = [DIL_HEADS * HEAD_DIM] * 3 + [SB_HEADS * HEAD_DIM] * 3 + [D_MODEL, D_MODEL]
    cuts = [int(v) for v in np.cumsum(widths)[:-1]]
    proj = h @ w_in
    qa, ka, va, qb, kb, vb, ga, gb = jnp.split(proj, cuts, axis=-1)
    qa = partial_rope(qa.reshape(b, s, DIL_HEADS, HEAD_DIM), positions)
    ka = partial_rope(ka.reshape(b, s, DIL_HEADS, HEAD_DIM), positions)
    va = va.reshape(b, s, DIL_HEADS, HEAD_DIM)
    ya = dilated_mixture(qa, ka, va).reshape(b, s, DIL_OUT).astype(h.dtype) @ w_branch_a
    yb = stick_breaking_attention(qb.reshape(b, s, SB_HEADS, HEAD_DIM),
                                  kb.reshape(b, s, SB_HEADS, HEAD_DIM),
                                  vb.reshape(b, s, SB_HEADS, HEAD_DIM)).reshape(b, s, SB_OUT).astype(h.dtype) @ w_branch_b
    merged = jax.nn.sigmoid(ga) * ya + jax.nn.sigmoid(gb) * yb
    return merged @ w_out

def clamped_swiglu(hu):
    x_glu = jnp.minimum(hu[..., ::2], SWIGLU_LIMIT)
    x_lin = jnp.clip(hu[..., 1::2], -SWIGLU_LIMIT, SWIGLU_LIMIT)
    return x_glu * jax.nn.sigmoid(SWIGLU_ALPHA * x_glu) * (x_lin + 1.0)

def moe_ffn(h, w_router, b_router, w_up, b_up, w_down, b_down):
    b, s, d = h.shape
    n_tok = b * s
    xf = h.reshape(n_tok, d)
    logits = (xf @ w_router + b_router).astype(jnp.float32)
    top_val, top_idx = lax.top_k(logits, TOP_K)
    top_w = jax.nn.softmax(top_val, axis=-1)
    n_assign = n_tok * TOP_K
    flat_e = top_idx.reshape(-1)
    flat_tok = jnp.arange(n_assign, dtype=jnp.int32) // TOP_K
    order = jnp.argsort(flat_e, stable=True)
    e_sorted = flat_e[order]
    counts = jnp.bincount(flat_e, length=N_EXPERTS)
    padded = (counts + MOE_BLOCK - 1) // MOE_BLOCK * MOE_BLOCK
    pad_end = jnp.cumsum(padded)
    pad_start = pad_end - padded
    start = jnp.cumsum(counts) - counts
    dest = pad_start[e_sorted] + jnp.arange(n_assign) - start[e_sorted]
    n_blocks = -(-n_assign // MOE_BLOCK) + N_EXPERTS
    n_slots = n_blocks * MOE_BLOCK
    tok_buf = jnp.full((n_slots,), n_tok, jnp.int32).at[dest].set(flat_tok[order])
    gate_buf = jnp.zeros((n_slots,), jnp.float32).at[dest].set(top_w.reshape(-1)[order])
    block_expert = jnp.minimum(jnp.searchsorted(pad_end, jnp.arange(n_blocks) * MOE_BLOCK, side='right'),
                               N_EXPERTS - 1)
    x_pad = jnp.concatenate([xf, jnp.zeros((1, d), xf.dtype)], axis=0)

    def expert_chunk(args):
        toks, e = args
        hu = x_pad[toks] @ w_up[e] + b_up[e]
        return clamped_swiglu(hu) @ w_down[e] + b_down[e]

    ys = lax.map(expert_chunk, (tok_buf.reshape(n_blocks, MOE_BLOCK), block_expert))
    ys = ys.reshape(n_slots, d).astype(jnp.float32) * gate_buf[:, None]
    out = jnp.zeros((n_tok + 1, d), jnp.float32).at[tok_buf].add(ys)[:n_tok]
    return out.reshape(b, s, d).astype(h.dtype)

def setup_inputs(seed: int = 0) -> dict:
    key = jax.random.key(seed)
    ks = jax.random.split(key, 24)

    def normal(k, shape, scale):
        return jax.random.normal(k, shape, jnp.float32) * scale

    L, D, E, F = DEPTH, D_MODEL, N_EXPERTS, D_EXPERT
    positions = (jnp.arange(SEQ, dtype=jnp.int32)[None, :]
                 + jax.random.randint(ks[2], (BATCH, 1), 0, 4096, dtype=jnp.int32))
    return {
        "x": normal(ks[0], (BATCH, SEQ, D), 1.0),
        "c": normal(ks[1], (BATCH, D), 1.0),
        "positions": positions,
        "ada_w": normal(ks[3], (L, D, 6 * D), D ** -0.5),
        "ada_b": normal(ks[4], (L, 6 * D), 0.01),
        "norm_mix_pre": 1.0 + normal(ks[5], (L, D), 0.05),
        "norm_mix_post": 1.0 + normal(ks[6], (L, D), 0.05),
        "norm_ffn_pre": 1.0 + normal(ks[7], (L, D), 0.05),
        "norm_ffn_post": 1.0 + normal(ks[8], (L, D), 0.05),
        "w_in": normal(ks[9], (L, D, IN_COLS), D ** -0.5),
        "w_branch_a": normal(ks[10], (L, DIL_OUT, D), DIL_OUT ** -0.5),
        "w_branch_b": normal(ks[11], (L, SB_OUT, D), SB_OUT ** -0.5),
        "w_out": normal(ks[12], (L, D, D), D ** -0.5),
        "w_router": normal(ks[13], (L, D, E), D ** -0.5),
        "b_router": normal(ks[14], (L, E), 0.01),
        "w_up": normal(ks[15], (L, E, D, 2 * F), D ** -0.5),
        "b_up": normal(ks[16], (L, E, 2 * F), 0.01),
        "w_down": normal(ks[17], (L, E, F, D), F ** -0.5),
        "b_down": normal(ks[18], (L, E, D), 0.01),
    }

def reference(x, c, positions, ada_w, ada_b, norm_mix_pre, norm_mix_post, norm_ffn_pre, norm_ffn_post,
              w_in, w_branch_a, w_branch_b, w_out, w_router, b_router, w_up, b_up, w_down, b_down):
    for layer in range(DEPTH):
        mod = (jax.nn.silu(c) @ ada_w[layer] + ada_b[layer]).astype(x.dtype)
        shift1, scale1, gate1, shift2, scale2, gate2 = jnp.split(mod[:, None, :], 6, axis=-1)
        h = rms_norm(x, norm_mix_pre[layer]) * (1.0 + scale1) + shift1
        y = hybrid_mixer(h, positions, w_in[layer], w_branch_a[layer], w_branch_b[layer], w_out[layer])
        x = (x + gate1 * rms_norm(y, norm_mix_post[layer])).astype(x.dtype)
        h = rms_norm(x, norm_ffn_pre[layer]) * (1.0 + scale2) + shift2
        y = moe_ffn(h, w_router[layer], b_router[layer], w_up[layer], b_up[layer], w_down[layer], b_down[layer])
        x = (x + gate2 * rms_norm(y, norm_ffn_post[layer])).astype(x.dtype)
    return x


_drawn_inputs = setup_inputs


def setup_inputs(seed=0):
    import zlib

    import numpy as np

    out = dict(_drawn_inputs(seed))
    spreads = {}
    factors = {'b_up': 8.0, 'b_down': 8.0}
    for name, (base, spread) in spreads.items():
        noise = np.random.default_rng([zlib.crc32(name.encode()), seed]).standard_normal(out[name].shape)
        drawn = base * np.exp(spread * noise) if base else spread * noise
        out[name] = __import__('jax').numpy.asarray(drawn.astype(out[name].dtype))
    for name, factor in factors.items():
        out[name] = (out[name] * factor).astype(out[name].dtype)
    return out
```

```python
from contextlib import ExitStack

import numpy as np

import concourse.bass as bass
from concourse import mybir

ALU = mybir.AluOpType
ACT = mybir.ActivationFunctionType
F32 = mybir.dt.float32
I32 = mybir.dt.int32
AX_X = mybir.AxisListType.X
ds = bass.ds

P = 128
D = 1024
KT = D // P
T = 256
TT = T // P
HD = 64
NG, SLOTS = 3, 4
DIL_W = NG * SLOTS * HD
SB_H = 8
SB_W = SB_H * HD
QA, KA, VA = 0, DIL_W, 2 * DIL_W
QB = 3 * DIL_W
KB, VB = QB + SB_W, QB + 2 * SB_W
GA = QB + 3 * SB_W
GB = GA + D
HALF = 8
E = 32
TOPK = 4
F = 1024
FT = F // P
LIMIT, ALPHA = 7.0, 1.702
EPS = 1e-6
SCALE = HD ** -0.5
NEG = -1e30
CW = 512
RING = 6
BLK = 64
NBLK = T // BLK
TRI = 384

C_ID, C_ONE, C_LE, C_GE, C_ST, C_NG, C_IOTA = 0, 128, 256, 384, 512, 640, 768
C_MASK = C_IOTA + T
C_FREQ = C_MASK + NG * P + NG * T
C_EPS = C_FREQ + HALF
C_W = C_EPS + 1

R_ADAB, R_G = 0, 48
R_C = R_G + 4 * KT
R_N = R_C + KT


def constants():
    i = np.arange(P)
    c = np.zeros((P, C_W), np.float32)
    c[:, C_ID:C_ID + P] = np.eye(P)
    c[:, C_ONE:C_ONE + P] = 1.0
    c[:, C_LE:C_LE + P] = i[:, None] <= i[None, :]
    c[:, C_GE:C_GE + P] = i[:, None] >= i[None, :]
    c[:, C_ST:C_ST + P] = i[:, None] < i[None, :]
    c[:, C_NG:C_NG + P] = np.where(i[:, None] < i[None, :], 0.0, NEG)
    c[:, C_IOTA:C_IOTA + T] = np.arange(T)[None, :]
    at = C_MASK
    for tt in range(TT):
        for window, dil in ((128, 1), (512, 4), (2048, 16)):
            dist = (tt * P + i)[:, None] - np.arange((tt + 1) * P)[None, :]
            ok = (dist >= 0) & (dist <= window) & (dist % dil == 0)
            c[:, at:at + dist.shape[1]] = np.where(ok, 0.0, NEG)
            at += dist.shape[1]
    freq = (500000.0 ** (-(np.arange(HALF, dtype=np.float32) * 2.0 / (2 * HALF)))).astype(np.float32)
    c[:, C_FREQ:C_FREQ + HALF] = freq[None, :]
    c[:, C_EPS] = EPS
    return c


def two_pi_parts():
    a = np.float32(6.28125)
    b = np.float32(np.round((2 * np.pi - float(a)) * 2.0 ** 20) / 2.0 ** 20)
    return float(a), float(b), float(np.float32(2 * np.pi - float(a) - float(b)))


class Units:

    def __init__(self, full, free):
        self.full, self.free, self.count, self.place = full, free, [0] * 8, {}

    def add(self, name, bank):
        self.place[name] = (bank, self.count[bank])
        self.count[bank] += 1

    def bank(self, name):
        return self.place[name][0]

    def wait_free(self, eng, name):
        b, n = self.place[name]
        if not isinstance(n, int) or n > 0:
            eng.wait_ge(self.free[b], n)

    def wait_full(self, eng, name):
        b, n = self.place[name]
        eng.wait_ge(self.full[b], n + 1)

    def wait_read(self, eng, name):
        b, n = self.place[name]
        eng.wait_ge(self.free[b], n + 1)


X_UNITS = ["gt"] + [f"xg{q}" for q in range(4)] + [f"up{j}" for j in range(8)] + \
          [f"dn{q}" for q in range(4)] + [f"yt{q}" for q in range(4)]
X_PER = [len([k for k in range(len(X_UNITS)) if k % 4 == b]) for b in range(4)]


def layer_kernel(nc, a, out):
    ctx = ExitStack()
    with ctx:
        def sb(name, width, dt=F32, rows=P):
            return ctx.enter_context(nc.sbuf_tensor(name, [rows, width], dt))

        def sem(name):
            return ctx.enter_context(nc.semaphore(name))

        ring = sb("ring", RING * KT * CW)
        cst = sb("cst", C_W)
        x_res = sb("x_res", TT * D)
        xn = sb("xn", TT * D)
        hT = sb("hT", KT * T)
        arena = sb("arena", 14848)
        yaT = sb("yaT", 2 * T)
        ybT = sb("ybT", 4 * T)
        grow = sb("grow", D)
        b_down_sb = sb("b_down_sb", D, rows=E)
        bup = sb("bup", 16 * E)
        w_router_sb = sb("w_router_sb", KT * E)
        cols = sb("cols", R_N)
        mod = sb("mod", 48)
        small = sb("small", 96)
        rope = sb("rope", 6 * TT * HALF)
        pos_i = sb("pos_i", TT, I32)
        small_rows = sb("small_rows", P, rows=R_N)
        b_router_sb = sb("b_router_sb", E, rows=1)
        cls_i = sb("cls_i", E, I32)

        ident = cst[:, C_ID:C_ID + P]
        ones = cst[:, C_ONE:C_ONE + P]
        tri_le = cst[:, C_LE:C_LE + P]
        tri_ge = cst[:, C_GE:C_GE + P]
        iota = cst[:, C_IOTA:C_IOTA + T]

        def slot(g):
            s = g % RING
            return ring[:, s * KT * CW:(s + 1) * KT * CW]

        def chunk(g, width=CW, kt=KT):
            return slot(g)[:, 0:kt * width].rearrange("p (k n) -> p k n", k=kt)

        x3 = x_res[:, :].rearrange("p (t d) -> p t d", t=TT)
        xn3 = xn[:, :].rearrange("p (t d) -> p t d", t=TT)
        hT3 = hT[:, :].rearrange("p (k t) -> p k t", k=KT)

        def region(at, shape):
            n = int(np.prod(shape))
            v = arena[:, at:at + n]
            if len(shape) == 2:
                v = v.rearrange("p (x y) -> p x y", x=shape[0])
            elif len(shape) == 3:
                v = v.rearrange("p (x y z) -> p x y z", x=shape[0], y=shape[1])
            return v

        qk = region(0, (TT, 2 * DIL_W))
        vtok = region(3072, (TT, DIL_W + SB_W))
        qkT = region(5632, (12, T))
        sbT = region(8704, (8, T))
        gates = region(10752, (16, T))
        bup_rows = region(10752, (2 * F,))[0:E, :]
        sbw = region(10752, (10, TRI))
        prob = xn[:, 0:NG * P + NG * T]
        probT = region(8704, (NG, TRI))
        merged = region(0, (KT, T))
        brw = region(2048, (4, T))
        h2 = region(0, (TT, D))
        XT = region(2048, (KT, T))
        actT = region(4096, (FT, T))
        YT = region(6144, (KT, T))
        Y = region(8192, (2, D))
        S = region(10240, (TT, T))
        Sg = region(10752, (TT, T))
        GT = region(11264, (2, T))
        xw = region(11776, (8, T))
        lg = region(13824, (8, TT * E))
        posm = region(14336, (TT, E + 1))
        gate = region(14336 + 2 * (E + 1), (TT, E + 1))
        top = region(14336 + 4 * (E + 1), (TT, 8))
        gT = region(14528, (T,))
        def junk(tt):
            return arena[:, 8192 + tt * D:8192 + (tt + 1) * D]

        diag1 = hT[:, 0:D]
        diag2 = region(2048, (D,))

        psum = ctx.enter_context(nc.psum_tensor("psum", [P, 8 * 512], F32))
        ps = [psum[:, b * 512:(b + 1) * 512] for b in range(8)]

        bank_full = [sem(f"bank_full{b}") for b in range(8)]
        bank_free = [sem(f"bank_free{b}") for b in range(8)]
        slot_full = [sem(f"slot_full{s}") for s in range(RING)]
        ada_used = sem("ada_used")
        ld_cst, ld_rows, ld_x, ld_pos, ld_bup, ld_small = map(sem, (
            "ld_cst", "ld_rows", "ld_x", "ld_pos", "ld_bup", "ld_small"))
        xn_ready, ec_ready, silu_ready, ang_ready, rope_ready = map(sem, (
            "xn_ready", "ec_ready", "silu_ready", "ang_ready", "rope_ready"))
        rot_done, bcur_ready, sb_na, sb_e, sb_ln = map(sem, (
            "rot_done", "bcur_ready", "sb_na", "sb_e", "sb_ln"))
        sb_sp, sb_l, sb_w, dl_max, dl_exp = map(sem, (
            "sb_sp", "sb_l", "sb_w", "dl_max", "dl_exp"))
        dl_p, sig_ready, merged_ready, diag_ready, x1_ready = map(sem, (
            "dl_p", "sig_ready", "merged_ready", "diag_ready", "x1_ready"))
        x1n_ready, sel_ready, lexp_ready, lmax_ready, gate_ready = map(sem, (
            "x1n_ready", "sel_ready", "lexp_ready", "lmax_ready", "gate_ready"))
        cls_ready, s_ready, g_ready, sg_ready, l_ready = map(sem, (
            "cls_ready", "s_ready", "g_ready", "sg_ready", "l_ready"))
        m_ready, act_ready, acc_done, out_ready, stored = map(sem, (
            "m_ready", "act_ready", "acc_done", "out_ready", "stored"))
        rms_ready, sq_ready = map(sem, (
            "rms_ready", "sq_ready"))
        chain = sem("chain")

        front = []
        where = {}

        def add_chunk(name, src, kt=KT, width=CW):
            where[name] = len(front)
            front.append((src.rearrange("(k p) n -> p k n", p=P), kt, width))

        ada = a["ada_w"][0]
        w_in = a["w_in"][0]
        for m in range(4):
            add_chunk(f"ada{m}", ada[:, m * CW:(m + 1) * CW])
        for name, c0 in (("sbq", QB), ("sbk", KB), ("sbv", VB), ("qk0", 0), ("qk1", CW), ("qk2", 2 * CW), ("va0", VA)):
            add_chunk(name, w_in[:, c0:c0 + CW])
        add_chunk("va1", w_in[:, VA + CW:VA + DIL_W], KT, DIL_W - CW)
        for m in range(4):
            add_chunk(f"gate{m}", w_in[:, GA + m * CW:GA + (m + 1) * CW])
        add_chunk("wa", a["w_branch_a"][0], 2, D)
        add_chunk("wb", a["w_branch_b"][0], 4, D)
        for m in range(4, 10):
            add_chunk(f"ada{m}", ada[:, m * CW:(m + 1) * CW])
        for m in range(2):
            add_chunk(f"wo{m}", a["w_out"][0][:, m * CW:(m + 1) * CW])
        for m in range(10, 12):
            add_chunk(f"ada{m}", ada[:, m * CW:(m + 1) * CW])
        NF = len(front)

        un = Units(bank_full, bank_free)
        un.add("rows", 7)
        for q in range(4):
            un.add(f"hT{q}", q)
        un.add("bup", 6)
        un.add("ada_a", 7)
        rot = []
        for n in ("sbq0", "sbq1", "sbk0", "sbk1", "sbv0", "sbv1", "qk00", "qk01", "qk10", "qk11", "qk20", "qk21",
                  "va00", "va01", "va1", "qkT0", "qkT1", "qkT2", "qkT3", "qkT4", "qkT5"):
            un.add(n, len(rot) % 2)
            rot.append(n)
        for h in range(SB_H):
            un.add(f"z{h}", 2 + h % 2)
            un.add(f"c{h}", 4 + h % 2)
            if h % 2:
                un.add(f"sbo{h // 2}", 6 + h // 2 % 2)
        for i in range(SLOTS):
            for b in range(3):
                un.add(f"s{i}{b}", 2 + b)
            un.add(f"g{2 * i}", 0)
            for g in range(NG):
                un.add(f"pT{i}{g}", 5 + g)
            un.add(f"g{2 * i + 1}", 0)
            if i % 2:
                un.add(f"dlo{i // 2}", 1)
        for m in range(KT):
            un.add(f"br{m}", 2 + m % 4)
        un.add("ada_b", 6)
        un.add("grow1a", 6)
        un.add("grow1b", 7)
        for dh in range(2):
            for tt in range(TT):
                un.add(f"y{tt}{dh}", 2 * tt + dh)
        for q in range(4):
            un.add(f"h2T{q}", 4 + q)
        un.add("logit", 0)
        for n, b in (("hb00", 4), ("hb01", 5), ("hb10", 6), ("hb11", 7)):
            un.add(n, b)
        un.add("ada_c", 1)
        un.add("gateT", 2)
        un.add("rank", 3)
        un.add("grow2a", 4)
        un.add("grow2b", 5)
        for b in range(4):
            un.add(f"acc{b}", b)
        base = list(un.count)

        released = {f"ada{m}": (ada_used, n + 1) for n, m in enumerate([0, 1, 2, 4, 5, 6, 7, 8, 10])}
        for name, unit in (("ada3", "ada_a"), ("ada9", "ada_b"), ("ada11", "ada_c"), ("sbq", "sbq1"), ("sbk", "sbk1"),
                           ("sbv", "sbv1"), ("qk0", "qk01"), ("qk1", "qk11"), ("qk2", "qk21"), ("va0", "va01"),
                           ("va1", "va1"), ("gate0", "g1"), ("gate1", "g3"), ("gate2", "g5"), ("gate3", "g7"),
                           ("wa", "br7"), ("wb", "br7"), ("wo0", "y10"), ("wo1", "y11")):
            b, n = un.place[unit]
            released[name] = (bank_full[b], n + 1)
        names = sorted(where, key=where.get)

        def xunits(e):
            u = Units(bank_full, bank_free)
            for k, name in enumerate(X_UNITS):
                b = k % 4
                u.place[name] = (4 + b, e * X_PER[b] + base[4 + b] + k // 4)
            return u

        def by_size(eng, n_blk, body):
            with eng.If(n_blk <= 2):
                with eng.If(n_blk <= 1):
                    body(1)
                with eng.Else():
                    body(2)
            with eng.Else():
                with eng.If(n_blk <= 3):
                    body(3)
                with eng.Else():
                    body(4)

        block = ctx.enter_context(nc.Block())

        @block.sync
        def _(sp):
            for g, (src, kt, width) in enumerate(front):
                if g >= RING:
                    sp.wait_ge(*released[names[g - RING]])
                sp.dma_start(chunk(g, width, kt), src).then_inc(slot_full[g % RING], 16)

            def expert_chunks(e, first):
                for c in range(6):
                    g = NF + c
                    if first:
                        sp.wait_ge(*released[names[g - RING]])
                    else:
                        last = xunits(e - 1)
                        last.wait_full(sp, f"up{2 * c + 1}" if c < 4 else f"dn{2 * (c - 4) + 1}")
                    if c < 4:
                        src = a["w_up"][0][ds(e, 1), :, c * CW:(c + 1) * CW]
                    else:
                        src = a["w_down"][0][ds(e, 1), :, (c - 4) * CW:(c - 3) * CW]
                    sp.dma_start(chunk(g), src.rearrange("e (k p) n -> p (e k) n", p=P)).then_inc(
                        slot_full[g % RING], 16)

            expert_chunks(0, True)
            with sp.Fori(1, E) as e:
                expert_chunks(e, False)
            for tt in range(TT):
                sp.wait_ge(out_ready, 2 * (tt + 1))
                sp.dma_start(out[0, tt * P:(tt + 1) * P, :], xn3[:, tt, :]).then_inc(stored, 16)
            sp.wait_ge(stored, 16 * TT)

        @block.tensor
        def _(pe):
            def arrived(name):
                g = where[name]
                pe.wait_ge(slot_full[g % RING], 16 * (g // RING + 1))
                return g

            def fill(name, steps):
                un.wait_free(pe, name)
                for s in steps:
                    ins = pe.matmul(s[0], s[1], s[2], start=s[3], stop=s[4], skip_group_check=True)
                ins.then_inc(bank_full[un.bank(name)], 1)

            def turn(name, pairs):
                un.wait_free(pe, name)
                for o, i_, idn in pairs:
                    ins = pe.transpose(o, i_, idn)
                ins.then_inc(bank_full[un.bank(name)], 1)

            def bank(name):
                return ps[un.bank(name)]

            def tok_unit(name, w, tt, width=CW, col=0, last=True, first=True):
                o = bank(name)[:, col:col + width]
                return [(o, hT3[:, k, tt * P:(tt + 1) * P], w[:, k, 0:width], k == 0, k == KT - 1) for k in range(KT)]

            def chan_unit(name, w, m0):
                r = []
                for m in range(2):
                    c0 = (m0 + m) * P
                    r += [(bank(name)[:, m * T:(m + 1) * T], w[:, k, c0:c0 + P], hT3[:, k, :], k == 0, k == KT - 1)
                          for k in range(KT)]
                return r

            def ada_part(unit, ms):
                un.wait_free(pe, unit)
                pe.wait_ge(silu_ready, 1)
                for n, m in enumerate(ms):
                    g = arrived(f"ada{m}")
                    w = chunk(g)
                    for q in range(4):
                        for k in range(KT):
                            ins = pe.matmul(bank(unit)[:, 4 * n + q:4 * n + q + 1], w[:, k, q * P:(q + 1) * P],
                                            small[:, k:k + 1], start=(k == 0), stop=(k == KT - 1),
                                            skip_group_check=True)
                    if n < len(ms) - 1:
                        ins.then_inc(ada_used, 1)
                ins.then_inc(bank_full[un.bank(unit)], 1)

            pe.wait_ge(ld_cst, 16)
            pe.wait_ge(ld_rows, 96)
            turn("rows", [(bank("rows")[:, 0:R_N], small_rows[:, :], cst[0:R_N, C_ID:C_ID + R_N])])
            pe.wait_ge(ld_bup, 16)
            turn("bup", [(bank("bup")[:, q * E:(q + 1) * E],
                          bup_rows.rearrange("p (j c two) -> p j two c", j=FT, two=2)[:, q // 2, q % 2, :],
                          cst[0:E, C_ID:C_ID + E]) for q in range(16)])
            for q in range(4):
                if q == 0:
                    pe.wait_ge(xn_ready, 1)
                turn(f"hT{q}", [(ps[q][:, i * T + tt * P:i * T + (tt + 1) * P],
                                 xn3[:, tt, (2 * q + i) * P:(2 * q + i + 1) * P], ident)
                                for i in range(2) for tt in range(TT)])
            ada_part("ada_a", range(4))
            for q in range(4):
                un.wait_read(pe, f"hT{q}")
            for n in ("sbq", "sbk"):
                g = arrived(n)
                for m in range(2):
                    fill(f"{n}{m}", chan_unit(f"{n}{m}", chunk(g), 2 * m))
            g = arrived("sbv")
            for tt in range(TT):
                fill(f"sbv{tt}", tok_unit(f"sbv{tt}", chunk(g), tt))

            def sb_head(h):
                r = slice(h % 2 * HD, h % 2 * HD + HD)
                return sbT[r, h // 2, :], sbT[r, 4 + h // 2, :]

            def sb_scores(h):
                if h == 0:
                    for n in ("sbv0", "sbv1"):
                        un.wait_read(pe, n)
                q, k = sb_head(h)
                z = bank(f"z{h}")
                fill(f"z{h}", [(z[:, 0:T], k[:, 0:P], q, True, True),
                               (z[:, T:TRI], k[:, P:T], q[:, P:T], True, True)])

            def sb_sums(h):
                pe.wait_ge(sb_sp, h + 1)
                sp_ = sbw[:, 6 + h % 2, :]
                c = bank(f"c{h}")
                fill(f"c{h}", [(c[:, 0:T], tri_ge, sp_[:, 0:T], True, False),
                               (c[:, P:T], ones, sp_[:, T:TRI], False, True),
                               (c[:, T:TRI], tri_ge, sp_[:, T:TRI], True, True)])

            def sb_out(h):
                pe.wait_ge(sb_w, h + 1)
                w = sbw[:, 4 + h % 2, :]
                v = [vtok[:, tt, DIL_W + h * HD:DIL_W + (h + 1) * HD] for tt in range(TT)]
                name = f"sbo{h // 2}"
                if h % 2 == 0:
                    un.wait_free(pe, name)
                o = bank(name)[h % 2 * HD:h % 2 * HD + HD, :]
                pe.matmul(o[:, 0:T], v[0], w[:, 0:T], start=True, stop=False, skip_group_check=True)
                ins = pe.matmul(o[:, P:T], v[1], w[:, T:TRI], start=False, stop=True, skip_group_check=True)
                if h % 2:
                    ins.then_inc(bank_full[un.bank(name)], 1)

            dil = [("qk00", "qk0", 0), ("qk01", "qk0", 1), ("qk10", "qk1", 0), ("qk11", "qk1", 1),
                   ("qk20", "qk2", 0), ("qk21", "qk2", 1), ("va00", "va0", 0), ("va01", "va0", 1)]
            for h in range(SB_H + 2):
                if h < len(dil):
                    unit, cname, tt = dil[h]
                    g = arrived(cname)
                    fill(unit, tok_unit(unit, chunk(g), tt))
                elif h == len(dil):
                    g = arrived("va1")
                    w = chunk(g, DIL_W - CW)
                    fill("va1", tok_unit("va1", w, 0, DIL_W - CW) + tok_unit("va1", w, 1, DIL_W - CW, T))
                if h < SB_H:
                    sb_scores(h)
                if 1 <= h <= SB_H:
                    sb_sums(h - 1)
                if h >= 2:
                    sb_out(h - 2)
            pe.wait_ge(rot_done, 1)
            for u in range(6):
                turn(f"qkT{u}", [(bank(f"qkT{u}")[:, i * T + tt * P:i * T + (tt + 1) * P],
                                  qk[:, tt, (2 * u + i) * P:(2 * u + i + 1) * P], ident)
                                 for i in range(2) for tt in range(TT)])

            def gate_unit(n):
                cname = f"gate{n // 2}"
                g = arrived(cname)
                fill(f"g{n}", chan_unit(f"g{n}", chunk(g), 2 * (n % 2)))

            def dil_head(i, g):
                h = g * SLOTS + i
                r = slice(h % 2 * HD, h % 2 * HD + HD)
                return qkT[r, h // 2, :], qkT[r, 6 + h // 2, :]

            for i in range(SLOTS):
                if i == 0:
                    un.wait_read(pe, "qkT4")
                    un.wait_read(pe, "qkT5")
                qk_h = [dil_head(i, g) for g in range(NG)]
                fill(f"s{i}0", [(ps[2][:, g * P:(g + 1) * P], q[:, 0:P], k[:, 0:P], True, True)
                                for g, (q, k) in enumerate(qk_h)])
                fill(f"s{i}1", [(ps[3][:, g * T:(g + 1) * T], q[:, P:T], k, True, True)
                                for g, (q, k) in enumerate(qk_h[0:2])])
                fill(f"s{i}2", [(ps[4][:, 0:T], qk_h[2][0][:, P:T], qk_h[2][1], True, True)])
                gate_unit(2 * i)
                pe.wait_ge(dl_p, i + 1)
                for g in range(NG):
                    b = bank(f"pT{i}{g}")
                    p1 = NG * P + g * T
                    turn(f"pT{i}{g}", [(b[:, 0:P], prob[:, g * P:(g + 1) * P], ident),
                                       (b[:, P:T], prob[:, p1:p1 + P], ident),
                                       (b[:, T:TRI], prob[:, p1 + P:p1 + T], ident)])
                gate_unit(2 * i + 1)
                for g in range(NG):
                    un.wait_read(pe, f"pT{i}{g}")
                name = f"dlo{i // 2}"
                if i % 2 == 0:
                    un.wait_free(pe, name)
                o = bank(name)[i % 2 * HD:i % 2 * HD + HD, :]
                for g in range(NG):
                    h = g * SLOTS + i
                    pe.matmul(o[:, 0:T], vtok[:, 0, h * HD:(h + 1) * HD], probT[:, g, 0:T],
                              start=(g == 0), stop=False, skip_group_check=True)
                    ins = pe.matmul(o[:, P:T], vtok[:, 1, h * HD:(h + 1) * HD], probT[:, g, T:TRI],
                                    start=False, stop=(g == NG - 1), skip_group_check=True)
                if i % 2:
                    ins.then_inc(bank_full[un.bank(name)], 1)

            ga_, gb_ = arrived("wa"), arrived("wb")
            wa, wb = chunk(ga_, D, 2), chunk(gb_, D, 4)
            for n in ("sbo0", "sbo1", "sbo2", "sbo3", "dlo0", "dlo1"):
                un.wait_read(pe, n)
            for m in range(KT):
                b = bank(f"br{m}")
                fill(f"br{m}", [(b[:, 0:T], wa[:, k, m * P:(m + 1) * P],
                                        yaT[:, k * T:(k + 1) * T], k == 0, k == 1) for k in range(2)] +
                            [(b[:, T:2 * T], wb[:, k, m * P:(m + 1) * P],
                              ybT[:, k * T:(k + 1) * T], k == 0, k == 3) for k in range(4)])
            ada_part("ada_b", range(4, 10))

            def spread(unit, n, dg, half):
                pe.wait_ge(diag_ready, n)
                fill(unit, [(bank(unit)[:, :], ones, dg[:, half * 512:(half + 1) * 512], True, True)])

            spread("grow1a", 1, diag1, 0)
            spread("grow1b", 1, diag1, 1)
            pe.wait_ge(merged_ready, 1)
            for dh in range(2):
                g = arrived(f"wo{dh}")
                for tt in range(TT):
                    n = f"y{tt}{dh}"
                    fill(n, [(bank(n)[:, :], merged[:, k, tt * P:(tt + 1) * P], chunk(g)[:, k, :],
                                    k == 0, k == KT - 1) for k in range(KT)])
            pe.wait_ge(x1n_ready, 1)
            for q in range(4):
                turn(f"h2T{q}", [(ps[4 + q][:, i * T + tt * P:i * T + (tt + 1) * P],
                                  xn3[:, tt, (2 * q + i) * P:(2 * q + i + 1) * P], ident)
                                 for i in range(2) for tt in range(TT)])
            for q in range(4):
                un.wait_read(pe, f"h2T{q}")
            pe.wait_ge(ld_small, 48)
            fill("logit", [s for tt in range(TT) for s in
                           [(ps[0][:, tt * E:(tt + 1) * E], hT3[:, k, tt * P:(tt + 1) * P],
                             w_router_sb[:, k * E:(k + 1) * E], k == 0, False) for k in range(KT)] +
                           [(ps[0][:, tt * E:(tt + 1) * E], cst[0:1, C_ONE:C_ONE + P],
                             b_router_sb[0:1, :], False, True)]])
            for tt in range(TT):
                for hf in range(2):
                    n = f"hb{tt}{hf}"
                    turn(n, [(bank(n)[:, k * P:(k + 1) * P], hT3[:, 4 * hf + k, tt * P:(tt + 1) * P], ident)
                             for k in range(4)])
            ada_part("ada_c", range(10, 12))
            pe.wait_ge(sel_ready, 1)
            sel = lg[:, 2, :]
            fill("rank", [(ps[3][:, 0:E], tri_le, sel[:, 0:E], True, True),
                          (ps[3][:, E:2 * E], ones, sel[:, 0:E], True, False),
                          (ps[3][:, E:2 * E], tri_le, sel[:, E:2 * E], False, True),
                          (ps[3][:, 2 * E:3 * E], ones, sel[:, 0:E], True, False),
                          (ps[3][:, 2 * E:3 * E], ones, sel[:, E:2 * E], False, True)])
            pe.wait_ge(gate_ready, 1)
            turn("gateT", [(ps[2][0:E, tt * P:(tt + 1) * P], gate[:, tt, 0:E], ident) for tt in range(TT)])
            spread("grow2a", 2, diag2, 0)
            spread("grow2b", 2, diag2, 1)
            un.wait_read(pe, "gateT")
            for b in range(4):
                tt, dh = b // 2, b % 2
                un.wait_free(pe, f"acc{b}")
                pe.matmul(ps[b][:, :], gT[0:E, tt * P:(tt + 1) * P], b_down_sb[:, dh * 512:(dh + 1) * 512],
                          start=True, stop=True, skip_group_check=True)

            for n in ("hb00", "hb01", "hb10", "hb11"):
                un.wait_read(pe, n)
            pe.wait_ge(cls_ready, 1)
            with pe.Fori(0, E) as e:
                u = xunits(e)
                n_blk = pe.value_load(cls_i[0:1, ds(e, 1)])

                def body(nb):
                    n = nb * BLK
                    halves = [min(P, n - hf * P) for hf in range(2) if n > hf * P]

                    def begin(name):
                        u.wait_free(pe, name)
                        return ps[u.bank(name)]

                    def end(ins, name):
                        ins.then_inc(bank_full[u.bank(name)], 1)

                    pe.wait_ge(s_ready, e + 1)
                    b = begin("gt")
                    for hf, w in enumerate(halves):
                        for tt in range(TT):
                            ins = pe.transpose(b[:, hf * T + tt * P:hf * T + (tt + 1) * P],
                                               Sg[:, tt, hf * P:(hf + 1) * P], ident)
                    end(ins, "gt")
                    for q in range(4):
                        b = begin(f"xg{q}")
                        for i in range(2):
                            for tt in range(TT):
                                ins = pe.matmul(b[:, i * T:i * T + n], h2[:, tt, (2 * q + i) * P:(2 * q + i + 1) * P],
                                                S[:, tt, 0:n], start=(tt == 0), stop=(tt == 1), skip_group_check=True)
                        end(ins, f"xg{q}")
                    for q in range(4):
                        u.wait_read(pe, f"xg{q}")
                    for j in range(8):
                        g = NF + j // 2
                        if j % 2 == 0:
                            pe.wait_ge(slot_full[g % RING], (e + g // RING + 1) * 16)
                        w = chunk(g).rearrange("p k (j c two) -> p k j two c", j=2, two=2)
                        b = begin(f"up{j}")
                        for i in range(2):
                            for k in range(KT):
                                ins = pe.matmul(b[:, i * T:i * T + n], w[:, k, j % 2, i, :], XT[:, k, 0:n],
                                                start=(k == 0), stop=(k == KT - 1), skip_group_check=True)
                        end(ins, f"up{j}")
                    pe.wait_ge(act_ready, 8 * e + 8)
                    for q in range(4):
                        g = NF + 4 + q // 2
                        if q % 2 == 0:
                            pe.wait_ge(slot_full[g % RING], (e + g // RING + 1) * 16)
                        b = begin(f"dn{q}")
                        for i in range(2):
                            c0 = (2 * (q % 2) + i) * P
                            for k in range(FT):
                                ins = pe.matmul(b[:, i * T:i * T + n], chunk(g)[:, k, c0:c0 + P], actT[:, k, 0:n],
                                                start=(k == 0), stop=(k == FT - 1), skip_group_check=True)
                        end(ins, f"dn{q}")
                    for q in range(4):
                        u.wait_read(pe, f"dn{q}")
                        b = begin(f"yt{q}")
                        for hf, w in enumerate(halves):
                            for i in range(2):
                                ins = pe.transpose(b[:, hf * T + i * P:hf * T + (i + 1) * P],
                                                   YT[:, 2 * q + i, hf * P:(hf + 1) * P], ident)
                        end(ins, f"yt{q}")
                    u.wait_read(pe, "gt")
                    for q in range(4):
                        u.wait_read(pe, f"yt{q}")
                    for hf, w in enumerate(halves):
                        for bb in range(4):
                            tt, dh = bb // 2, bb % 2
                            ins = pe.matmul(ps[bb][:, :], GT[0:w, hf, tt * P:(tt + 1) * P],
                                            Y[0:w, hf, dh * 512:(dh + 1) * 512], start=False, stop=True,
                                            skip_group_check=True)
                    ins.then_inc(acc_done, 1)

                by_size(pe, n_blk, body)

        @block.scalar
        def _(act):
            act.dma_start(small_rows[R_G:R_G + KT, :], a["norm_mix_pre"][0].rearrange("(k p) -> k p", p=P)).then_inc(ld_rows, 16)
            act.dma_start(small_rows[R_C:R_C + KT, :], a["c"][0].rearrange("(k p) -> k p", p=P)).then_inc(ld_rows, 16)
            act.dma_start(small_rows[R_ADAB:R_ADAB + 48, :], a["ada_b"][0].rearrange("(k p) -> k p", p=P)).then_inc(ld_rows, 16)
            act.dma_start(cst[:, :], a["cst"]).then_inc(ld_cst, 16)
            act.dma_start(x3, a["x"][0].rearrange("(t p) d -> p t d", p=P)).then_inc(ld_x, 16)
            for n, name in enumerate(("norm_mix_post", "norm_ffn_pre", "norm_ffn_post")):
                r = R_G + (n + 1) * KT
                act.dma_start(small_rows[r:r + KT, :], a[name][0].rearrange("(k p) -> k p", p=P)).then_inc(ld_rows, 16)
            for tt in range(TT):
                act.dma_start(pos_i[:, tt:tt + 1], a["positions"][0, tt * P:(tt + 1) * P].rearrange(
                    "(p o) -> p o", o=1)).then_inc(ld_pos, 16)
            act.dma_start(bup_rows, a["b_up"][0]).then_inc(ld_bup, 16)
            act.dma_start(w_router_sb[:, :].rearrange("p (k n) -> p k n", k=KT),
                          a["w_router"][0].rearrange("(k p) n -> p k n", p=P)).then_inc(ld_small, 16)
            act.dma_start(b_router_sb[:, :], a["b_router"]).then_inc(ld_small, 16)
            act.dma_start(b_down_sb[:, :], a["b_down"][0]).then_inc(ld_small, 16)

            act.wait_ge(ld_x, 16)
            n_sq = [0]

            def root_mean_square(src, tt, dst, junk):
                n_sq[0] += 1
                act.activation(junk, src, ACT.Square, accum_out=small[:, dst + tt:dst + tt + 1]).then_inc(sq_ready, 1)
                act.wait_ge(sq_ready, n_sq[0])
                act.activation(small[:, dst + tt:dst + tt + 1], small[:, dst + tt:dst + tt + 1], ACT.Sqrt,
                               scale=1.0 / D, bias=cst[:, C_EPS:C_EPS + 1]).then_inc(rms_ready, 1)

            act.wait_ge(ld_cst, 16)
            for tt in range(TT):
                root_mean_square(x3[:, tt, :], tt, 18, qk[:, tt, 0:D])
            un.wait_read(act, "rows")
            act.activation(small[:, 8:16], cols[:, R_C:R_C + KT], ACT.Exp, scale=-1.0).then_inc(ec_ready, 1)
            act.wait_ge(ang_ready, 1)
            act.activation(rope[:, 4 * 16:6 * 16], rope[:, 2 * 16:4 * 16], ACT.Sin).then_inc(rope_ready, 1)

            def copy_out(name, dst, src=None):
                un.wait_full(act, name)
                b = ps[un.bank(name)]
                ins = act.activation(dst, b[:, :] if src is None else src, ACT.Copy)
                ins.then_inc(bank_free[un.bank(name)], 1)

            def two(ap):
                return ap.rearrange("p a b -> p (a b)")

            copy_out("bup", bup[:, :])
            for m in range(2):
                copy_out(f"sbq{m}", two(sbT[:, 2 * m:2 * m + 2, :]))
            for m in range(2):
                copy_out(f"sbk{m}", two(sbT[:, 4 + 2 * m:6 + 2 * m, :]))
            for tt in range(TT):
                copy_out(f"sbv{tt}", vtok[:, tt, DIL_W:DIL_W + SB_W])

            def sb_exp(h):
                act.wait_ge(sb_na, h + 1)
                act.activation(sbw[:, 2 + h % 2, :], sbw[:, h % 2, :], ACT.Exp).then_inc(sb_e, 1)
                act.wait_ge(sb_e, h + 1)
                act.activation(sbw[:, h % 2, :], sbw[:, 2 + h % 2, :], ACT.Ln, bias=1.0).then_inc(sb_ln, 1)

            def sb_weights(h):
                act.wait_ge(sb_l, h + 1)
                act.activation(sbw[:, 4 + h % 2, :], sbw[:, 8 + h % 2, :], ACT.Exp).then_inc(sb_w, 1)

            def sb_copy(p):
                copy_out(f"sbo{p}", ybT[:, p * T:(p + 1) * T], ps[un.bank(f"sbo{p}")][:, 0:T])

            dil = [("qk00", 0, 0), ("qk01", 1, 0), ("qk10", 0, 1), ("qk11", 1, 1), ("qk20", 0, 2), ("qk21", 1, 2),
                   ("va00", 0, 3), ("va01", 1, 3)]
            for h in range(SB_H + 2):
                if h < len(dil):
                    n, tt, c = dil[h]
                    dst = qk[:, tt, c * CW:(c + 1) * CW] if c < 3 else vtok[:, tt, 0:CW]
                    copy_out(n, dst)
                elif h == len(dil):
                    copy_out("va1", vtok[:, :, CW:DIL_W], ps[un.bank("va1")][:, :].rearrange("p (t n) -> p t n", t=TT))
                if h < SB_H:
                    sb_exp(h)
                if 1 <= h <= SB_H:
                    sb_weights(h - 1)
                if h >= 2 and h % 2 == 1:
                    sb_copy((h - 2) // 2)
            for u in range(6):
                copy_out(f"qkT{u}", two(qkT[:, 2 * u:2 * u + 2, :]))

            def gate_copy(n):
                copy_out(f"g{n}", two(gates[:, 2 * n:2 * n + 2, :]))

            for i in range(SLOTS):
                act.wait_ge(dl_max, i + 1)
                act.activation(prob[:, 0:NG * P], prob[:, 0:NG * P], ACT.Exp, bias=small[:, 26:27], scale=SCALE,
                               accum_out=small[:, 28:29]).then_inc(dl_exp, 1)
                act.activation(prob[:, NG * P:], prob[:, NG * P:], ACT.Exp, bias=small[:, 27:28], scale=SCALE,
                               accum_out=small[:, 29:30]).then_inc(dl_exp, 1)
                gate_copy(2 * i)
                for g in range(NG):
                    copy_out(f"pT{i}{g}", probT[:, g, :], ps[un.bank(f"pT{i}{g}")][:, 0:TRI])
                gate_copy(2 * i + 1)
                if i % 2:
                    p = i // 2
                    copy_out(f"dlo{p}", yaT[:, p * T:(p + 1) * T], ps[un.bank(f"dlo{p}")][:, 0:T])
            un.wait_read(act, "g7")
            for q in range(4):
                act.activation(two(gates[:, 4 * q:4 * q + 4, :]), two(gates[:, 4 * q:4 * q + 4, :]),
                               ACT.Sigmoid).then_inc(sig_ready, 1)
            copy_out("grow1a", grow[:, 0:512])
            copy_out("grow1b", grow[:, 512:D])
            for tt in range(TT):
                for dh in range(2):
                    un.wait_full(act, f"y{tt}{dh}")
                root_mean_square(psum[:, 2 * tt * 512:(2 * tt + 2) * 512], tt, 38, junk(tt))
            for tt in range(TT):
                act.wait_ge(x1_ready, 2 * tt + 2)
                root_mean_square(x3[:, tt, :], tt, 42, junk(tt))
            for tt in range(TT):
                for hf in range(2):
                    copy_out(f"hb{tt}{hf}", h2[:, tt, hf * 512:(hf + 1) * 512])
            act.wait_ge(lmax_ready, 1)
            for tt in range(TT):
                act.activation(lg[:, 1, tt * E:(tt + 1) * E], lg[:, 0, tt * E:(tt + 1) * E], ACT.Exp,
                               bias=small[:, 50 + tt:51 + tt]).then_inc(lexp_ready, 1)
            copy_out("gateT", gT[0:E, :], ps[un.bank("gateT")][0:E, 0:T])
            act.wait_ge(x1_ready, 4)
            copy_out("grow2a", grow[:, 0:512])
            copy_out("grow2b", grow[:, 512:D])

            act.wait_ge(cls_ready, 1)
            with act.Fori(0, E) as e:
                u = xunits(e)
                n_blk = act.value_load(cls_i[0:1, ds(e, 1)])

                def body(nb):
                    n = nb * BLK
                    halves = [min(P, n - hf * P) for hf in range(2) if n > hf * P]

                    def leave(name, dst, src):
                        ins = act.activation(dst, src, ACT.Copy)
                        ins.then_inc(bank_free[u.bank(name)], 1)

                    def pair(name, w=n, rows=P):
                        return ps[u.bank(name)][0:rows, :].rearrange("p (i t) -> p i t", i=2)[:, :, 0:w]

                    u.wait_full(act, "gt")
                    rows, nh = max(halves), len(halves)
                    for hf, w in enumerate(halves):
                        ins = act.activation(GT[0:w, hf, :], ps[u.bank("gt")][0:w, hf * T:(hf + 1) * T], ACT.Copy)
                        if hf == nh - 1:
                            ins.then_inc(bank_free[u.bank("gt")], 1)
                    for q in range(4):
                        u.wait_full(act, f"xg{q}")
                        leave(f"xg{q}", XT[:, 2 * q:2 * q + 2, 0:n], pair(f"xg{q}"))
                    for j in range(8):
                        act.wait_ge(g_ready, 8 * e + j + 1)
                        act.activation(xw[:, 4 + j % 2, 0:n], xw[:, j % 2, 0:n], ACT.Sigmoid,
                                       scale=ALPHA).then_inc(sg_ready, 1)
                    for q in range(4):
                        u.wait_full(act, f"dn{q}")
                        leave(f"dn{q}", YT[:, 2 * q:2 * q + 2, 0:n], pair(f"dn{q}"))
                    for q in range(4):
                        u.wait_full(act, f"yt{q}")
                        for hf, w in enumerate(halves):
                            ins = act.activation(Y[0:w, hf, q * T:(q + 1) * T],
                                                 ps[u.bank(f"yt{q}")][0:w, hf * T:(hf + 1) * T], ACT.Copy)
                            if hf == nh - 1:
                                ins.then_inc(bank_free[u.bank(f"yt{q}")], 1)

                by_size(act, n_blk, body)

            act.wait_ge(acc_done, E)
            for tt in range(TT):
                root_mean_square(psum[:, 2 * tt * 512:(2 * tt + 2) * 512], tt, 46, junk(tt))

        @block.vector
        def _(v):
            n_chain = [0]

            def link(ins):
                n_chain[0] += 1
                ins.then_inc(chain, 1)
                v.wait_ge(chain, n_chain[0])

            def rstd(dst, n):
                v.wait_ge(rms_ready, 2 * n)
                link(v.reciprocal(dst, dst))

            un.wait_full(v, "rows")
            ins = v.tensor_copy(cols[:, :], ps[7][:, 0:R_N])
            ins.then_inc(bank_free[7], 1)
            un.wait_read(v, "rows")
            rstd(small[:, 18:20], 1)
            for tt in range(TT):
                ins = v.tensor_scalar(xn3[:, tt, :], x3[:, tt, :], small[:, 18 + tt:19 + tt], None, ALU.mult)
            link(ins)
            v.sem_inc(xn_ready, 1)
            v.wait_ge(ec_ready, 1)
            link(v.tensor_scalar(small[:, 8:16], small[:, 8:16], 1.0, None, ALU.add))
            link(v.reciprocal(small[:, 8:16], small[:, 8:16]))
            v.tensor_tensor(small[:, 0:8], small[:, 8:16], cols[:, R_C:R_C + KT], ALU.mult).then_inc(silu_ready, 1)
            v.wait_ge(ld_pos, 16 * TT)
            v.wait_ge(ld_cst, 16)
            n = TT * HALF
            link(v.tensor_copy(small[:, 20:22], pos_i[:, :]))
            ang, turns, arg = rope[:, 0:n], rope[:, n:2 * n], rope[:, 2 * n:4 * n]
            for tt in range(TT):
                ins = v.tensor_scalar(ang[:, tt * HALF:(tt + 1) * HALF], cst[:, C_FREQ:C_FREQ + HALF],
                                      small[:, 20 + tt:21 + tt], None, ALU.mult)
            link(ins)
            c1, c2, c3 = two_pi_parts()
            magic = 1.5 * 2.0 ** 23
            for q, (quarter, add) in enumerate(((0.0, 0.0), (0.25, float(np.pi / 2)))):
                to = arg[:, q * n:(q + 1) * n]
                link(v.tensor_scalar(turns, ang, float(1 / (2 * np.pi)), quarter, ALU.mult, ALU.add))
                link(v.tensor_scalar(turns, turns, magic, None, ALU.add))
                link(v.tensor_scalar(turns, turns, magic, None, ALU.subtract))
                link(v.scalar_tensor_tensor(out=to, in0=turns, scalar=-c1, in1=ang, op0=ALU.mult, op1=ALU.add))
                link(v.scalar_tensor_tensor(out=to, in0=turns, scalar=-c2, in1=to, op0=ALU.mult, op1=ALU.add))
                link(v.scalar_tensor_tensor(out=to, in0=turns, scalar=-c3, in1=to, op0=ALU.mult, op1=ALU.add))
                link(v.tensor_scalar(to, to, add, 3.1415925, ALU.add, ALU.min))
                link(v.tensor_scalar(to, to, -3.1415925, None, ALU.max))
            v.sem_inc(ang_ready, 1)

            def mod_part(unit, m0, m1):
                un.wait_full(v, unit)
                ins = v.tensor_tensor(mod[:, m0:m1], ps[un.bank(unit)][:, 0:m1 - m0], cols[:, m0:m1], ALU.add)
                ins.then_inc(bank_free[un.bank(unit)], 1)
                un.wait_read(v, unit)

            def scale_cols(dst, m0, gain):
                link(v.scalar_tensor_tensor(out=small[:, dst:dst + KT], in0=mod[:, m0:m0 + KT], scalar=1.0,
                                            in1=cols[:, R_G + gain * KT:R_G + (gain + 1) * KT],
                                            op0=ALU.add, op1=ALU.mult))

            mod_part("ada_a", 0, 16)
            scale_cols(64, 8, 0)
            for q in range(4):
                un.wait_full(v, f"hT{q}")
                for i in range(2):
                    k = 2 * q + i
                    ins = v.tensor_scalar(hT3[:, k, :], ps[q][:, i * T:(i + 1) * T], small[:, 64 + k:65 + k],
                                          mod[:, k:k + 1], ALU.mult, ALU.add)
                ins.then_inc(bank_free[q], 1)

            def blocks(ap):
                return ap[:, 0:P], ap[:, T:TRI]

            def sb_first(h):
                un.wait_full(v, f"z{h}")
                z = ps[un.bank(f"z{h}")][:, 0:TRI]
                if h == 0:
                    un.wait_read(v, "bup")
                if h >= 2:
                    v.wait_ge(sb_w, h - 1)
                zs = sbw[:, 8 + h % 2, :]
                v.tensor_scalar(zs, z, SCALE, None, ALU.mult).then_inc(bank_free[un.bank(f"z{h}")], 1)
                un.wait_read(v, f"z{h}")
                v.scalar_tensor_tensor(out=sbw[:, h % 2, :], in0=zs, scalar=-1.0, in1=zs, op0=ALU.mult,
                                       op1=ALU.min).then_inc(sb_na, 1)
                link(v.tensor_scalar(sbw[:, 6 + h % 2, :], zs, 0.0, None, ALU.max))

            def sb_second(h):
                v.wait_ge(sb_ln, h + 1)
                s = sbw[:, 6 + h % 2, :]
                link(v.tensor_tensor(s, s, sbw[:, h % 2, :], ALU.add))
                for d_ in blocks(s):
                    ins = v.tensor_tensor(d_, d_, cst[:, C_ST:C_ST + P], ALU.mult)
                link(ins)
                v.sem_inc(sb_sp, 1)

            def sb_third(h):
                un.wait_full(v, f"c{h}")
                L = sbw[:, 8 + h % 2, :]
                ins = v.tensor_tensor(L, L, ps[un.bank(f"c{h}")][:, 0:TRI], ALU.subtract)
                ins.then_inc(bank_free[un.bank(f"c{h}")], 1)
                un.wait_read(v, f"c{h}")
                for d_ in blocks(L):
                    ins = v.tensor_tensor(d_, d_, cst[:, C_NG:C_NG + P], ALU.add)
                link(ins)
                v.sem_inc(sb_l, 1)

            for h in range(SB_H + 1):
                if h < SB_H:
                    sb_first(h)
                if h >= 1:
                    sb_third(h - 1)
                if h < SB_H:
                    sb_second(h)

            v.wait_ge(rope_ready, 1)
            un.wait_read(v, "qk20")
            un.wait_read(v, "qk21")
            nh = 2 * NG * SLOTS
            for tt in range(TT):
                q4 = qk[:, tt, :].rearrange("p (h d) -> p h d", h=nh)
                t1, t2 = q4[:, :, 0:HALF], q4[:, :, HALF:2 * HALF]
                sin = rope[:, 4 * n + tt * HALF:4 * n + (tt + 1) * HALF]
                cos = rope[:, 5 * n + tt * HALF:5 * n + (tt + 1) * HALF]
                sin = sin.rearrange("p (o d) -> p o d", o=1).broadcast_to([P, nh, HALF])
                cos = cos.rearrange("p (o d) -> p o d", o=1).broadcast_to([P, nh, HALF])
                w = [xn[:, k * nh * HALF:(k + 1) * nh * HALF].rearrange("p (h d) -> p h d", h=nh) for k in range(4)]
                v.tensor_tensor(w[0], t1, cos, ALU.mult)
                v.tensor_tensor(w[1], t2, sin, ALU.mult)
                v.tensor_tensor(w[2], t2, cos, ALU.mult)
                link(v.tensor_tensor(w[3], t1, sin, ALU.mult))
                v.tensor_tensor(t1, w[0], w[1], ALU.subtract)
                link(v.tensor_tensor(t2, w[2], w[3], ALU.add))
            v.sem_inc(rot_done, 1)

            for i in range(SLOTS):
                if i > 0:
                    for g in range(NG):
                        un.wait_read(v, f"pT{i - 1}{g}")
                c = C_MASK
                un.wait_full(v, f"s{i}0")
                ins = v.tensor_tensor_reduce(out=prob[:, 0:TRI], in0=ps[2][:, 0:TRI], in1=cst[:, c:c + TRI],
                                             scale=1.0, scalar=-3e38, op0=ALU.add, op1=ALU.max,
                                             accum_out=small[:, 24:25])
                ins.then_inc(bank_free[2], 1)
                un.wait_full(v, f"s{i}1")
                ins = v.tensor_tensor_reduce(out=prob[:, TRI:TRI + 2 * T], in0=ps[3][:, :],
                                             in1=cst[:, c + TRI:c + TRI + 2 * T], scale=1.0, scalar=-3e38,
                                             op0=ALU.add, op1=ALU.max, accum_out=small[:, 30:31])
                ins.then_inc(bank_free[3], 1)
                un.wait_read(v, f"s{i}1")
                un.wait_full(v, f"s{i}2")
                ins = v.tensor_tensor_reduce(out=prob[:, TRI + 2 * T:TRI + 3 * T], in0=ps[4][:, 0:T],
                                             in1=cst[:, c + TRI + 2 * T:c + TRI + 3 * T], scale=1.0,
                                             scalar=small[:, 30:31], op0=ALU.add, op1=ALU.max,
                                             accum_out=small[:, 25:26])
                ins.then_inc(bank_free[4], 1)
                un.wait_read(v, f"s{i}0")
                un.wait_read(v, f"s{i}2")
                link(v.tensor_scalar(small[:, 26:28], small[:, 24:26], -SCALE, None, ALU.mult))
                v.sem_inc(dl_max, 1)
                v.wait_ge(dl_exp, 2 * (i + 1))
                link(v.reciprocal(small[:, 22:24], small[:, 28:30]))
                v.tensor_scalar(prob[:, 0:TRI], prob[:, 0:TRI], small[:, 22:23], None, ALU.mult)
                link(v.tensor_scalar(prob[:, TRI:], prob[:, TRI:], small[:, 23:24], None, ALU.mult))
                v.sem_inc(dl_p, 1)

            v.wait_ge(sig_ready, 4)
            for m in range(KT):
                un.wait_full(v, f"br{m}")
                b = ps[un.bank(f"br{m}")]
                v.tensor_tensor(brw[:, 2 * (m % 2), :], b[:, 0:T], gates[:, m, :], ALU.mult)
                ins = v.tensor_tensor(brw[:, 2 * (m % 2) + 1, :], b[:, T:2 * T], gates[:, KT + m, :], ALU.mult)
                ins.then_inc(bank_free[un.bank(f"br{m}")], 1)
                un.wait_read(v, f"br{m}")
                ins = v.tensor_tensor(merged[:, m, :], brw[:, 2 * (m % 2), :], brw[:, 2 * (m % 2) + 1, :], ALU.add)
            link(ins)
            v.sem_inc(merged_ready, 1)

            def diagonals(dst, m0, gain, wait=None):
                link(v.tensor_tensor(small[:, 80:88], mod[:, m0:m0 + KT],
                                     cols[:, R_G + gain * KT:R_G + (gain + 1) * KT], ALU.mult))
                for k in range(KT):
                    ins = v.tensor_scalar(dst[:, k * P:(k + 1) * P], ident, small[:, 80 + k:81 + k], None, ALU.mult)
                link(ins)
                v.sem_inc(diag_ready, 1)

            mod_part("ada_b", 16, 40)
            un.wait_full(v, "g7")
            diagonals(diag1, 16, 1)
            scale_cols(72, 32, 2)

            rstd(small[:, 38:40], 2)
            un.wait_read(v, "grow1a")
            un.wait_read(v, "grow1b")
            for tt in range(TT):
                for dh in range(2):
                    n_ = f"y{tt}{dh}"
                    w = xn3[:, tt, dh * 512:(dh + 1) * 512]
                    ins = v.scalar_tensor_tensor(out=w, in0=ps[un.bank(n_)][:, :], scalar=small[:, 38 + tt:39 + tt],
                                                 in1=grow[:, dh * 512:(dh + 1) * 512], op0=ALU.mult, op1=ALU.mult)
                    ins.then_inc(bank_free[un.bank(n_)], 1)
                    un.wait_read(v, n_)
                    r = x3[:, tt, dh * 512:(dh + 1) * 512]
                    link(v.tensor_tensor(r, r, w, ALU.add))
                    v.sem_inc(x1_ready, 1)
            rstd(small[:, 42:44], 3)
            for tt in range(TT):
                ins = v.tensor_scalar(xn3[:, tt, :], x3[:, tt, :], small[:, 42 + tt:43 + tt], None, ALU.mult)
            link(ins)
            v.sem_inc(x1n_ready, 1)
            link(v.memset(arena[:, 6144:6144 + KT * T], 0.0))
            for q in range(4):
                un.wait_full(v, f"h2T{q}")
                for i in range(2):
                    k = 2 * q + i
                    ins = v.tensor_scalar(hT3[:, k, :], ps[4 + q][:, i * T:(i + 1) * T], small[:, 72 + k:73 + k],
                                          mod[:, 24 + k:25 + k], ALU.mult, ALU.add)
                ins.then_inc(bank_free[4 + q], 1)

            un.wait_full(v, "logit")
            logit, expl, sel, rest = lg[:, 0, :], lg[:, 1, :], lg[:, 2, :], lg[:, 3, :]
            ins = v.tensor_copy(logit, ps[0][:, 0:TT * E])
            ins.then_inc(bank_free[0], 1)
            un.wait_read(v, "logit")
            for tt in range(TT):
                ins = v.max(top[:, tt, :], logit[:, tt * E:(tt + 1) * E])
            link(ins)
            link(v.tensor_scalar(small[:, 50:52], top[:, :, 0:1].rearrange("p a b -> p (a b)"), -1.0, None, ALU.mult))
            v.sem_inc(lmax_ready, 1)
            link(v.memset(top[:, :, TOPK:8], 3e38))
            for tt in range(TT):
                ins = v.match_replace(out=rest[:, tt * E:(tt + 1) * E], in_to_replace=top[:, tt, :],
                                      in_values=logit[:, tt * E:(tt + 1) * E], imm_value=-3e38)
            link(ins)
            link(v.tensor_tensor(sel, rest, logit, ALU.not_equal))
            v.sem_inc(sel_ready, 1)
            v.wait_ge(lexp_ready, 2)
            link(v.tensor_tensor(expl, expl, sel, ALU.mult))
            link(v.tensor_reduce(small[:, 52:54], expl.rearrange("p (t e) -> p t e", t=TT), AX_X, ALU.add))
            link(v.reciprocal(small[:, 54:56], small[:, 52:54]))
            link(v.memset(arena[:, 14336:14336 + 4 * (E + 1)], 0.0))
            for tt in range(TT):
                ins = v.tensor_scalar(gate[:, tt, 0:E], expl[:, tt * E:(tt + 1) * E], small[:, 54 + tt:55 + tt], None,
                                      ALU.mult)
            link(ins)
            v.sem_inc(gate_ready, 1)
            un.wait_full(v, "rank")
            for tt in range(TT):
                ins = v.tensor_tensor(lg[:, 4, tt * E:(tt + 1) * E], ps[3][:, tt * E:(tt + 1) * E],
                                      sel[:, tt * E:(tt + 1) * E], ALU.mult)
            ins2 = v.tensor_scalar(lg[:, 5, 0:E], ps[3][:, 2 * E:3 * E], BLK + 0.5, None, ALU.is_ge)
            v.tensor_scalar(lg[:, 5, E:2 * E], ps[3][:, 2 * E:3 * E], 2 * BLK + 0.5, None, ALU.is_ge)
            ins = v.tensor_scalar(lg[:, 6, 0:E], ps[3][:, 2 * E:3 * E], 3 * BLK + 0.5, None, ALU.is_ge)
            ins.then_inc(bank_free[3], 1)
            un.wait_read(v, "rank")
            for tt in range(TT):
                v.tensor_scalar(posm[:, tt, 0:E], lg[:, 4, tt * E:(tt + 1) * E], -1.0, None, ALU.add)
            link(v.tensor_tensor(lg[:, 5, 0:E], lg[:, 5, 0:E], lg[:, 5, E:2 * E], ALU.add))
            link(v.scalar_tensor_tensor(out=lg[:, 5, 0:E], in0=lg[:, 5, 0:E], scalar=1.0, in1=lg[:, 6, 0:E],
                                        op0=ALU.add, op1=ALU.add))
            v.tensor_copy(cls_i[:, :], lg[:, 5, 0:E]).then_inc(cls_ready, 1)

            mod_part("ada_c", 40, 48)
            diagonals(diag2, 40, 3)

            def one_hot(e):
                for tt in range(TT):
                    v.tensor_scalar(S[:, tt, :], iota, posm[:, tt, ds(e, 1)], None, ALU.is_equal)
                    ins = v.tensor_scalar(Sg[:, tt, :], iota, posm[:, tt, ds(e, 1)], gate[:, tt, ds(e, 1)],
                                          ALU.is_equal, ALU.mult)
                ins.then_inc(s_ready, 1)

            v.wait_ge(cls_ready, 1)
            one_hot(0)
            bcur = lg[:, 7, 0:16]
            bup3 = bup[:, :].rearrange("p (q e) -> p q e", e=E)
            with v.Fori(0, E) as e:
                u = xunits(e)
                n_blk = v.value_load(cls_i[0:1, ds(e, 1)])
                v.tensor_copy(bcur, bup3[:, :, ds(e, 1)].rearrange("p q e -> p (q e)")).then_inc(bcur_ready, 1)
                u.wait_full(v, "xg3")
                one_hot(e + 1)

                def body(nb):
                    n = nb * BLK

                    def biased(j):
                        if j >= 2:
                            v.wait_ge(act_ready, 8 * e + j - 1)
                        u.wait_full(v, f"up{j}")
                        b = ps[u.bank(f"up{j}")]
                        v.tensor_scalar(xw[:, j % 2, 0:n], b[:, 0:n], bcur[:, 2 * j:2 * j + 1], LIMIT,
                                        ALU.add, ALU.min).then_inc(g_ready, 1)
                        v.tensor_scalar(xw[:, 2 + j % 2, 0:n], b[:, T:T + n], bcur[:, 2 * j + 1:2 * j + 2], LIMIT,
                                        ALU.add, ALU.min).then_inc(bank_free[u.bank(f"up{j}")], 1)

                    def finish(j):
                        u.wait_read(v, f"up{j}")
                        v.tensor_scalar(xw[:, 2 + j % 2, 0:n], xw[:, 2 + j % 2, 0:n], -LIMIT, 1.0,
                                        ALU.max, ALU.add).then_inc(l_ready, 1)
                        v.wait_ge(sg_ready, 8 * e + j + 1)
                        v.tensor_tensor(xw[:, 6 + j % 2, 0:n], xw[:, j % 2, 0:n], xw[:, 4 + j % 2, 0:n],
                                        ALU.mult).then_inc(m_ready, 1)
                        v.wait_ge(l_ready, 8 * e + j + 1)
                        v.wait_ge(m_ready, 8 * e + j + 1)
                        v.tensor_tensor(actT[:, j, 0:n], xw[:, 6 + j % 2, 0:n], xw[:, 2 + j % 2, 0:n],
                                        ALU.mult).then_inc(act_ready, 1)

                    v.wait_ge(bcur_ready, e + 1)
                    for j in range(9):
                        if j < 8:
                            biased(j)
                        if j >= 1:
                            finish(j - 1)

                by_size(v, n_blk, body)

            rstd(small[:, 46:48], 4)
            un.wait_read(v, "grow2a")
            un.wait_read(v, "grow2b")
            for tt in range(TT):
                for dh in range(2):
                    w = xn3[:, tt, dh * 512:(dh + 1) * 512]
                    link(v.scalar_tensor_tensor(out=w, in0=ps[2 * tt + dh][:, :], scalar=small[:, 46 + tt:47 + tt],
                                                in1=grow[:, dh * 512:(dh + 1) * 512], op0=ALU.mult, op1=ALU.mult))
                    v.tensor_tensor(w, w, x3[:, tt, dh * 512:(dh + 1) * 512], ALU.add).then_inc(out_ready, 1)


_OUT = (1, T, D)


def kernel(**inputs):
    import concourse.bacc as _bacc
    from concourse.bass_utils import run_bass_kernel_spmd as _run

    nc = _bacc.Bacc("TRN2", target_bir_lowering=False, num_devices=1)
    arrays, a = {}, {}
    for name, value in list(inputs.items()) + [("cst", constants())]:
        v = np.ascontiguousarray(value)
        arrays[f"in_{name}"] = v
        a[name] = nc.dram_tensor(f"in_{name}", v.shape, mybir.dt.from_np(v.dtype), kind="ExternalInput").ap()
    out = nc.dram_tensor("out_0", _OUT, F32, kind="ExternalOutput").ap()
    layer_kernel(nc, a, out)
    r = _run(nc, [arrays], core_ids=[0])
    return r.results[0]["out_0"]
```

```python
from contextlib import ExitStack

import numpy as np

import concourse.bass as bass
from concourse import mybir

ALU = mybir.AluOpType
ACT = mybir.ActivationFunctionType
F32 = mybir.dt.float32
I32 = mybir.dt.int32
AX_X = mybir.AxisListType.X
ds = bass.ds

P = 128
D = 1024
KT = D // P
T = 256
TT = T // P
HD = 64
NG, SLOTS = 3, 4
DIL_W = NG * SLOTS * HD
SB_H = 8
SB_W = SB_H * HD
QA, KA, VA = 0, DIL_W, 2 * DIL_W
QB = 3 * DIL_W
KB, VB = QB + SB_W, QB + 2 * SB_W
GA = QB + 3 * SB_W
GB = GA + D
HALF = 8
E = 32
TOPK = 4
F = 1024
FT = F // P
LIMIT, ALPHA = 7.0, 1.702
EPS = 1e-6
SCALE = HD ** -0.5
NEG = -1e30
CW = 512
RING = 6
PASSES = [[(4, 0)], [(2, 0)], [(1, 0)], [(1, 0), (4, 128)], [(1, 0), (2, 128)], [(1, 0), (1, 128)]]
CLASS_FROM = [33, 65, 129, 161, 193]
GROUPS = max(sum(G for G, _ in k) for k in PASSES) - 1
SUB = 4
TRI = 384

C_ID, C_ONE, C_LE, C_GE, C_ST, C_NG, C_IOTA = 0, 128, 256, 384, 512, 640, 768
C_MASK = C_IOTA + T
C_FREQ = C_MASK + NG * P + NG * T
C_EPS = C_FREQ + HALF
C_SEL = C_EPS + 1
C_I32 = C_SEL + 1
C_I64 = C_I32 + P
C_W = C_I64 + P

R_ADAB, R_G = 0, 48
R_C = R_G + 4 * KT
R_N = R_C + KT


def constants():
    i = np.arange(P)
    c = np.zeros((P, C_W), np.float32)
    c[:, C_ID:C_ID + P] = np.eye(P)
    c[:, C_ONE:C_ONE + P] = 1.0
    c[:, C_LE:C_LE + P] = i[:, None] <= i[None, :]
    c[:, C_GE:C_GE + P] = i[:, None] >= i[None, :]
    c[:, C_ST:C_ST + P] = i[:, None] < i[None, :]
    c[:, C_NG:C_NG + P] = np.where(i[:, None] < i[None, :], 0.0, NEG)
    c[:, C_IOTA:C_IOTA + T] = np.arange(T)[None, :]
    at = C_MASK
    for tt in range(TT):
        for window, dil in ((128, 1), (512, 4), (2048, 16)):
            dist = (tt * P + i)[:, None] - np.arange((tt + 1) * P)[None, :]
            ok = (dist >= 0) & (dist <= window) & (dist % dil == 0)
            c[:, at:at + dist.shape[1]] = np.where(ok, 0.0, NEG)
            at += dist.shape[1]
    freq = (500000.0 ** (-(np.arange(HALF, dtype=np.float32) * 2.0 / (2 * HALF)))).astype(np.float32)
    c[:, C_FREQ:C_FREQ + HALF] = freq[None, :]
    c[:, C_EPS] = EPS
    c[:, C_SEL] = i % 32 == 0
    c[:, C_I32:C_I32 + P] = (i % 32)[None, :]
    c[:, C_I64:C_I64 + P] = (i % 64)[None, :]
    return c


def two_pi_parts():
    a = np.float32(6.28125)
    b = np.float32(np.round((2 * np.pi - float(a)) * 2.0 ** 20) / 2.0 ** 20)
    return float(a), float(b), float(np.float32(2 * np.pi - float(a) - float(b)))


class Units:

    def __init__(self, full, free):
        self.full, self.free, self.count, self.place = full, free, [0] * 8, {}

    def add(self, name, bank):
        self.place[name] = (bank, self.count[bank])
        self.count[bank] += 1

    def bank(self, name):
        return self.place[name][0]

    def wait_free(self, eng, name):
        b, n = self.place[name]
        if not isinstance(n, int) or n > 0:
            eng.wait_ge(self.free[b], n)

    def wait_full(self, eng, name):
        b, n = self.place[name]
        eng.wait_ge(self.full[b], n + 1)

    def wait_read(self, eng, name):
        b, n = self.place[name]
        eng.wait_ge(self.free[b], n + 1)


def layer_kernel(nc, a, out):
    ctx = ExitStack()
    with ctx:
        def sb(name, width, dt=F32, rows=P):
            return ctx.enter_context(nc.sbuf_tensor(name, [rows, width], dt))

        def sem(name):
            return ctx.enter_context(nc.semaphore(name))

        ring = sb("ring", RING * KT * CW)
        cst = sb("cst", C_W)
        x_res = sb("x_res", TT * D)
        xn = sb("xn", TT * D)
        hT = sb("hT", KT * T)
        arena = sb("arena", 14848)
        yaT = sb("yaT", 2 * T)
        ybT = sb("ybT", 4 * T)
        grow = sb("grow", D)
        b_down_sb = sb("b_down_sb", D, rows=E)
        bup = sb("bup", CW)
        silu_rep = sb("silu_rep", KT * 32)
        w_router_sb = sb("w_router_sb", KT * E)
        cols = sb("cols", R_N)
        mod = sb("mod", 48)
        small = sb("small", 96)
        rope = sb("rope", 6 * TT * HALF)
        pos_i = sb("pos_i", TT, I32)
        small_rows = sb("small_rows", P, rows=R_N)
        b_router_sb = sb("b_router_sb", E, rows=1)
        cls_i = sb("cls_i", E + 1, I32)

        ident = cst[:, C_ID:C_ID + P]
        ones = cst[:, C_ONE:C_ONE + P]
        tri_le = cst[:, C_LE:C_LE + P]
        tri_ge = cst[:, C_GE:C_GE + P]
        iota = cst[:, C_IOTA:C_IOTA + T]

        def slot(g):
            s = g % RING
            return ring[:, s * KT * CW:(s + 1) * KT * CW]

        def chunk(g, width=CW, kt=KT):
            return slot(g)[:, 0:kt * width].rearrange("p (k n) -> p k n", k=kt)

        x3 = x_res[:, :].rearrange("p (t d) -> p t d", t=TT)
        xn3 = xn[:, :].rearrange("p (t d) -> p t d", t=TT)
        hT3 = hT[:, :].rearrange("p (k t) -> p k t", k=KT)

        def region(at, shape):
            n = int(np.prod(shape))
            v = arena[:, at:at + n]
            if len(shape) == 2:
                v = v.rearrange("p (x y) -> p x y", x=shape[0])
            elif len(shape) == 3:
                v = v.rearrange("p (x y z) -> p x y z", x=shape[0], y=shape[1])
            return v

        qk = region(0, (TT, 2 * DIL_W))
        vtok = region(3072, (TT, DIL_W + SB_W))
        qkT = region(5632, (12, T))
        sbT = region(8704, (8, T))
        gates = region(10752, (16, T))
        sbw = region(10752, (10, TRI))
        prob = xn[:, 0:NG * P + NG * T]
        probT = region(8704, (NG, TRI))
        merged = region(0, (KT, T))
        brw = region(2048, (4, T))
        h2 = region(0, (TT, D))
        XT = region(2048, (KT, T))
        hid = region(4096, (2, 4 * CW // 2))
        hidT = region(6144, (2, D))
        Y = region(8192, (2, D))
        S = region(10240, (TT, T))
        Sg = region(10752, (2, TT * P))
        GT = region(11264, (2, T))
        xw = region(11776, (8, T))
        pick = yaT[:, :].rearrange("p (c m) -> p c m", c=4)
        lg = region(13824, (8, TT * E))
        posm = region(14336, (TT, E + 1))
        gate = region(14336 + 2 * (E + 1), (TT, E + 1))
        top = region(14336 + 4 * (E + 1), (TT, 8))
        posm2 = region(14336 + 4 * (E + 1) + 16, (TT, E + 1))
        gT = region(14592, (T,))
        def junk(tt):
            return arena[:, 8192 + tt * D:8192 + (tt + 1) * D]

        diag1 = hT[:, 0:D]
        diag2 = region(2048, (D,))

        psum = ctx.enter_context(nc.psum_tensor("psum", [P, 8 * 512], F32))
        ps = [psum[:, b * 512:(b + 1) * 512] for b in range(8)]

        bank_full = [sem(f"bank_full{b}") for b in range(8)]
        bank_free = [sem(f"bank_free{b}") for b in range(8)]
        slot_full = [sem(f"slot_full{s}") for s in range(RING)]
        ld_cst, ld_rows, ld_x, ld_pos, ld_small = map(sem, (
            "ld_cst", "ld_rows", "ld_x", "ld_pos", "ld_small"))
        xn_ready, ec_ready, silu_ready, ang_ready, rope_ready = map(sem, (
            "xn_ready", "ec_ready", "silu_ready", "ang_ready", "rope_ready"))
        rot_done, pick_ready, sb_na, sb_e, sb_ln = map(sem, (
            "rot_done", "pick_ready", "sb_na", "sb_e", "sb_ln"))
        sb_sp, sb_l, sb_w, dl_max, dl_exp = map(sem, (
            "sb_sp", "sb_l", "sb_w", "dl_max", "dl_exp"))
        dl_p, sig_ready, merged_ready, diag_ready, x1_ready = map(sem, (
            "dl_p", "sig_ready", "merged_ready", "diag_ready", "x1_ready"))
        x1n_ready, sel_ready, lexp_ready, lmax_ready, gate_ready = map(sem, (
            "x1n_ready", "sel_ready", "lexp_ready", "lmax_ready", "gate_ready"))
        cls_ready, s_ready, g_ready, sg_ready = map(sem, (
            "cls_ready", "s_ready", "g_ready", "sg_ready"))
        m_ready, act_ready, acc_done, out_ready, stored = map(sem, (
            "m_ready", "act_ready", "acc_done", "out_ready", "stored"))
        rms_ready, sq_ready = map(sem, (
            "rms_ready", "sq_ready"))
        up_full, up_read, dn_full, dn_read, at_full, at_read, gt_full, gt_read, xg_full, xg_read = map(sem, (
            "up_full", "up_read", "dn_full", "dn_read", "at_full", "at_read", "gt_full", "gt_read",
            "xg_full", "xg_read"))
        part_full, part_read = sem("part_full"), sem("part_read")
        group_added = sem("group_added")
        chain = sem("chain")

        front = []
        where = {}

        def add_chunk(name, src, kt=KT, width=CW):
            where[name] = len(front)
            front.append((src.rearrange("(k p) n -> p k n", p=P), kt, width))

        ada = a["ada_w"][0]
        w_in = a["w_in"][0]
        for m in range(4):
            add_chunk(f"ada{m}", ada[:, m * CW:(m + 1) * CW])
        for name, c0 in (("sbq", QB), ("sbk", KB), ("sbv", VB), ("qk0", 0), ("qk1", CW), ("qk2", 2 * CW), ("va0", VA)):
            add_chunk(name, w_in[:, c0:c0 + CW])
        add_chunk("va1", w_in[:, VA + CW:VA + DIL_W], KT, DIL_W - CW)
        for m in range(4):
            add_chunk(f"gate{m}", w_in[:, GA + m * CW:GA + (m + 1) * CW])
        add_chunk("wa", a["w_branch_a"][0], 2, D)
        add_chunk("wb", a["w_branch_b"][0], 4, D)
        for m in range(4, 10):
            add_chunk(f"ada{m}", ada[:, m * CW:(m + 1) * CW])
        for m in range(2):
            add_chunk(f"wo{m}", a["w_out"][0][:, m * CW:(m + 1) * CW])
        for m in range(10, 12):
            add_chunk(f"ada{m}", ada[:, m * CW:(m + 1) * CW])
        NF = len(front)

        un = Units(bank_full, bank_free)
        un.add("rows", 7)
        for q in range(4):
            un.add(f"hT{q}", q)
        for m in range(4):
            un.add(f"ar{m}", 4 + m % 2)
        un.add("ada_a", 7)
        rot = []
        for n in ("sbq0", "sbq1", "sbk0", "sbk1", "sbv0", "sbv1", "qk00", "qk01", "qk10", "qk11", "qk20", "qk21",
                  "va00", "va01", "va1", "qkT0", "qkT1", "qkT2", "qkT3", "qkT4", "qkT5"):
            un.add(n, len(rot) % 2)
            rot.append(n)
        for h in range(SB_H):
            un.add(f"z{h}", 2 + h % 2)
            un.add(f"c{h}", 4 + h % 2)
            if h % 2:
                un.add(f"sbo{h // 2}", 6 + h // 2 % 2)
        for i in range(SLOTS):
            for b in range(3):
                un.add(f"s{i}{b}", 2 + b)
            un.add(f"g{2 * i}", 0)
            for g in range(NG):
                un.add(f"pT{i}{g}", 5 + g)
            un.add(f"g{2 * i + 1}", 0)
            if i % 2:
                un.add(f"dlo{i // 2}", 1)
        for m in range(KT):
            un.add(f"br{m}", 2 + m % 4)
        for m in range(4, 10):
            un.add(f"ar{m}", 4 + m % 2)
        un.add("ada_b", 6)
        un.add("grow1a", 6)
        un.add("grow1b", 7)
        for dh in range(2):
            for tt in range(TT):
                un.add(f"y{tt}{dh}", 2 * tt + dh)
        for q in range(4):
            un.add(f"h2T{q}", 4 + q)
        un.add("logit", 0)
        for n, b in (("hb00", 4), ("hb01", 5), ("hb10", 6), ("hb11", 7)):
            un.add(n, b)
        un.add("ar10", 2)
        un.add("ar11", 3)
        un.add("ada_c", 1)
        un.add("gateT", 2)
        un.add("rank", 3)
        un.add("grow2a", 4)
        un.add("grow2b", 5)
        for b in range(4):
            un.add(f"acc{b}", b)
        released = {}
        for name, unit in [(f"ada{m}", f"ar{m}") for m in range(12)] + [("sbq", "sbq1"), ("sbk", "sbk1"),
                           ("sbv", "sbv1"), ("qk0", "qk01"), ("qk1", "qk11"), ("qk2", "qk21"), ("va0", "va01"),
                           ("va1", "va1"), ("gate0", "g1"), ("gate1", "g3"), ("gate2", "g5"), ("gate3", "g7"),
                           ("wa", "br7"), ("wb", "br7"), ("wo0", "y10"), ("wo1", "y11")]:
            b, n = un.place[unit]
            released[name] = (bank_full[b], n + 1)
        names = sorted(where, key=where.get)

        front_fills = [16 * len(range(b, NF, RING)) for b in range(RING)]

        def expert_slot(e, c):
            b = (NF + c) % RING
            return slot(NF + c), slot_full[b], front_fills[b] + (e + 1) * (16 if c < 4 else 64)

        def by_class(eng, cls, body):
            def split(a, b):
                if a == b:
                    return body(a)
                m = (a + b) // 2
                with eng.If(cls <= m):
                    split(a, m)
                with eng.Else():
                    split(m + 1, b)
            split(0, len(PASSES) - 1)

        block = ctx.enter_context(nc.Block())

        @block.sync
        def _(sp):
            rows = small_rows
            for r, name, count in ((R_C, "c", KT), (R_ADAB, "ada_b", 48), (R_G, "norm_mix_pre", KT),
                                   (R_G + KT, "norm_mix_post", KT), (R_G + 2 * KT, "norm_ffn_pre", KT),
                                   (R_G + 3 * KT, "norm_ffn_post", KT)):
                sp.dma_start(rows[r:r + count, :], a[name][0].rearrange("(k p) -> k p", p=P)).then_inc(ld_rows, 16)
            sp.dma_start(cst[:, :], a["cst"]).then_inc(ld_cst, 16)
            sp.dma_start(x3, a["x"][0].rearrange("(t p) d -> p t d", p=P)).then_inc(ld_x, 16)
            for g, (src, kt, width) in enumerate(front):
                if g >= RING:
                    sp.wait_ge(*released[names[g - RING]])
                sp.dma_start(chunk(g, width, kt), src).then_inc(slot_full[g % RING], 16)

            def expert_chunks(e, first):
                for c in range(6):
                    if first:
                        sp.wait_ge(*released[names[NF + c - RING]])
                    elif c < 4:
                        sp.wait_ge(up_full, e * 4 - 3 + c)
                    else:
                        sp.wait_ge(dn_full, e * 2 - 1 + c - 4)
                    to, full, _ = expert_slot(e, c)
                    to = to.rearrange("p (k n) -> p k n", k=KT)
                    if c < 4:
                        src = a["w_up"][0][ds(e, 1), :, c * CW:(c + 1) * CW]
                        sp.dma_start(to, src.rearrange("e (k p) n -> p (e k) n", p=P)).then_inc(full, 16)
                        continue
                    src = a["w_down"][0][ds(e, 1), :, (c - 4) * CW:(c - 3) * CW]
                    src = src.rearrange("e (u h s f) n -> u h f (e s) n", u=2, h=2, s=SUB)
                    for u in range(2):
                        for h in range(2):
                            sp.dma_start(to[h * 64:(h + 1) * 64, u * SUB:(u + 1) * SUB, :],
                                         src[u, h]).then_inc(full, 16)

            expert_chunks(0, True)
            with sp.Fori(1, E) as e:
                expert_chunks(e, False)
            for tt in range(TT):
                sp.wait_ge(out_ready, 2 * (tt + 1))
                sp.dma_start(out[0, tt * P:(tt + 1) * P, :], xn3[:, tt, :]).then_inc(stored, 16)
            sp.wait_ge(stored, 16 * TT)

        @block.tensor
        def _(pe):
            def arrived(name):
                g = where[name]
                pe.wait_ge(slot_full[g % RING], 16 * (g // RING + 1))
                return g

            def fill(name, steps):
                un.wait_free(pe, name)
                for s in steps:
                    ins = pe.matmul(s[0], s[1], s[2], start=s[3], stop=s[4], skip_group_check=True)
                ins.then_inc(bank_full[un.bank(name)], 1)

            def turn(name, pairs):
                un.wait_free(pe, name)
                for o, i_, idn in pairs:
                    ins = pe.transpose(o, i_, idn)
                ins.then_inc(bank_full[un.bank(name)], 1)

            def bank(name):
                return ps[un.bank(name)]

            def tok_unit(name, w, tt, width=CW, col=0, last=True, first=True):
                o = bank(name)[:, col:col + width]
                return [(o, hT3[:, k, tt * P:(tt + 1) * P], w[:, k, 0:width], k == 0, k == KT - 1) for k in range(KT)]

            def chan_unit(name, w, m0):
                r = []
                for m in range(2):
                    c0 = (m0 + m) * P
                    r += [(bank(name)[:, m * T:(m + 1) * T], w[:, k, c0:c0 + P], hT3[:, k, :], k == 0, k == KT - 1)
                          for k in range(KT)]
                return r

            def ada_part(unit, ms):
                def rows(m):
                    name = f"ar{m}"
                    w = chunk(arrived(f"ada{m}"))
                    fill(name, [(bank(name)[32 * (k % 4):32 * (k % 4) + 32, :], silu_rep[:, k * 32:(k + 1) * 32],
                                 w[:, k, :], k < 4, k >= 4) for k in range(KT)])

                def columns(n, m):
                    un.wait_read(pe, f"ar{m}")
                    for q in range(4):
                        ins = pe.matmul(bank(unit)[:, 4 * n + q:4 * n + q + 1],
                                        grow[:, m % 2 * CW + q * P:m % 2 * CW + (q + 1) * P],
                                        cst[:, C_SEL:C_SEL + 1], start=True, stop=True, skip_group_check=True)
                    return ins

                un.wait_free(pe, unit)
                pe.wait_ge(silu_ready, 1)
                for n, m in enumerate(ms):
                    rows(m)
                    if n:
                        columns(n - 1, ms[n - 1])
                columns(len(ms) - 1, ms[-1]).then_inc(bank_full[un.bank(unit)], 1)

            pe.wait_ge(ld_cst, 16)
            pe.wait_ge(ld_rows, 96)
            turn("rows", [(bank("rows")[:, 0:R_N], small_rows[:, :], cst[0:R_N, C_ID:C_ID + R_N])])
            for q in range(4):
                if q == 0:
                    pe.wait_ge(xn_ready, 1)
                turn(f"hT{q}", [(ps[q][:, i * T + tt * P:i * T + (tt + 1) * P],
                                 xn3[:, tt, (2 * q + i) * P:(2 * q + i + 1) * P], ident)
                                for i in range(2) for tt in range(TT)])
            ada_part("ada_a", range(4))
            for q in range(4):
                un.wait_read(pe, f"hT{q}")
            for n in ("sbq", "sbk"):
                g = arrived(n)
                for m in range(2):
                    fill(f"{n}{m}", chan_unit(f"{n}{m}", chunk(g), 2 * m))
            g = arrived("sbv")
            for tt in range(TT):
                fill(f"sbv{tt}", tok_unit(f"sbv{tt}", chunk(g), tt))

            def sb_head(h):
                r = slice(h % 2 * HD, h % 2 * HD + HD)
                return sbT[r, h // 2, :], sbT[r, 4 + h // 2, :]

            def sb_scores(h):
                if h == 0:
                    for n in ("sbv0", "sbv1"):
                        un.wait_read(pe, n)
                q, k = sb_head(h)
                z = bank(f"z{h}")
                fill(f"z{h}", [(z[:, 0:T], k[:, 0:P], q, True, True),
                               (z[:, T:TRI], k[:, P:T], q[:, P:T], True, True)])

            def sb_sums(h):
                pe.wait_ge(sb_sp, h + 1)
                sp_ = sbw[:, 6 + h % 2, :]
                c = bank(f"c{h}")
                fill(f"c{h}", [(c[:, 0:T], tri_ge, sp_[:, 0:T], True, False),
                               (c[:, P:T], ones, sp_[:, T:TRI], False, True),
                               (c[:, T:TRI], tri_ge, sp_[:, T:TRI], True, True)])

            def sb_out(h):
                pe.wait_ge(sb_w, h + 1)
                w = sbw[:, 4 + h % 2, :]
                v = [vtok[:, tt, DIL_W + h * HD:DIL_W + (h + 1) * HD] for tt in range(TT)]
                name = f"sbo{h // 2}"
                if h % 2 == 0:
                    un.wait_free(pe, name)
                o = bank(name)[h % 2 * HD:h % 2 * HD + HD, :]
                pe.matmul(o[:, 0:T], v[0], w[:, 0:T], start=True, stop=False, skip_group_check=True)
                ins = pe.matmul(o[:, P:T], v[1], w[:, T:TRI], start=False, stop=True, skip_group_check=True)
                if h % 2:
                    ins.then_inc(bank_full[un.bank(name)], 1)

            dil = [("qk00", "qk0", 0), ("qk01", "qk0", 1), ("qk10", "qk1", 0), ("qk11", "qk1", 1),
                   ("qk20", "qk2", 0), ("qk21", "qk2", 1), ("va00", "va0", 0), ("va01", "va0", 1)]
            for h in range(SB_H + 2):
                if h < len(dil):
                    unit, cname, tt = dil[h]
                    g = arrived(cname)
                    fill(unit, tok_unit(unit, chunk(g), tt))
                elif h == len(dil):
                    g = arrived("va1")
                    w = chunk(g, DIL_W - CW)
                    fill("va1", tok_unit("va1", w, 0, DIL_W - CW) + tok_unit("va1", w, 1, DIL_W - CW, T))
                if h < SB_H:
                    sb_scores(h)
                if 1 <= h <= SB_H:
                    sb_sums(h - 1)
                if h >= 2:
                    sb_out(h - 2)
            pe.wait_ge(rot_done, 1)
            for u in range(6):
                turn(f"qkT{u}", [(bank(f"qkT{u}")[:, i * T + tt * P:i * T + (tt + 1) * P],
                                  qk[:, tt, (2 * u + i) * P:(2 * u + i + 1) * P], ident)
                                 for i in range(2) for tt in range(TT)])

            def gate_unit(n):
                cname = f"gate{n // 2}"
                g = arrived(cname)
                fill(f"g{n}", chan_unit(f"g{n}", chunk(g), 2 * (n % 2)))

            def dil_head(i, g):
                h = g * SLOTS + i
                r = slice(h % 2 * HD, h % 2 * HD + HD)
                return qkT[r, h // 2, :], qkT[r, 6 + h // 2, :]

            for i in range(SLOTS):
                if i == 0:
                    un.wait_read(pe, "qkT4")
                    un.wait_read(pe, "qkT5")
                qk_h = [dil_head(i, g) for g in range(NG)]
                fill(f"s{i}0", [(ps[2][:, g * P:(g + 1) * P], q[:, 0:P], k[:, 0:P], True, True)
                                for g, (q, k) in enumerate(qk_h)])
                fill(f"s{i}1", [(ps[3][:, g * T:(g + 1) * T], q[:, P:T], k, True, True)
                                for g, (q, k) in enumerate(qk_h[0:2])])
                fill(f"s{i}2", [(ps[4][:, 0:T], qk_h[2][0][:, P:T], qk_h[2][1], True, True)])
                gate_unit(2 * i)
                pe.wait_ge(dl_p, i + 1)
                for g in range(NG):
                    b = bank(f"pT{i}{g}")
                    p1 = NG * P + g * T
                    turn(f"pT{i}{g}", [(b[:, 0:P], prob[:, g * P:(g + 1) * P], ident),
                                       (b[:, P:T], prob[:, p1:p1 + P], ident),
                                       (b[:, T:TRI], prob[:, p1 + P:p1 + T], ident)])
                gate_unit(2 * i + 1)
                for g in range(NG):
                    un.wait_read(pe, f"pT{i}{g}")
                name = f"dlo{i // 2}"
                if i % 2 == 0:
                    un.wait_free(pe, name)
                o = bank(name)[i % 2 * HD:i % 2 * HD + HD, :]
                for g in range(NG):
                    h = g * SLOTS + i
                    pe.matmul(o[:, 0:T], vtok[:, 0, h * HD:(h + 1) * HD], probT[:, g, 0:T],
                              start=(g == 0), stop=False, skip_group_check=True)
                    ins = pe.matmul(o[:, P:T], vtok[:, 1, h * HD:(h + 1) * HD], probT[:, g, T:TRI],
                                    start=False, stop=(g == NG - 1), skip_group_check=True)
                if i % 2:
                    ins.then_inc(bank_full[un.bank(name)], 1)

            ga_, gb_ = arrived("wa"), arrived("wb")
            wa, wb = chunk(ga_, D, 2), chunk(gb_, D, 4)
            for n in ("sbo0", "sbo1", "sbo2", "sbo3", "dlo0", "dlo1"):
                un.wait_read(pe, n)
            for m in range(KT):
                b = bank(f"br{m}")
                fill(f"br{m}", [(b[:, 0:T], wa[:, k, m * P:(m + 1) * P],
                                        yaT[:, k * T:(k + 1) * T], k == 0, k == 1) for k in range(2)] +
                            [(b[:, T:2 * T], wb[:, k, m * P:(m + 1) * P],
                              ybT[:, k * T:(k + 1) * T], k == 0, k == 3) for k in range(4)])
            ada_part("ada_b", range(4, 10))

            def spread(unit, n, dg, half):
                pe.wait_ge(diag_ready, n)
                fill(unit, [(bank(unit)[:, :], ones, dg[:, half * 512:(half + 1) * 512], True, True)])

            spread("grow1a", 1, diag1, 0)
            spread("grow1b", 1, diag1, 1)
            pe.wait_ge(merged_ready, 1)
            for dh in range(2):
                g = arrived(f"wo{dh}")
                for tt in range(TT):
                    n = f"y{tt}{dh}"
                    fill(n, [(bank(n)[:, :], merged[:, k, tt * P:(tt + 1) * P], chunk(g)[:, k, :],
                                    k == 0, k == KT - 1) for k in range(KT)])
            pe.wait_ge(x1n_ready, 1)
            for q in range(4):
                turn(f"h2T{q}", [(ps[4 + q][:, i * T + tt * P:i * T + (tt + 1) * P],
                                  xn3[:, tt, (2 * q + i) * P:(2 * q + i + 1) * P], ident)
                                 for i in range(2) for tt in range(TT)])
            for q in range(4):
                un.wait_read(pe, f"h2T{q}")
            pe.wait_ge(ld_small, 64)
            fill("logit", [s for tt in range(TT) for s in
                           [(ps[0][:, tt * E:(tt + 1) * E], hT3[:, k, tt * P:(tt + 1) * P],
                             w_router_sb[:, k * E:(k + 1) * E], k == 0, False) for k in range(KT)] +
                           [(ps[0][:, tt * E:(tt + 1) * E], cst[0:1, C_ONE:C_ONE + P],
                             b_router_sb[0:1, :], False, True)]])
            for tt in range(TT):
                for hf in range(2):
                    n = f"hb{tt}{hf}"
                    turn(n, [(bank(n)[:, k * P:(k + 1) * P], hT3[:, 4 * hf + k, tt * P:(tt + 1) * P], ident)
                             for k in range(4)])
            ada_part("ada_c", range(10, 12))
            pe.wait_ge(sel_ready, 1)
            sel = lg[:, 2, :]
            fill("rank", [(ps[3][:, 0:E], tri_le, sel[:, 0:E], True, True),
                          (ps[3][:, E:2 * E], ones, sel[:, 0:E], True, False),
                          (ps[3][:, E:2 * E], tri_le, sel[:, E:2 * E], False, True),
                          (ps[3][:, 2 * E:3 * E], ones, sel[:, 0:E], True, False),
                          (ps[3][:, 2 * E:3 * E], ones, sel[:, E:2 * E], False, True)])
            pe.wait_ge(gate_ready, 1)
            turn("gateT", [(ps[2][0:E, tt * P:(tt + 1) * P], gate[:, tt, 0:E], ident) for tt in range(TT)])
            spread("grow2a", 2, diag2, 0)
            spread("grow2b", 2, diag2, 1)
            un.wait_read(pe, "gateT")
            for b in range(4):
                tt, dh = b // 2, b % 2
                un.wait_free(pe, f"acc{b}")
                pe.matmul(ps[b][:, :], gT[0:E, tt * P:(tt + 1) * P], b_down_sb[:, dh * 512:(dh + 1) * 512],
                          start=True, stop=True, skip_group_check=True)

            for n in ("hb00", "hb01", "hb10", "hb11"):
                un.wait_read(pe, n)
            un.wait_read(pe, "grow2a")
            un.wait_read(pe, "grow2b")
            pe.wait_ge(cls_ready, 1)
            with pe.Fori(0, E) as e:
                cls = pe.value_load(cls_i[0:1, ds(e, 1)])

                def body(k):
                    passes = PASSES[k]
                    n_p = len(passes)
                    n = passes[-1][1] + P // passes[-1][0]

                    def groups(bank_, lhsT, rhs, G, first, last):
                        M, W = P // G, CW // G
                        for g in range(G):
                            ins = pe.matmul(bank_[g * M:(g + 1) * M, 0:W], lhsT, rhs[:, g * W:(g + 1) * W],
                                            start=first, stop=last, skip_group_check=True)
                        return ins

                    pe.wait_ge(s_ready, e + 1)
                    for p in range(n_p):
                        for tt in range(TT):
                            ins = pe.transpose(ps[6][:, p * T + tt * P:p * T + (tt + 1) * P],
                                               Sg[:, p, tt * P:(tt + 1) * P], ident)
                    ins.then_inc(gt_full, 1)
                    for q in range(4):
                        b = ps[4 + q % 2]
                        if q >= 2:
                            pe.wait_ge(xg_read, 4 * e + q - 1)
                        for i in range(2):
                            for tt in range(TT):
                                ins = pe.matmul(b[:, i * T:i * T + n], h2[:, tt, (2 * q + i) * P:(2 * q + i + 1) * P],
                                                S[:, tt, 0:n], start=(tt == 0), stop=(tt == 1), skip_group_check=True)
                        ins.then_inc(xg_full, 1)
                    pe.wait_ge(gt_read, e + 1)
                    pe.wait_ge(pick_ready, e + 1)
                    pe.wait_ge(xg_read, 4 * e + 4)
                    for c in range(4):
                        w, full, at = expert_slot(e, c)
                        w = w.rearrange("p (k n) -> p k n", k=KT)
                        pe.wait_ge(full, at)
                        for p, (G, t0) in enumerate(passes):
                            last = p == n_p - 1
                            if c >= 2:
                                pe.wait_ge(up_read if last else part_read, e * (4 if last else 8) + c - 1)
                            b = ps[(4 if last else 6) + c % 2]
                            groups(b, pick[:, c, 0:P // G], bup[:, :], G, True, False)
                            for kk in range(KT):
                                ins = groups(b, XT[:, kk, t0:t0 + P // G], w[:, kk, :], G, False, kk == KT - 1)
                            ins.then_inc(up_full if last else part_full, 1)
                    pe.wait_ge(act_ready, 8 * e + 4 * n_p)
                    for p, (G, _) in enumerate(passes):
                        last = p == n_p - 1
                        hk = hid[:, p, 0:4 * CW // 2 // G].rearrange("p (n f) -> p n f", f=P)
                        for u in range(2):
                            for q in range(SUB // G):
                                ins = pe.transpose(ps[(6 if last else 4) + u][:, q * P:(q + 1) * P],
                                                   hk[:, u * (SUB // G) + q, :], ident)
                            ins.then_inc(at_full if last else part_full, 1)
                    pe.wait_ge(at_read, 2 * e + 2)
                    for d in range(2):
                        w, full, at = expert_slot(e, 4 + d)
                        w = w.rearrange("p (k n) -> p k n", k=KT)
                        pe.wait_ge(full, at)
                        for p, (G, _) in enumerate(passes):
                            last = p == n_p - 1
                            M = P // G
                            b = ps[(4 if last else 6) + d]
                            for kk in range(FT):
                                ins = groups(b, hidT[:, p, kk * M:(kk + 1) * M], w[:, kk, :], G, kk == 0, kk == FT - 1)
                            ins.then_inc(dn_full if last else part_full, 1)
                    pe.wait_ge(dn_read, 2 * e + 2)
                    done = 0
                    for p, (G, _) in enumerate(passes):
                        M, W = P // G, CW // G
                        for g in range(G):
                            r = slice(g * M, (g + 1) * M)
                            if done:
                                ins.then_inc(group_added, 1)
                                pe.wait_ge(group_added, GROUPS * e + done)
                            done += 1
                            for tt in range(TT):
                                for d in range(2):
                                    ins = pe.matmul(ps[2 * tt + d][:, g * W:(g + 1) * W],
                                                    GT[r, p, tt * P:(tt + 1) * P], Y[r, p, d * W:(d + 1) * W],
                                                    start=False, stop=True, skip_group_check=True)
                    ins.then_inc(acc_done, 1)
                    if done <= GROUPS:
                        pe.sem_inc(group_added, GROUPS + 1 - done)
                    if n_p == 1:
                        pe.sem_inc(part_full, 8)

                by_class(pe, cls, body)

        @block.scalar
        def _(act):
            for tt in range(TT):
                act.dma_start(pos_i[:, tt:tt + 1], a["positions"][0, tt * P:(tt + 1) * P].rearrange(
                    "(p o) -> p o", o=1)).then_inc(ld_pos, 16)
            act.dma_start(bup[:, :], a["b_up"][0].rearrange("e (c n) -> (e c) n", c=4)).then_inc(ld_small, 16)
            act.dma_start(w_router_sb[:, :].rearrange("p (k n) -> p k n", k=KT),
                          a["w_router"][0].rearrange("(k p) n -> p k n", p=P)).then_inc(ld_small, 16)
            act.dma_start(b_router_sb[:, :], a["b_router"]).then_inc(ld_small, 16)
            act.dma_start(b_down_sb[:, :], a["b_down"][0]).then_inc(ld_small, 16)

            act.wait_ge(ld_x, 16)
            n_sq = [0]

            def root_mean_square(src, tt, dst, junk):
                n_sq[0] += 1
                act.activation(junk, src, ACT.Square, accum_out=small[:, dst + tt:dst + tt + 1]).then_inc(sq_ready, 1)
                act.wait_ge(sq_ready, n_sq[0])
                act.activation(small[:, dst + tt:dst + tt + 1], small[:, dst + tt:dst + tt + 1], ACT.Sqrt,
                               scale=1.0 / D, bias=cst[:, C_EPS:C_EPS + 1]).then_inc(rms_ready, 1)

            act.wait_ge(ld_cst, 16)
            for tt in range(TT):
                root_mean_square(x3[:, tt, :], tt, 18, qk[:, tt, 0:D])
            un.wait_read(act, "rows")
            act.activation(small[:, 8:16], cols[:, R_C:R_C + KT], ACT.Exp, scale=-1.0).then_inc(ec_ready, 1)
            act.wait_ge(ang_ready, 1)
            act.activation(rope[:, 4 * 16:6 * 16], rope[:, 2 * 16:4 * 16], ACT.Sin).then_inc(rope_ready, 1)

            def copy_out(name, dst, src=None):
                un.wait_full(act, name)
                b = ps[un.bank(name)]
                ins = act.activation(dst, b[:, :] if src is None else src, ACT.Copy)
                ins.then_inc(bank_free[un.bank(name)], 1)

            def two(ap):
                return ap.rearrange("p a b -> p (a b)")

            def ada_rows(ms):
                for m in ms:
                    copy_out(f"ar{m}", grow[:, m % 2 * CW:(m % 2 + 1) * CW])

            ada_rows(range(4))
            for m in range(2):
                copy_out(f"sbq{m}", two(sbT[:, 2 * m:2 * m + 2, :]))
            for m in range(2):
                copy_out(f"sbk{m}", two(sbT[:, 4 + 2 * m:6 + 2 * m, :]))
            for tt in range(TT):
                copy_out(f"sbv{tt}", vtok[:, tt, DIL_W:DIL_W + SB_W])

            def sb_exp(h):
                act.wait_ge(sb_na, h + 1)
                act.activation(sbw[:, 2 + h % 2, :], sbw[:, h % 2, :], ACT.Exp).then_inc(sb_e, 1)
                act.wait_ge(sb_e, h + 1)
                act.activation(sbw[:, h % 2, :], sbw[:, 2 + h % 2, :], ACT.Ln, bias=1.0).then_inc(sb_ln, 1)

            def sb_weights(h):
                act.wait_ge(sb_l, h + 1)
                act.activation(sbw[:, 4 + h % 2, :], sbw[:, 8 + h % 2, :], ACT.Exp).then_inc(sb_w, 1)

            def sb_copy(p):
                copy_out(f"sbo{p}", ybT[:, p * T:(p + 1) * T], ps[un.bank(f"sbo{p}")][:, 0:T])

            dil = [("qk00", 0, 0), ("qk01", 1, 0), ("qk10", 0, 1), ("qk11", 1, 1), ("qk20", 0, 2), ("qk21", 1, 2),
                   ("va00", 0, 3), ("va01", 1, 3)]
            for h in range(SB_H + 2):
                if h < len(dil):
                    n, tt, c = dil[h]
                    dst = qk[:, tt, c * CW:(c + 1) * CW] if c < 3 else vtok[:, tt, 0:CW]
                    copy_out(n, dst)
                elif h == len(dil):
                    copy_out("va1", vtok[:, :, CW:DIL_W], ps[un.bank("va1")][:, :].rearrange("p (t n) -> p t n", t=TT))
                if h < SB_H:
                    sb_exp(h)
                if 1 <= h <= SB_H:
                    sb_weights(h - 1)
                if h >= 2 and h % 2 == 1:
                    sb_copy((h - 2) // 2)
            for u in range(6):
                copy_out(f"qkT{u}", two(qkT[:, 2 * u:2 * u + 2, :]))

            def gate_copy(n):
                copy_out(f"g{n}", two(gates[:, 2 * n:2 * n + 2, :]))

            for i in range(SLOTS):
                act.wait_ge(dl_max, i + 1)
                act.activation(prob[:, 0:NG * P], prob[:, 0:NG * P], ACT.Exp, bias=small[:, 26:27], scale=SCALE,
                               accum_out=small[:, 28:29]).then_inc(dl_exp, 1)
                act.activation(prob[:, NG * P:], prob[:, NG * P:], ACT.Exp, bias=small[:, 27:28], scale=SCALE,
                               accum_out=small[:, 29:30]).then_inc(dl_exp, 1)
                gate_copy(2 * i)
                for g in range(NG):
                    copy_out(f"pT{i}{g}", probT[:, g, :], ps[un.bank(f"pT{i}{g}")][:, 0:TRI])
                gate_copy(2 * i + 1)
                if i % 2:
                    p = i // 2
                    copy_out(f"dlo{p}", yaT[:, p * T:(p + 1) * T], ps[un.bank(f"dlo{p}")][:, 0:T])
            un.wait_read(act, "g7")
            for q in range(4):
                act.activation(two(gates[:, 4 * q:4 * q + 4, :]), two(gates[:, 4 * q:4 * q + 4, :]),
                               ACT.Sigmoid).then_inc(sig_ready, 1)
            ada_rows(range(4, 10))
            copy_out("grow1a", grow[:, 0:512])
            copy_out("grow1b", grow[:, 512:D])
            for tt in range(TT):
                for dh in range(2):
                    un.wait_full(act, f"y{tt}{dh}")
                root_mean_square(psum[:, 2 * tt * 512:(2 * tt + 2) * 512], tt, 38, junk(tt))
            for tt in range(TT):
                act.wait_ge(x1_ready, 2 * tt + 2)
                root_mean_square(x3[:, tt, :], tt, 42, junk(tt))
            for tt in range(TT):
                for hf in range(2):
                    copy_out(f"hb{tt}{hf}", h2[:, tt, hf * 512:(hf + 1) * 512])
            ada_rows(range(10, 12))
            act.wait_ge(lmax_ready, 1)
            for tt in range(TT):
                act.activation(lg[:, 1, tt * E:(tt + 1) * E], lg[:, 0, tt * E:(tt + 1) * E], ACT.Exp,
                               bias=small[:, 50 + tt:51 + tt]).then_inc(lexp_ready, 1)
            copy_out("gateT", gT[0:E, :], ps[un.bank("gateT")][0:E, 0:T])
            act.wait_ge(x1_ready, 4)
            copy_out("grow2a", grow[:, 0:512])
            copy_out("grow2b", grow[:, 512:D])

            act.wait_ge(cls_ready, 1)
            with act.Fori(0, E) as e:
                cls = act.value_load(cls_i[0:1, ds(e, 1)])

                def body(k):
                    passes = PASSES[k]
                    n_p = len(passes)
                    n = passes[-1][1] + P // passes[-1][0]
                    act.wait_ge(gt_full, e + 1)
                    act.activation(GT[:, 0:n_p, :], ps[6][:, 0:n_p * T].rearrange("p (a b) -> p a b", a=n_p),
                                   ACT.Copy).then_inc(gt_read, 1)
                    for q in range(4):
                        act.wait_ge(xg_full, 4 * e + q + 1)
                        act.activation(XT[:, 2 * q:2 * q + 2, 0:n],
                                       ps[4 + q % 2][:, :].rearrange("p (i t) -> p i t", i=2)[:, :, 0:n],
                                       ACT.Copy).then_inc(xg_read, 1)
                    for j in range(4 * n_p):
                        h = CW // 2 // passes[j % n_p][0]
                        act.wait_ge(g_ready, 8 * e + j + 1)
                        act.activation(xw[:, 4 + j % 2, 0:h], xw[:, j % 2, 0:h], ACT.Sigmoid,
                                       scale=ALPHA).then_inc(sg_ready, 1)
                    if n_p == 1:
                        act.wait_ge(sg_ready, 8 * e + 4)
                        act.sem_inc(sg_ready, 4)

                by_class(act, cls, body)

            act.wait_ge(acc_done, E)
            for tt in range(TT):
                root_mean_square(psum[:, 2 * tt * 512:(2 * tt + 2) * 512], tt, 46, junk(tt))

        @block.vector
        def _(v):
            n_chain = [0]

            def link(ins):
                n_chain[0] += 1
                ins.then_inc(chain, 1)
                v.wait_ge(chain, n_chain[0])

            def rstd(dst, n):
                v.wait_ge(rms_ready, 2 * n)
                link(v.reciprocal(dst, dst))

            un.wait_full(v, "rows")
            ins = v.tensor_copy(cols[:, :], ps[7][:, 0:R_N])
            ins.then_inc(bank_free[7], 1)
            un.wait_read(v, "rows")
            rstd(small[:, 18:20], 1)
            for tt in range(TT):
                ins = v.tensor_scalar(xn3[:, tt, :], x3[:, tt, :], small[:, 18 + tt:19 + tt], None, ALU.mult)
            link(ins)
            v.sem_inc(xn_ready, 1)
            v.wait_ge(ec_ready, 1)
            link(v.tensor_scalar(small[:, 8:16], small[:, 8:16], 1.0, None, ALU.add))
            link(v.reciprocal(small[:, 8:16], small[:, 8:16]))
            link(v.tensor_tensor(small[:, 0:8], small[:, 8:16], cols[:, R_C:R_C + KT], ALU.mult))
            v.tensor_copy(silu_rep[:, :].rearrange("p (k r) -> p k r", k=KT),
                          small[:, 0:8].rearrange("p (k r) -> p k r", r=1).broadcast_to([P, KT, 32])
                          ).then_inc(silu_ready, 1)
            v.wait_ge(ld_pos, 16 * TT)
            v.wait_ge(ld_cst, 16)
            n = TT * HALF
            link(v.tensor_copy(small[:, 20:22], pos_i[:, :]))
            ang, turns, arg = rope[:, 0:n], rope[:, n:2 * n], rope[:, 2 * n:4 * n]
            for tt in range(TT):
                ins = v.tensor_scalar(ang[:, tt * HALF:(tt + 1) * HALF], cst[:, C_FREQ:C_FREQ + HALF],
                                      small[:, 20 + tt:21 + tt], None, ALU.mult)
            link(ins)
            c1, c2, c3 = two_pi_parts()
            magic = 1.5 * 2.0 ** 23
            for q, (quarter, add) in enumerate(((0.0, 0.0), (0.25, float(np.pi / 2)))):
                to = arg[:, q * n:(q + 1) * n]
                link(v.tensor_scalar(turns, ang, float(1 / (2 * np.pi)), quarter, ALU.mult, ALU.add))
                link(v.tensor_scalar(turns, turns, magic, None, ALU.add))
                link(v.tensor_scalar(turns, turns, magic, None, ALU.subtract))
                link(v.scalar_tensor_tensor(out=to, in0=turns, scalar=-c1, in1=ang, op0=ALU.mult, op1=ALU.add))
                link(v.scalar_tensor_tensor(out=to, in0=turns, scalar=-c2, in1=to, op0=ALU.mult, op1=ALU.add))
                link(v.scalar_tensor_tensor(out=to, in0=turns, scalar=-c3, in1=to, op0=ALU.mult, op1=ALU.add))
                link(v.tensor_scalar(to, to, add, 3.1415925, ALU.add, ALU.min))
                link(v.tensor_scalar(to, to, -3.1415925, None, ALU.max))
            v.sem_inc(ang_ready, 1)

            def mod_part(unit, m0, m1):
                un.wait_full(v, unit)
                ins = v.tensor_tensor(mod[:, m0:m1], ps[un.bank(unit)][:, 0:m1 - m0], cols[:, m0:m1], ALU.add)
                ins.then_inc(bank_free[un.bank(unit)], 1)
                un.wait_read(v, unit)

            def scale_cols(dst, m0, gain):
                link(v.scalar_tensor_tensor(out=small[:, dst:dst + KT], in0=mod[:, m0:m0 + KT], scalar=1.0,
                                            in1=cols[:, R_G + gain * KT:R_G + (gain + 1) * KT],
                                            op0=ALU.add, op1=ALU.mult))

            mod_part("ada_a", 0, 16)
            scale_cols(64, 8, 0)
            for q in range(4):
                un.wait_full(v, f"hT{q}")
                for i in range(2):
                    k = 2 * q + i
                    ins = v.tensor_scalar(hT3[:, k, :], ps[q][:, i * T:(i + 1) * T], small[:, 64 + k:65 + k],
                                          mod[:, k:k + 1], ALU.mult, ALU.add)
                ins.then_inc(bank_free[q], 1)

            def blocks(ap):
                return ap[:, 0:P], ap[:, T:TRI]

            def sb_first(h):
                un.wait_full(v, f"z{h}")
                z = ps[un.bank(f"z{h}")][:, 0:TRI]
                if h >= 2:
                    v.wait_ge(sb_w, h - 1)
                zs = sbw[:, 8 + h % 2, :]
                v.tensor_scalar(zs, z, SCALE, None, ALU.mult).then_inc(bank_free[un.bank(f"z{h}")], 1)
                un.wait_read(v, f"z{h}")
                v.scalar_tensor_tensor(out=sbw[:, h % 2, :], in0=zs, scalar=-1.0, in1=zs, op0=ALU.mult,
                                       op1=ALU.min).then_inc(sb_na, 1)
                link(v.tensor_scalar(sbw[:, 6 + h % 2, :], zs, 0.0, None, ALU.max))

            def sb_second(h):
                v.wait_ge(sb_ln, h + 1)
                s = sbw[:, 6 + h % 2, :]
                link(v.tensor_tensor(s, s, sbw[:, h % 2, :], ALU.add))
                for d_ in blocks(s):
                    ins = v.tensor_tensor(d_, d_, cst[:, C_ST:C_ST + P], ALU.mult)
                link(ins)
                v.sem_inc(sb_sp, 1)

            def sb_third(h):
                un.wait_full(v, f"c{h}")
                L = sbw[:, 8 + h % 2, :]
                ins = v.tensor_tensor(L, L, ps[un.bank(f"c{h}")][:, 0:TRI], ALU.subtract)
                ins.then_inc(bank_free[un.bank(f"c{h}")], 1)
                un.wait_read(v, f"c{h}")
                for d_ in blocks(L):
                    ins = v.tensor_tensor(d_, d_, cst[:, C_NG:C_NG + P], ALU.add)
                link(ins)
                v.sem_inc(sb_l, 1)

            for h in range(SB_H + 1):
                if h < SB_H:
                    sb_first(h)
                if h >= 1:
                    sb_third(h - 1)
                if h < SB_H:
                    sb_second(h)

            v.wait_ge(rope_ready, 1)
            un.wait_read(v, "qk20")
            un.wait_read(v, "qk21")
            nh = 2 * NG * SLOTS
            for tt in range(TT):
                q4 = qk[:, tt, :].rearrange("p (h d) -> p h d", h=nh)
                t1, t2 = q4[:, :, 0:HALF], q4[:, :, HALF:2 * HALF]
                sin = rope[:, 4 * n + tt * HALF:4 * n + (tt + 1) * HALF]
                cos = rope[:, 5 * n + tt * HALF:5 * n + (tt + 1) * HALF]
                sin = sin.rearrange("p (o d) -> p o d", o=1).broadcast_to([P, nh, HALF])
                cos = cos.rearrange("p (o d) -> p o d", o=1).broadcast_to([P, nh, HALF])
                w = [xn[:, k * nh * HALF:(k + 1) * nh * HALF].rearrange("p (h d) -> p h d", h=nh) for k in range(4)]
                v.tensor_tensor(w[0], t1, cos, ALU.mult)
                v.tensor_tensor(w[1], t2, sin, ALU.mult)
                v.tensor_tensor(w[2], t2, cos, ALU.mult)
                link(v.tensor_tensor(w[3], t1, sin, ALU.mult))
                v.tensor_tensor(t1, w[0], w[1], ALU.subtract)
                link(v.tensor_tensor(t2, w[2], w[3], ALU.add))
            v.sem_inc(rot_done, 1)

            for i in range(SLOTS):
                if i > 0:
                    for g in range(NG):
                        un.wait_read(v, f"pT{i - 1}{g}")
                c = C_MASK
                un.wait_full(v, f"s{i}0")
                ins = v.tensor_tensor_reduce(out=prob[:, 0:TRI], in0=ps[2][:, 0:TRI], in1=cst[:, c:c + TRI],
                                             scale=1.0, scalar=-3e38, op0=ALU.add, op1=ALU.max,
                                             accum_out=small[:, 24:25])
                ins.then_inc(bank_free[2], 1)
                un.wait_full(v, f"s{i}1")
                ins = v.tensor_tensor_reduce(out=prob[:, TRI:TRI + 2 * T], in0=ps[3][:, :],
                                             in1=cst[:, c + TRI:c + TRI + 2 * T], scale=1.0, scalar=-3e38,
                                             op0=ALU.add, op1=ALU.max, accum_out=small[:, 30:31])
                ins.then_inc(bank_free[3], 1)
                un.wait_read(v, f"s{i}1")
                un.wait_full(v, f"s{i}2")
                ins = v.tensor_tensor_reduce(out=prob[:, TRI + 2 * T:TRI + 3 * T], in0=ps[4][:, 0:T],
                                             in1=cst[:, c + TRI + 2 * T:c + TRI + 3 * T], scale=1.0,
                                             scalar=small[:, 30:31], op0=ALU.add, op1=ALU.max,
                                             accum_out=small[:, 25:26])
                ins.then_inc(bank_free[4], 1)
                un.wait_read(v, f"s{i}0")
                un.wait_read(v, f"s{i}2")
                link(v.tensor_scalar(small[:, 26:28], small[:, 24:26], -SCALE, None, ALU.mult))
                v.sem_inc(dl_max, 1)
                v.wait_ge(dl_exp, 2 * (i + 1))
                link(v.reciprocal(small[:, 22:24], small[:, 28:30]))
                v.tensor_scalar(prob[:, 0:TRI], prob[:, 0:TRI], small[:, 22:23], None, ALU.mult)
                link(v.tensor_scalar(prob[:, TRI:], prob[:, TRI:], small[:, 23:24], None, ALU.mult))
                v.sem_inc(dl_p, 1)

            v.wait_ge(sig_ready, 4)
            for m in range(KT):
                un.wait_full(v, f"br{m}")
                b = ps[un.bank(f"br{m}")]
                v.tensor_tensor(brw[:, 2 * (m % 2), :], b[:, 0:T], gates[:, m, :], ALU.mult)
                ins = v.tensor_tensor(brw[:, 2 * (m % 2) + 1, :], b[:, T:2 * T], gates[:, KT + m, :], ALU.mult)
                ins.then_inc(bank_free[un.bank(f"br{m}")], 1)
                un.wait_read(v, f"br{m}")
                ins = v.tensor_tensor(merged[:, m, :], brw[:, 2 * (m % 2), :], brw[:, 2 * (m % 2) + 1, :], ALU.add)
            link(ins)
            v.sem_inc(merged_ready, 1)

            def diagonals(dst, m0, gain, wait=None):
                link(v.tensor_tensor(small[:, 80:88], mod[:, m0:m0 + KT],
                                     cols[:, R_G + gain * KT:R_G + (gain + 1) * KT], ALU.mult))
                for k in range(KT):
                    ins = v.tensor_scalar(dst[:, k * P:(k + 1) * P], ident, small[:, 80 + k:81 + k], None, ALU.mult)
                link(ins)
                v.sem_inc(diag_ready, 1)

            mod_part("ada_b", 16, 40)
            un.wait_full(v, "g7")
            diagonals(diag1, 16, 1)
            scale_cols(72, 32, 2)

            rstd(small[:, 38:40], 2)
            un.wait_read(v, "grow1a")
            un.wait_read(v, "grow1b")
            for tt in range(TT):
                for dh in range(2):
                    n_ = f"y{tt}{dh}"
                    w = xn3[:, tt, dh * 512:(dh + 1) * 512]
                    ins = v.scalar_tensor_tensor(out=w, in0=ps[un.bank(n_)][:, :], scalar=small[:, 38 + tt:39 + tt],
                                                 in1=grow[:, dh * 512:(dh + 1) * 512], op0=ALU.mult, op1=ALU.mult)
                    ins.then_inc(bank_free[un.bank(n_)], 1)
                    un.wait_read(v, n_)
                    r = x3[:, tt, dh * 512:(dh + 1) * 512]
                    link(v.tensor_tensor(r, r, w, ALU.add))
                    v.sem_inc(x1_ready, 1)
            rstd(small[:, 42:44], 3)
            for tt in range(TT):
                ins = v.tensor_scalar(xn3[:, tt, :], x3[:, tt, :], small[:, 42 + tt:43 + tt], None, ALU.mult)
            link(ins)
            v.sem_inc(x1n_ready, 1)
            for q in range(4):
                un.wait_full(v, f"h2T{q}")
                for i in range(2):
                    k = 2 * q + i
                    ins = v.tensor_scalar(hT3[:, k, :], ps[4 + q][:, i * T:(i + 1) * T], small[:, 72 + k:73 + k],
                                          mod[:, 24 + k:25 + k], ALU.mult, ALU.add)
                ins.then_inc(bank_free[4 + q], 1)

            un.wait_full(v, "logit")
            logit, expl, sel, rest = lg[:, 0, :], lg[:, 1, :], lg[:, 2, :], lg[:, 3, :]
            ins = v.tensor_copy(logit, ps[0][:, 0:TT * E])
            ins.then_inc(bank_free[0], 1)
            un.wait_read(v, "logit")
            for tt in range(TT):
                ins = v.max(top[:, tt, :], logit[:, tt * E:(tt + 1) * E])
            link(ins)
            link(v.tensor_scalar(small[:, 50:52], top[:, :, 0:1].rearrange("p a b -> p (a b)"), -1.0, None, ALU.mult))
            v.sem_inc(lmax_ready, 1)
            link(v.memset(top[:, :, TOPK:8], 3e38))
            for tt in range(TT):
                ins = v.match_replace(out=rest[:, tt * E:(tt + 1) * E], in_to_replace=top[:, tt, :],
                                      in_values=logit[:, tt * E:(tt + 1) * E], imm_value=-3e38)
            link(ins)
            link(v.tensor_tensor(sel, rest, logit, ALU.not_equal))
            v.sem_inc(sel_ready, 1)
            v.wait_ge(lexp_ready, 2)
            link(v.tensor_tensor(expl, expl, sel, ALU.mult))
            link(v.tensor_reduce(small[:, 52:54], expl.rearrange("p (t e) -> p t e", t=TT), AX_X, ALU.add))
            link(v.reciprocal(small[:, 54:56], small[:, 52:54]))
            link(v.memset(arena[:, 14336:14336 + 4 * (E + 1)], 0.0))
            link(v.memset(posm2, 0.0))
            for tt in range(TT):
                ins = v.tensor_scalar(gate[:, tt, 0:E], expl[:, tt * E:(tt + 1) * E], small[:, 54 + tt:55 + tt], None,
                                      ALU.mult)
            link(ins)
            v.sem_inc(gate_ready, 1)
            un.wait_full(v, "rank")
            for tt in range(TT):
                ins = v.tensor_tensor(lg[:, 4, tt * E:(tt + 1) * E], ps[3][:, tt * E:(tt + 1) * E],
                                      sel[:, tt * E:(tt + 1) * E], ALU.mult)
            ins = v.tensor_copy(lg[:, 5, 0:E], ps[3][:, 2 * E:3 * E])
            ins.then_inc(bank_free[3], 1)
            un.wait_read(v, "rank")
            for tt in range(TT):
                v.tensor_scalar(posm[:, tt, 0:E], lg[:, 4, tt * E:(tt + 1) * E], -1.0, None, ALU.add)
                v.tensor_scalar(posm2[:, tt, 0:E], lg[:, 4, tt * E:(tt + 1) * E], -1.0 - P, None, ALU.add)
            link(v.memset(lg[:, 6, 0:E + 1], 0.0))
            for least in CLASS_FROM:
                link(v.scalar_tensor_tensor(out=lg[:, 6, 0:E], in0=lg[:, 5, 0:E], scalar=least - 0.5,
                                            in1=lg[:, 6, 0:E], op0=ALU.is_ge, op1=ALU.add))
            v.tensor_copy(cls_i[:, :], lg[:, 6, 0:E + 1]).then_inc(cls_ready, 1)

            mod_part("ada_c", 40, 48)
            diagonals(diag2, 40, 3)

            def one_hot(e, cls):
                for tt in range(TT):
                    ins = v.tensor_scalar(S[:, tt, :], iota, posm[:, tt, ds(e, 1)], None, ALU.is_equal)

                def gated(k):
                    for p, (G, t0) in enumerate(PASSES[k]):
                        slots = cst[:, {1: C_IOTA, 2: C_I64, 4: C_I32}[G]:][:, 0:P]
                        for tt in range(TT):
                            ins = v.tensor_scalar(Sg[:, p, tt * P:(tt + 1) * P], slots,
                                                  (posm2 if t0 else posm)[:, tt, ds(e, 1)],
                                                  gate[:, tt, ds(e, 1)], ALU.is_equal, ALU.mult)
                    ins.then_inc(s_ready, 1)

                by_class(v, cls, gated)

            v.wait_ge(cls_ready, 1)
            one_hot(0, v.value_load(cls_i[0:1, 0:1]))
            v.wait_ge(ld_small, 64)
            with v.Fori(0, E) as e:
                cls = v.value_load(cls_i[0:1, ds(e, 1)])
                v.wait_ge(xg_full, 4 * e + 4)
                v.tensor_copy(pick, ident[:, ds(e * 4, 4)].rearrange("p (c m) -> p c m", m=1).broadcast_to(
                    [P, 4, P])).then_inc(pick_ready, 1)
                one_hot(e + 1, v.value_load(cls_i[0:1, ds(e + 1, 1)]))

                def body(k):
                    passes = PASSES[k]
                    n_p = len(passes)

                    def clamped(j):
                        c, p = j // n_p, j % n_p
                        last = p == n_p - 1
                        W = CW // passes[p][0]
                        if j >= 2:
                            v.wait_ge(act_ready, 8 * e + j - 1)
                        v.wait_ge(up_full if last else part_full, e * (4 if last else 8) + c + 1)
                        b = ps[(4 if last else 6) + c % 2][:, 0:W].rearrange("p (n two) -> p two n", two=2)
                        v.tensor_scalar(xw[:, j % 2, 0:W // 2], b[:, 0, :], LIMIT, None, ALU.min).then_inc(g_ready, 1)
                        v.tensor_scalar(xw[:, 2 + j % 2, 0:W // 2], b[:, 1, :], LIMIT, -LIMIT, ALU.min,
                                        ALU.max).then_inc(up_read if last else part_read, 1)

                    def finish(j):
                        c, p = j // n_p, j % n_p
                        h = CW // 2 // passes[p][0]
                        v.wait_ge(sg_ready, 8 * e + j + 1)
                        v.tensor_tensor(xw[:, 6 + j % 2, 0:h], xw[:, j % 2, 0:h], xw[:, 4 + j % 2, 0:h],
                                        ALU.mult).then_inc(m_ready, 1)
                        v.wait_ge(m_ready, 8 * e + j + 1)
                        to = hid[:, p, c // 2 * 2 * h:(c // 2 + 1) * 2 * h].rearrange("p (q c f) -> p q c f", c=2, f=64)
                        v.scalar_tensor_tensor(out=to[:, :, c % 2, :],
                                               in0=xw[:, 2 + j % 2, 0:h].rearrange("p (q f) -> p q f", f=64), scalar=1.0,
                                               in1=xw[:, 6 + j % 2, 0:h].rearrange("p (q f) -> p q f", f=64),
                                               op0=ALU.add, op1=ALU.mult).then_inc(act_ready, 1)

                    for j in range(4 * n_p + 1):
                        if j < 4 * n_p:
                            clamped(j)
                        if j >= 1:
                            finish(j - 1)
                    if n_p == 1:
                        v.wait_ge(act_ready, 8 * e + 4)
                        for s_ in (g_ready, m_ready, act_ready):
                            v.sem_inc(s_, 4)
                    for p, (G, _) in enumerate(passes):
                        last = p == n_p - 1
                        M, Q = P // G, SUB // G
                        for u in range(2):
                            v.wait_ge(at_full if last else part_full, e * (2 if last else 8) + u + (1 if last else 5))
                            v.tensor_copy(
                                hidT[:, p, u * 4 * M:(u + 1) * 4 * M].rearrange("p (g q t) -> p q g t", g=G, q=Q),
                                ps[(6 if last else 4) + u][:, 0:Q * P].rearrange("p (q g t) -> p q g t", q=Q, g=G)
                            ).then_inc(at_read if last else part_read, 1)
                    for d in range(2):
                        for p, (G, _) in enumerate(passes):
                            last = p == n_p - 1
                            W = CW // G
                            v.wait_ge(dn_full if last else part_full, e * (2 if last else 8) + d + (1 if last else 7))
                            v.tensor_copy(Y[:, p, d * W:(d + 1) * W], ps[(4 if last else 6) + d][:, 0:W]).then_inc(
                                dn_read if last else part_read, 1)
                    if n_p == 1:
                        v.sem_inc(part_read, 8)

                by_class(v, cls, body)

            rstd(small[:, 46:48], 4)
            un.wait_read(v, "grow2a")
            un.wait_read(v, "grow2b")
            for tt in range(TT):
                for dh in range(2):
                    w = xn3[:, tt, dh * 512:(dh + 1) * 512]
                    link(v.scalar_tensor_tensor(out=w, in0=ps[2 * tt + dh][:, :], scalar=small[:, 46 + tt:47 + tt],
                                                in1=grow[:, dh * 512:(dh + 1) * 512], op0=ALU.mult, op1=ALU.mult))
                    v.tensor_tensor(w, w, x3[:, tt, dh * 512:(dh + 1) * 512], ALU.add).then_inc(out_ready, 1)


_OUT = (1, T, D)


def kernel(**inputs):
    import concourse.bacc as _bacc
    from concourse.bass_utils import run_bass_kernel_spmd as _run

    nc = _bacc.Bacc("TRN2", target_bir_lowering=False, num_devices=1)
    arrays, a = {}, {}
    for name, value in list(inputs.items()) + [("cst", constants())]:
        v = np.ascontiguousarray(value)
        arrays[f"in_{name}"] = v
        a[name] = nc.dram_tensor(f"in_{name}", v.shape, mybir.dt.from_np(v.dtype), kind="ExternalInput").ap()
    out = nc.dram_tensor("out_0", _OUT, F32, kind="ExternalOutput").ap()
    layer_kernel(nc, a, out)
    r = _run(nc, [arrays], core_ids=[0])
    return r.results[0]["out_0"]
```

```python
from contextlib import ExitStack

import numpy as np

import concourse.bass as bass
from concourse import mybir

ALU = mybir.AluOpType
ACT = mybir.ActivationFunctionType
F32 = mybir.dt.float32
I32 = mybir.dt.int32
AX_X = mybir.AxisListType.X
ds = bass.ds

P = 128
D = 1024
KT = D // P
T = 256
TT = T // P
HD = 64
NG, SLOTS = 3, 4
DIL_W = NG * SLOTS * HD
SB_H = 8
SB_W = SB_H * HD
QA, KA, VA = 0, DIL_W, 2 * DIL_W
QB = 3 * DIL_W
KB, VB = QB + SB_W, QB + 2 * SB_W
GA = QB + 3 * SB_W
GB = GA + D
HALF = 8
E = 32
TOPK = 4
F = 1024
FT = F // P
LIMIT, ALPHA = 7.0, 1.702
EPS = 1e-6
SCALE = HD ** -0.5
NEG = -1e30
CW = 512
RING = 6
PASSES = [[(4, 0)], [(2, 0)], [(1, 0)], [(1, 0), (4, 128)], [(1, 0), (2, 128)], [(1, 0), (1, 128)]]
CLASS_FROM = [33, 65, 129, 161, 193]
SUB = 4
TRI = 384

C_ID = 0
C_EPS = C_ID + P
C_SEL = C_EPS + 1
C_FREQ = C_SEL + 1
C_FIRST = C_FREQ + HALF
C_ONE, C_LE, C_GE, C_ST, C_NG, C_IOTA = (C_FIRST + i * P for i in range(6))
C_MASK = C_IOTA + T
C_I32 = C_MASK + NG * P + NG * T
C_I64 = C_I32 + P
C_STACK = C_I64 + P
C_W = C_STACK + E

R_ADAB, R_G = 0, 48
R_C = R_G + 4 * KT
R_N = R_C + KT


def constants():
    i = np.arange(P)
    c = np.zeros((P, C_W), np.float32)
    c[:, C_ID:C_ID + P] = np.eye(P)
    c[:, C_ONE:C_ONE + P] = 1.0
    c[:, C_LE:C_LE + P] = i[:, None] <= i[None, :]
    c[:, C_GE:C_GE + P] = i[:, None] >= i[None, :]
    c[:, C_ST:C_ST + P] = i[:, None] < i[None, :]
    c[:, C_NG:C_NG + P] = np.where(i[:, None] < i[None, :], 0.0, NEG)
    c[:, C_IOTA:C_IOTA + T] = np.arange(T)[None, :]
    at = C_MASK
    for tt in range(TT):
        for window, dil in ((128, 1), (512, 4), (2048, 16)):
            dist = (tt * P + i)[:, None] - np.arange((tt + 1) * P)[None, :]
            ok = (dist >= 0) & (dist <= window) & (dist % dil == 0)
            c[:, at:at + dist.shape[1]] = np.where(ok, 0.0, NEG)
            at += dist.shape[1]
    freq = (500000.0 ** (-(np.arange(HALF, dtype=np.float32) * 2.0 / (2 * HALF)))).astype(np.float32)
    c[:, C_FREQ:C_FREQ + HALF] = freq[None, :]
    c[:, C_EPS] = EPS
    c[:, C_SEL] = i % 32 == 0
    c[:, C_I32:C_I32 + P] = (i % 32)[None, :]
    c[:, C_I64:C_I64 + P] = (i % 64)[None, :]
    c[:, C_STACK:C_STACK + E] = i[:, None] % E == np.arange(E)[None, :]
    return c


def two_pi_parts():
    a = np.float32(6.28125)
    b = np.float32(np.round((2 * np.pi - float(a)) * 2.0 ** 20) / 2.0 ** 20)
    return float(a), float(b), float(np.float32(2 * np.pi - float(a) - float(b)))


class Units:

    def __init__(self, full, free):
        self.full, self.free, self.count, self.place = full, free, [0] * 8, {}

    def add(self, name, bank):
        self.place[name] = (bank, self.count[bank])
        self.count[bank] += 1

    def bank(self, name):
        return self.place[name][0]

    def wait_free(self, eng, name):
        b, n = self.place[name]
        if not isinstance(n, int) or n > 0:
            eng.wait_ge(self.free[b], n)

    def wait_full(self, eng, name):
        b, n = self.place[name]
        eng.wait_ge(self.full[b], n + 1)

    def wait_read(self, eng, name):
        b, n = self.place[name]
        eng.wait_ge(self.free[b], n + 1)


def layer_kernel(nc, a, out):
    ctx = ExitStack()
    with ctx:
        def sb(name, width, dt=F32, rows=P):
            return ctx.enter_context(nc.sbuf_tensor(name, [rows, width], dt))

        def sem(name):
            return ctx.enter_context(nc.semaphore(name))

        ring = sb("ring", RING * KT * CW)
        cst = sb("cst", C_W)
        x_res = sb("x_res", TT * D)
        hT = sb("hT", KT * T)
        area = sb("area", TT * D + 14848)
        yaT = sb("yaT", 2 * T)
        ybT = sb("ybT", 4 * T)
        grow = sb("grow", D)
        b_down_sb = sb("b_down_sb", D, rows=E)
        bup = sb("bup", CW)
        silu_rep = sb("silu_rep", KT * 32)
        w_router_sb = sb("w_router_sb", KT * E)
        cols = sb("cols", R_N)
        mod = sb("mod", 48)
        small = sb("small", 96)
        rope = sb("rope", 6 * TT * HALF)
        pos_i = sb("pos_i", TT, I32)
        small_rows = sb("small_rows", P, rows=R_N)
        b_router_sb = sb("b_router_sb", E, rows=1)
        cls_i = sb("cls_i", E + 1, I32)

        xn = area[:, 0:TT * D]
        arena = area[:, TT * D:]
        spare = area[:, 0:KT * CW]

        ident = cst[:, C_ID:C_ID + P]
        ones = cst[:, C_ONE:C_ONE + P]
        tri_le = cst[:, C_LE:C_LE + P]
        tri_ge = cst[:, C_GE:C_GE + P]
        iota = cst[:, C_IOTA:C_IOTA + T]

        def slot(g):
            s = g % RING
            return ring[:, s * KT * CW:(s + 1) * KT * CW]

        def chunk(g, width=CW, kt=KT):
            return slot(g)[:, 0:kt * width].rearrange("p (k n) -> p k n", k=kt)

        x3 = x_res[:, :].rearrange("p (t d) -> p t d", t=TT)
        xn3 = xn[:, :].rearrange("p (t d) -> p t d", t=TT)
        hT3 = hT[:, :].rearrange("p (k t) -> p k t", k=KT)

        def region(at, shape):
            n = int(np.prod(shape))
            v = arena[:, at:at + n]
            if len(shape) == 2:
                v = v.rearrange("p (x y) -> p x y", x=shape[0])
            elif len(shape) == 3:
                v = v.rearrange("p (x y z) -> p x y z", x=shape[0], y=shape[1])
            return v

        qk = region(0, (TT, 2 * DIL_W))
        vtok = region(3072, (TT, DIL_W + SB_W))
        qkT = region(5632, (12, T))
        sbT = region(8704, (8, T))
        gates = region(10752, (16, T))
        sbw = region(10752, (10, TRI))
        prob = xn[:, 0:NG * P + NG * T]
        probT = region(8704, (NG, TRI))
        merged = region(0, (KT, T))
        brw = region(2048, (4, T))
        h2 = region(8192, (TT, D))
        XT = region(2048, (KT, T))
        hid = region(4096, (2, 4 * CW // 2))
        hidT = region(6144, (2, D))
        Y = hid
        S = region(10240, (TT, T))
        Sg = region(10752, (2, TT * P))
        GT = region(11264, (2, T))
        GTg = {4: hT[:, 0:4 * T].rearrange("p (g t) -> p g t", g=4),
               2: hT[:, 4 * T:6 * T].rearrange("p (g t) -> p g t", g=2)}
        xw = region(11776, (8, T))
        pick = yaT[:, :].rearrange("p (c m) -> p c m", c=4)
        lg = region(13824, (8, TT * E))
        posm = region(14336, (TT, E + 1))
        gate = region(14336 + 2 * (E + 1), (TT, E + 1))
        top = region(14336 + 4 * (E + 1), (TT, 8))
        posm2 = region(14336 + 4 * (E + 1) + 16, (TT, E + 1))
        gT = region(14592, (T,))
        lpT = region(10240, (T,))
        row2 = region(4096, (D,))
        def junk(tt):
            return arena[:, 8192 + tt * D:8192 + (tt + 1) * D]

        diag1 = hT[:, 0:D]
        diag2 = region(2048, (D,))

        psum = ctx.enter_context(nc.psum_tensor("psum", [P, 8 * 512], F32))
        ps = [psum[:, b * 512:(b + 1) * 512] for b in range(8)]

        bank_full = [sem(f"bank_full{b}") for b in range(8)]
        bank_free = [sem(f"bank_free{b}") for b in range(8)]
        slot_full = [sem(f"slot_full{s}") for s in range(RING)]
        spare_full = sem("spare_full")
        ld_cst, ld_rows, ld_x, ld_pos, ld_small = map(sem, (
            "ld_cst", "ld_rows", "ld_x", "ld_pos", "ld_small"))
        xn_ready, ec_ready, silu_ready, ang_ready, rope_ready = map(sem, (
            "xn_ready", "ec_ready", "silu_ready", "ang_ready", "rope_ready"))
        rot_done, pick_ready, sb_na, sb_e, sb_ln = map(sem, (
            "rot_done", "pick_ready", "sb_na", "sb_e", "sb_ln"))
        sb_sp, sb_l, sb_w, dl_max, dl_exp = map(sem, (
            "sb_sp", "sb_l", "sb_w", "dl_max", "dl_exp"))
        dl_p, sig_ready, merged_ready, diag_ready, x1_ready = map(sem, (
            "dl_p", "sig_ready", "merged_ready", "diag_ready", "x1_ready"))
        x1n_ready, sel_ready, lexp_ready, lmax_ready, gate_ready = map(sem, (
            "x1n_ready", "sel_ready", "lexp_ready", "lmax_ready", "gate_ready"))
        cls_ready, s_ready, g_ready, sg_ready = map(sem, (
            "cls_ready", "s_ready", "g_ready", "sg_ready"))
        m_ready, act_ready, acc_done, out_ready, stored = map(sem, (
            "m_ready", "act_ready", "acc_done", "out_ready", "stored"))
        rms_ready, sq_ready = map(sem, (
            "rms_ready", "sq_ready"))
        up_full, up_read, dn_full, dn_read, at_full, at_read, gt_full, gt_read, xg_full, xg_read = map(sem, (
            "up_full", "up_read", "dn_full", "dn_read", "at_full", "at_read", "gt_full", "gt_read",
            "xg_full", "xg_read"))
        part_full, part_read, gt_zero = sem("part_full"), sem("part_read"), sem("gt_zero")
        xe_full, xe_read = sem("xe_full"), sem("xe_read")
        chain = sem("chain")

        front = []
        where = {}

        def add_chunk(name, src, kt=KT, width=CW):
            where[name] = len(front)
            front.append((src.rearrange("(k p) n -> p k n", p=P), kt, width))

        ada = a["ada_w"][0]
        w_in = a["w_in"][0]
        for m in range(4):
            add_chunk(f"ada{m}", ada[:, m * CW:(m + 1) * CW])
        for name, c0 in (("sbq", QB), ("sbk", KB), ("sbv", VB), ("qk0", 0), ("qk1", CW), ("qk2", 2 * CW), ("va0", VA)):
            add_chunk(name, w_in[:, c0:c0 + CW])
        add_chunk("va1", w_in[:, VA + CW:VA + DIL_W], KT, DIL_W - CW)
        for m in range(4):
            add_chunk(f"gate{m}", w_in[:, GA + m * CW:GA + (m + 1) * CW])
        add_chunk("wa", a["w_branch_a"][0], 2, D)
        add_chunk("wb", a["w_branch_b"][0], 4, D)
        add_chunk("wo0", a["w_out"][0][:, 0:CW])
        for m in range(4, 10):
            add_chunk(f"ada{m}", ada[:, m * CW:(m + 1) * CW])
        add_chunk("wo1", a["w_out"][0][:, CW:D])
        for m in range(10, 12):
            add_chunk(f"ada{m}", ada[:, m * CW:(m + 1) * CW])
        NF = len(front)

        un = Units(bank_full, bank_free)
        un.add("rows", 7)
        for q in range(4):
            un.add(f"hT{q}", q)
        for m in range(4):
            un.add(f"ar{m}", 4 + m % 2)
        un.add("ada_a", 7)
        rot = []
        for n in ("sbq0", "sbq1", "sbk0", "sbk1", "sbv0", "sbv1", "qk00", "qk01", "qk10", "qk11", "qk20", "qk21",
                  "va00", "va01", "va1", "qkT0", "qkT1", "qkT2", "qkT3", "qkT4", "qkT5"):
            un.add(n, len(rot) % 2)
            rot.append(n)
        for h in range(SB_H):
            un.add(f"z{h}", 2 + h % 2)
            un.add(f"c{h}", 4 + h % 2)
            if h % 2:
                un.add(f"sbo{h // 2}", 6 + h // 2 % 2)
        for i in range(SLOTS):
            for b in range(3):
                un.add(f"s{i}{b}", 2 + b)
            un.add(f"g{2 * i}", 0)
            for g in range(NG):
                un.add(f"pT{i}{g}", 5 + g)
            un.add(f"g{2 * i + 1}", 0)
            if i % 2:
                un.add(f"dlo{i // 2}", 1)
        for m in range(KT):
            un.add(f"br{m}", 2 + m % 4)
        for m in range(4, 10):
            un.add(f"ar{m}", 4 + m % 2)
        un.add("ada_b", 6)
        un.add("grow1a", 6)
        un.add("grow1b", 7)
        for dh in range(2):
            for tt in range(TT):
                un.add(f"y{tt}{dh}", 2 * tt + dh)
        for q in range(4):
            un.add(f"h2T{q}", 4 + q)
        un.add("ar10", 0)
        un.add("ar11", 1)
        un.add("ada_c", 0)
        un.add("lpart", 2)
        un.add("logit", 3)
        for n, b in (("hb00", 4), ("hb01", 5), ("hb10", 6), ("hb11", 7)):
            un.add(n, b)
        un.add("gateT", 2)
        un.add("rank", 1)
        un.add("grow2a", 4)
        un.add("grow2b", 5)
        for b in range(4):
            un.add(f"acc{b}", b)
        released = {}
        for name, unit in [(f"ada{m}", f"ar{m}") for m in range(12)] + [("sbq", "sbq1"), ("sbk", "sbk1"),
                           ("sbv", "sbv1"), ("qk0", "qk01"), ("qk1", "qk11"), ("qk2", "qk21"), ("va0", "va01"),
                           ("va1", "va1"), ("gate0", "g1"), ("gate1", "g3"), ("gate2", "g5"), ("gate3", "g7"),
                           ("wa", "br7"), ("wb", "br7"), ("wo0", "y10"), ("wo1", "y11")]:
            b, n = un.place[unit]
            released[name] = (bank_full[b], n + 1)
        names = sorted(where, key=where.get)

        front_fills = [16 * len(range(b, NF, RING)) for b in range(RING)]

        def expert_slot(e, c):
            pair, odd = e
            b = (NF + c) % RING
            if c == 0:
                if odd:
                    return spare, spare_full, (pair + 1) * 16
                return slot(NF), slot_full[b], front_fills[b] + (pair + 1) * 16
            return slot(NF + c), slot_full[b], front_fills[b] + (pair * 2 + odd + 1) * (16 if c < 4 else 64)

        def by_class(eng, cls, body):
            def split(a, b):
                if a == b:
                    return body(a)
                m = (a + b) // 2
                with eng.If(cls <= m):
                    split(a, m)
                with eng.Else():
                    split(m + 1, b)
            split(0, len(PASSES) - 1)

        XG_BANK = ((4, 6, 6, 7), (6, 7, 4, 5))
        XE_BANK = (7, 4, 5, 7)

        def at_bank(n_p, last, u):
            if n_p == 1:
                return (7, 5)[u]
            return (6 if last else 4) + u

        block = ctx.enter_context(nc.Block())

        @block.sync
        def _(sp):
            rows = small_rows
            for r, name, count in ((R_C, "c", KT), (R_ADAB, "ada_b", 48), (R_G, "norm_mix_pre", KT),
                                   (R_G + KT, "norm_mix_post", KT), (R_G + 2 * KT, "norm_ffn_pre", KT),
                                   (R_G + 3 * KT, "norm_ffn_post", KT)):
                sp.dma_start(rows[r:r + count, :], a[name][0].rearrange("(k p) -> k p", p=P)).then_inc(ld_rows, 16)
            sp.dma_start(cst[:, 0:C_FIRST], a["cst"][:, 0:C_FIRST]).then_inc(ld_cst, 16)
            sp.dma_start(x3, a["x"][0].rearrange("(t p) d -> p t d", p=P)).then_inc(ld_x, 16)
            for g, (src, kt, width) in enumerate(front):
                if g >= RING:
                    sp.wait_ge(*released[names[g - RING]])
                sp.dma_start(chunk(g, width, kt), src).then_inc(slot_full[g % RING], 16)

            def expert_chunks(pair, odd, first=False, second=False):
                e = pair * 2 + odd
                for c in range(6):
                    if first:
                        sp.wait_ge(*released[names[NF + c - RING]])
                    elif c == 0 and second:
                        un.wait_full(sp, "h2T3")
                    elif c == 0:
                        sp.wait_ge(up_full, e * 4 - 7)
                    elif c < 4:
                        sp.wait_ge(up_full, e * 4 - 3 + c)
                    else:
                        sp.wait_ge(dn_full, e * 2 - 1 + c - 4)
                    to, full, _ = expert_slot((pair, odd), c)
                    to = to.rearrange("p (k n) -> p k n", k=KT)
                    if c < 4:
                        src = a["w_up"][0][ds(e, 1), :, c * CW:(c + 1) * CW]
                        sp.dma_start(to, src.rearrange("e (k p) n -> p (e k) n", p=P)).then_inc(full, 16)
                        continue
                    src = a["w_down"][0][ds(e, 1), :, (c - 4) * CW:(c - 3) * CW]
                    src = src.rearrange("e (u h s f) n -> u h f (e s) n", u=2, h=2, s=SUB)
                    for u in range(2):
                        for h in range(2):
                            sp.dma_start(to[h * 64:(h + 1) * 64, u * SUB:(u + 1) * SUB, :],
                                         src[u, h]).then_inc(full, 16)

            expert_chunks(0, 0, first=True)
            expert_chunks(0, 1, second=True)
            with sp.Fori(1, E // 2) as pair:
                for odd in range(2):
                    expert_chunks(pair, odd)
            for tt in range(TT):
                sp.wait_ge(out_ready, 2 * (tt + 1))
                sp.dma_start(out[0, tt * P:(tt + 1) * P, :], xn3[:, tt, :]).then_inc(stored, 16)
            sp.wait_ge(stored, 16 * TT)

        @block.tensor
        def _(pe):
            def arrived(name):
                g = where[name]
                pe.wait_ge(slot_full[g % RING], 16 * (g // RING + 1))
                return g

            def fill(name, steps):
                un.wait_free(pe, name)
                for s in steps:
                    ins = pe.matmul(s[0], s[1], s[2], start=s[3], stop=s[4], skip_group_check=True)
                ins.then_inc(bank_full[un.bank(name)], 1)

            def turn(name, pairs):
                un.wait_free(pe, name)
                for o, i_, idn in pairs:
                    ins = pe.transpose(o, i_, idn)
                ins.then_inc(bank_full[un.bank(name)], 1)

            def bank(name):
                return ps[un.bank(name)]

            def tok_unit(name, w, tt, width=CW, col=0, last=True, first=True):
                o = bank(name)[:, col:col + width]
                return [(o, hT3[:, k, tt * P:(tt + 1) * P], w[:, k, 0:width], k == 0, k == KT - 1) for k in range(KT)]

            def chan_unit(name, w, m0):
                r = []
                for m in range(2):
                    c0 = (m0 + m) * P
                    r += [(bank(name)[:, m * T:(m + 1) * T], w[:, k, c0:c0 + P], hT3[:, k, :], k == 0, k == KT - 1)
                          for k in range(KT)]
                return r

            def ada_part(unit, ms, rows_sb):
                def rows(m):
                    name = f"ar{m}"
                    w = chunk(arrived(f"ada{m}"))
                    fill(name, [(bank(name)[32 * (k % 4):32 * (k % 4) + 32, :], silu_rep[:, k * 32:(k + 1) * 32],
                                 w[:, k, :], k < 4, k >= 4) for k in range(KT)])

                def columns(n, m):
                    un.wait_read(pe, f"ar{m}")
                    if n == 0:
                        un.wait_free(pe, unit)
                    for q in range(4):
                        ins = pe.matmul(bank(unit)[:, 4 * n + q:4 * n + q + 1],
                                        rows_sb[:, m % 2 * CW + q * P:m % 2 * CW + (q + 1) * P],
                                        cst[:, C_SEL:C_SEL + 1], start=True, stop=True, skip_group_check=True)
                    return ins

                pe.wait_ge(silu_ready, 1)
                for n, m in enumerate(ms):
                    rows(m)
                    if n:
                        columns(n - 1, ms[n - 1])
                columns(len(ms) - 1, ms[-1]).then_inc(bank_full[un.bank(unit)], 1)

            pe.wait_ge(ld_cst, 16)
            pe.wait_ge(ld_rows, 96)
            turn("rows", [(bank("rows")[:, 0:R_N], small_rows[:, :], cst[0:R_N, C_ID:C_ID + R_N])])
            for q in range(4):
                if q == 0:
                    pe.wait_ge(xn_ready, 1)
                turn(f"hT{q}", [(ps[q][:, i * T + tt * P:i * T + (tt + 1) * P],
                                 xn3[:, tt, (2 * q + i) * P:(2 * q + i + 1) * P], ident)
                                for i in range(2) for tt in range(TT)])
            ada_part("ada_a", range(4), grow)
            for n in ("sbq", "sbk"):
                g = arrived(n)
                for m in range(2):
                    steps = chan_unit(f"{n}{m}", chunk(g), 2 * m)
                    if n == "sbq" and m == 0:
                        un.wait_free(pe, "sbq0")
                        for k in range(KT - 1):
                            if k % 2 == 0:
                                un.wait_read(pe, f"hT{k // 2}")
                            pe.matmul(steps[k][0], steps[k][1], steps[k][2], start=k == 0, stop=False,
                                      skip_group_check=True)
                        steps = steps[KT - 1:]
                    fill(f"{n}{m}", steps)
            pe.wait_ge(ld_cst, 32)
            g = arrived("sbv")
            for tt in range(TT):
                fill(f"sbv{tt}", tok_unit(f"sbv{tt}", chunk(g), tt))

            def sb_head(h):
                r = slice(h % 2 * HD, h % 2 * HD + HD)
                return sbT[r, h // 2, :], sbT[r, 4 + h // 2, :]

            def sb_scores(h):
                if h == 0:
                    for n in ("sbv0", "sbv1"):
                        un.wait_read(pe, n)
                q, k = sb_head(h)
                z = bank(f"z{h}")
                fill(f"z{h}", [(z[:, 0:T], k[:, 0:P], q, True, True),
                               (z[:, T:TRI], k[:, P:T], q[:, P:T], True, True)])

            def sb_sums(h):
                pe.wait_ge(sb_sp, h + 1)
                sp_ = sbw[:, 6 + h % 2, :]
                c = bank(f"c{h}")
                fill(f"c{h}", [(c[:, 0:T], tri_ge, sp_[:, 0:T], True, False),
                               (c[:, P:T], ones, sp_[:, T:TRI], False, True),
                               (c[:, T:TRI], tri_ge, sp_[:, T:TRI], True, True)])

            def sb_out(h):
                pe.wait_ge(sb_w, h + 1)
                w = sbw[:, 4 + h % 2, :]
                v = [vtok[:, tt, DIL_W + h * HD:DIL_W + (h + 1) * HD] for tt in range(TT)]
                name = f"sbo{h // 2}"
                if h % 2 == 0:
                    un.wait_free(pe, name)
                o = bank(name)[h % 2 * HD:h % 2 * HD + HD, :]
                pe.matmul(o[:, 0:T], v[0], w[:, 0:T], start=True, stop=False, skip_group_check=True)
                ins = pe.matmul(o[:, P:T], v[1], w[:, T:TRI], start=False, stop=True, skip_group_check=True)
                if h % 2:
                    ins.then_inc(bank_full[un.bank(name)], 1)

            dil = [("qk00", "qk0", 0), ("qk01", "qk0", 1), ("qk10", "qk1", 0), ("qk11", "qk1", 1),
                   ("qk20", "qk2", 0), ("qk21", "qk2", 1), ("va00", "va0", 0), ("va01", "va0", 1)]
            for h in range(SB_H + 2):
                if h < len(dil):
                    unit, cname, tt = dil[h]
                    g = arrived(cname)
                    fill(unit, tok_unit(unit, chunk(g), tt))
                elif h == len(dil):
                    g = arrived("va1")
                    w = chunk(g, DIL_W - CW)
                    fill("va1", tok_unit("va1", w, 0, DIL_W - CW) + tok_unit("va1", w, 1, DIL_W - CW, T))
                if h < SB_H:
                    sb_scores(h)
                if 1 <= h <= SB_H:
                    sb_sums(h - 1)
                if h >= 2:
                    sb_out(h - 2)
            pe.wait_ge(rot_done, 1)
            for u in range(6):
                turn(f"qkT{u}", [(bank(f"qkT{u}")[:, i * T + tt * P:i * T + (tt + 1) * P],
                                  qk[:, tt, (2 * u + i) * P:(2 * u + i + 1) * P], ident)
                                 for i in range(2) for tt in range(TT)])

            def gate_unit(n):
                cname = f"gate{n // 2}"
                g = arrived(cname)
                fill(f"g{n}", chan_unit(f"g{n}", chunk(g), 2 * (n % 2)))

            def dil_head(i, g):
                h = g * SLOTS + i
                r = slice(h % 2 * HD, h % 2 * HD + HD)
                return qkT[r, h // 2, :], qkT[r, 6 + h // 2, :]

            for i in range(SLOTS):
                if i == 0:
                    un.wait_read(pe, "qkT4")
                    un.wait_read(pe, "qkT5")
                qk_h = [dil_head(i, g) for g in range(NG)]
                fill(f"s{i}0", [(ps[2][:, g * P:(g + 1) * P], q[:, 0:P], k[:, 0:P], True, True)
                                for g, (q, k) in enumerate(qk_h)])
                fill(f"s{i}1", [(ps[3][:, g * T:(g + 1) * T], q[:, P:T], k, True, True)
                                for g, (q, k) in enumerate(qk_h[0:2])])
                fill(f"s{i}2", [(ps[4][:, 0:T], qk_h[2][0][:, P:T], qk_h[2][1], True, True)])
                gate_unit(2 * i)
                pe.wait_ge(dl_p, i + 1)
                for g in range(NG):
                    b = bank(f"pT{i}{g}")
                    p1 = NG * P + g * T
                    turn(f"pT{i}{g}", [(b[:, 0:P], prob[:, g * P:(g + 1) * P], ident),
                                       (b[:, P:T], prob[:, p1:p1 + P], ident),
                                       (b[:, T:TRI], prob[:, p1 + P:p1 + T], ident)])
                gate_unit(2 * i + 1)
                for g in range(NG):
                    un.wait_read(pe, f"pT{i}{g}")
                name = f"dlo{i // 2}"
                if i % 2 == 0:
                    un.wait_free(pe, name)
                o = bank(name)[i % 2 * HD:i % 2 * HD + HD, :]
                for g in range(NG):
                    h = g * SLOTS + i
                    pe.matmul(o[:, 0:T], vtok[:, 0, h * HD:(h + 1) * HD], probT[:, g, 0:T],
                              start=(g == 0), stop=False, skip_group_check=True)
                    ins = pe.matmul(o[:, P:T], vtok[:, 1, h * HD:(h + 1) * HD], probT[:, g, T:TRI],
                                    start=False, stop=(g == NG - 1), skip_group_check=True)
                if i % 2:
                    ins.then_inc(bank_full[un.bank(name)], 1)

            ga_, gb_ = arrived("wa"), arrived("wb")
            wa, wb = chunk(ga_, D, 2), chunk(gb_, D, 4)
            for n in ("sbo0", "sbo1", "sbo2", "sbo3", "dlo0", "dlo1"):
                un.wait_read(pe, n)
            for m in range(KT):
                b = bank(f"br{m}")
                fill(f"br{m}", [(b[:, 0:T], wa[:, k, m * P:(m + 1) * P],
                                        yaT[:, k * T:(k + 1) * T], k == 0, k == 1) for k in range(2)] +
                            [(b[:, T:2 * T], wb[:, k, m * P:(m + 1) * P],
                              ybT[:, k * T:(k + 1) * T], k == 0, k == 3) for k in range(4)])

            def y_unit(tt, dh):
                w = chunk(arrived(f"wo{dh}"))
                n = f"y{tt}{dh}"
                fill(n, [(bank(n)[:, :], merged[:, k, tt * P:(tt + 1) * P], w[:, k, :], k == 0, k == KT - 1)
                         for k in range(KT)])

            pe.wait_ge(merged_ready, 1)
            y_unit(0, 0)
            y_unit(1, 0)
            ada_part("ada_b", range(4, 10), grow)

            def spread(unit, n, dg, half):
                pe.wait_ge(diag_ready, n)
                fill(unit, [(bank(unit)[:, :], ones, dg[:, half * 512:(half + 1) * 512], True, True)])

            y_unit(0, 1)
            spread("grow1a", 1, diag1, 0)
            spread("grow1b", 1, diag1, 1)
            y_unit(1, 1)
            ada_part("ada_c", range(10, 12), row2)
            pe.wait_ge(x1n_ready, 2)
            for q in range(4):
                turn(f"h2T{q}", [(ps[4 + q][:, i * T + tt * P:i * T + (tt + 1) * P],
                                  xn3[:, tt, (2 * q + i) * P:(2 * q + i + 1) * P], ident)
                                 for i in range(2) for tt in range(TT)])
            pe.wait_ge(ld_small, 64)
            un.wait_free(pe, "lpart")
            for k in range(KT):
                if k % 2 == 0:
                    un.wait_read(pe, f"h2T{k // 2}")
                ins = pe.matmul(ps[2][E * (k % 4):E * (k % 4 + 1), 0:T], w_router_sb[:, k * E:(k + 1) * E], hT3[:, k, :],
                                start=k < 4, stop=k >= 4, skip_group_check=True)
            ins.then_inc(bank_full[2], 1)

            def turn_back(tt):
                for hf in range(2):
                    n = f"hb{tt}{hf}"
                    turn(n, [(bank(n)[:, k * P:(k + 1) * P], hT3[:, 4 * hf + k, tt * P:(tt + 1) * P], ident)
                             for k in range(4)])

            turn_back(0)
            un.wait_read(pe, "lpart")
            fill("logit", [s for tt in range(TT) for s in
                           [(ps[3][:, tt * E:(tt + 1) * E], lpT[:, tt * P:(tt + 1) * P], cst[:, C_STACK:C_STACK + E],
                             True, False),
                            (ps[3][:, tt * E:(tt + 1) * E], cst[0:1, C_ONE:C_ONE + P], b_router_sb[0:1, :],
                             False, True)]])
            turn_back(1)
            pe.wait_ge(sel_ready, 1)
            sel = lg[:, 2, :]
            fill("rank", [(ps[1][:, 0:E], tri_le, sel[:, 0:E], True, True),
                          (ps[1][:, E:2 * E], ones, sel[:, 0:E], True, False),
                          (ps[1][:, E:2 * E], tri_le, sel[:, E:2 * E], False, True),
                          (ps[1][:, 2 * E:3 * E], ones, sel[:, 0:E], True, False),
                          (ps[1][:, 2 * E:3 * E], ones, sel[:, E:2 * E], False, True)])
            spread("grow2a", 2, diag2, 0)
            spread("grow2b", 2, diag2, 1)
            pe.wait_ge(gate_ready, 1)
            turn("gateT", [(ps[2][0:E, tt * P:(tt + 1) * P], gate[:, tt, 0:E], ident) for tt in range(TT)])
            un.wait_read(pe, "gateT")
            for b in range(4):
                tt, dh = b // 2, b % 2
                un.wait_free(pe, f"acc{b}")
                pe.matmul(ps[b][:, :], gT[0:E, tt * P:(tt + 1) * P], b_down_sb[:, dh * 512:(dh + 1) * 512],
                          start=True, stop=True, skip_group_check=True)

            for n in ("hb00", "hb01", "hb10", "hb11"):
                un.wait_read(pe, n)
            un.wait_read(pe, "grow2a")
            un.wait_read(pe, "grow2b")
            pe.wait_ge(cls_ready, 1)

            def gather(b, q, first, end):
                for i in range(2):
                    for tt in range(TT):
                        ins = pe.matmul(ps[b][:, i * T:i * T + end - first], h2[:, tt, (2 * q + i) * P:(2 * q + i + 1) * P],
                                        S[:, tt, first:end], start=(tt == 0), stop=(tt == 1), skip_group_check=True)
                return ins

            pe.wait_ge(s_ready, 1)
            for q in range(4):
                gather(4 + q, q, 0, P).then_inc(xg_full, 1)

            def expert(pair, odd):
                e = pair * 2 + odd
                cls = pe.value_load(cls_i[0:1, ds(e, 1)])

                def body(k):
                    passes = PASSES[k]
                    n_p = len(passes)
                    n = passes[-1][1] + P // passes[-1][0]

                    def groups(bank_, lhsT, rhs, G, first, last):
                        M, W = P // G, CW // G
                        for g in range(G):
                            ins = pe.matmul(bank_[g * M:(g + 1) * M, 0:W], lhsT, rhs[:, g * W:(g + 1) * W],
                                            start=first, stop=last, skip_group_check=True)
                        return ins

                    two = n_p == 2
                    pe.wait_ge(xg_read, 4 * e + 4)
                    for p in range(n_p):
                        for tt in range(TT):
                            ins = pe.transpose(ps[6][:, p * T + tt * P:p * T + (tt + 1) * P],
                                               Sg[:, p, tt * P:(tt + 1) * P], ident)
                    ins.then_inc(gt_full, 1)
                    if two:
                        for q in range(4):
                            if q == 3:
                                pe.wait_ge(xe_read, 4 * e + 1)
                            gather(XE_BANK[q], q, P, n).then_inc(xe_full, 1)
                        pe.wait_ge(xe_read, 4 * e + 4)
                        pe.wait_ge(gt_read, e + 1)
                    else:
                        pe.sem_inc(xe_full, 4)
                    pe.wait_ge(pick_ready, e + 1)
                    for c in range(4):
                        w, full, at = expert_slot((pair, odd), c)
                        w = w.rearrange("p (k n) -> p k n", k=KT)
                        pe.wait_ge(full, at)
                        for p, (G, t0) in enumerate(passes):
                            last = p == n_p - 1
                            if c >= 2:
                                pe.wait_ge(up_read if last else part_read, e * (4 if last else 8) + c - 1)
                            b = ps[(4 if last else 6) + c % 2]
                            groups(b, pick[:, c, 0:P // G], bup[:, :], G, True, False)
                            for kk in range(KT):
                                ins = groups(b, XT[:, kk, t0:t0 + P // G], w[:, kk, :], G, False, kk == KT - 1)
                            ins.then_inc(up_full if last else part_full, 1)
                    pe.wait_ge(s_ready, e + 2)
                    if not two:
                        pe.wait_ge(up_read, 4 * e + 3)
                        pe.wait_ge(gt_read, e + 1)
                        for q in range(2):
                            gather(XG_BANK[0][q], q, 0, P).then_inc(xg_full, 1)
                    pe.wait_ge(act_ready, 8 * e + 4 * n_p)
                    for p, (G, _) in enumerate(passes):
                        last = p == n_p - 1
                        hk = hid[:, p, 0:4 * CW // 2 // G].rearrange("p (n f) -> p n f", f=P)
                        for u in range(2):
                            for q in range(SUB // G):
                                ins = pe.transpose(ps[at_bank(n_p, last, u)][:, q * P:(q + 1) * P],
                                                   hk[:, u * (SUB // G) + q, :], ident)
                            ins.then_inc(at_full if last else part_full, 1)
                    if not two:
                        pe.wait_ge(xg_read, 4 * e + 6)
                        gather(XG_BANK[0][2], 2, 0, P).then_inc(xg_full, 1)
                    pe.wait_ge(at_read, 2 * e + 2)
                    for d in range(2):
                        w, full, at = expert_slot((pair, odd), 4 + d)
                        w = w.rearrange("p (k n) -> p k n", k=KT)
                        pe.wait_ge(full, at)
                        for p, (G, _) in enumerate(passes):
                            last = p == n_p - 1
                            M = P // G
                            b = ps[(4 if last else 6) + d]
                            for kk in range(FT):
                                ins = groups(b, hidT[:, p, kk * M:(kk + 1) * M], w[:, kk, :], G, kk == 0, kk == FT - 1)
                            ins.then_inc(dn_full if last else part_full, 1)
                    if two:
                        pe.wait_ge(part_read, 8 * e + 8)
                        for q in range(2):
                            gather(XG_BANK[1][q], q, 0, P).then_inc(xg_full, 1)
                    else:
                        gather(XG_BANK[0][3], 3, 0, P).then_inc(xg_full, 1)
                    pe.wait_ge(dn_read, 2 * e + 2)
                    for p, (G, _) in enumerate(passes):
                        W = CW // G
                        for g in range(G):
                            for tt in range(TT):
                                gates_ = (GT[:, p, :] if G == 1 else GTg[G][:, g, :])[:, tt * P:(tt + 1) * P]
                                for d in range(2):
                                    ins = pe.matmul(ps[2 * tt + d][:, g * W:(g + 1) * W], gates_,
                                                    Y[:, p, d * W:(d + 1) * W],
                                                    start=False, stop=True, skip_group_check=True)
                    ins.then_inc(acc_done, 1)
                    if two:
                        for q in range(2, 4):
                            gather(XG_BANK[1][q], q, 0, P).then_inc(xg_full, 1)
                    if n_p == 1:
                        pe.sem_inc(part_full, 8)

                by_class(pe, cls, body)

            with pe.Fori(0, E // 2) as pair:
                for odd in range(2):
                    expert(pair, odd)

        @block.scalar
        def _(act):
            for tt in range(TT):
                act.dma_start(pos_i[:, tt:tt + 1], a["positions"][0, tt * P:(tt + 1) * P].rearrange(
                    "(p o) -> p o", o=1)).then_inc(ld_pos, 16)

            act.wait_ge(ld_x, 16)
            n_sq = [0]

            def root_mean_square(src, tt, dst, junk):
                n_sq[0] += 1
                act.activation(junk, src, ACT.Square, accum_out=small[:, dst + tt:dst + tt + 1]).then_inc(sq_ready, 1)
                act.wait_ge(sq_ready, n_sq[0])
                act.activation(small[:, dst + tt:dst + tt + 1], small[:, dst + tt:dst + tt + 1], ACT.Sqrt,
                               scale=1.0 / D, bias=cst[:, C_EPS:C_EPS + 1]).then_inc(rms_ready, 1)

            act.wait_ge(ld_cst, 16)
            for tt in range(TT):
                root_mean_square(x3[:, tt, :], tt, 18, qk[:, tt, 0:D])
            un.wait_read(act, "rows")
            act.activation(small[:, 8:16], cols[:, R_C:R_C + KT], ACT.Exp, scale=-1.0).then_inc(ec_ready, 1)
            act.wait_ge(ang_ready, 1)
            act.activation(rope[:, 4 * 16:6 * 16], rope[:, 2 * 16:4 * 16], ACT.Sin).then_inc(rope_ready, 1)

            def copy_out(name, dst, src=None):
                un.wait_full(act, name)
                b = ps[un.bank(name)]
                ins = act.activation(dst, b[:, :] if src is None else src, ACT.Copy)
                ins.then_inc(bank_free[un.bank(name)], 1)

            def two(ap):
                return ap.rearrange("p a b -> p (a b)")

            def ada_rows(ms, to):
                for m in ms:
                    copy_out(f"ar{m}", to[:, m % 2 * CW:(m % 2 + 1) * CW])

            ada_rows(range(4), grow)
            act.dma_start(cst[:, C_FIRST:], a["cst"][:, C_FIRST:]).then_inc(ld_cst, 16)
            act.dma_start(bup[:, :], a["b_up"][0].rearrange("e (c n) -> (e c) n", c=4)).then_inc(ld_small, 16)
            act.dma_start(w_router_sb[:, :].rearrange("p (k n) -> p k n", k=KT),
                          a["w_router"][0].rearrange("(k p) n -> p k n", p=P)).then_inc(ld_small, 16)
            act.dma_start(b_router_sb[:, :], a["b_router"]).then_inc(ld_small, 16)
            act.dma_start(b_down_sb[:, :], a["b_down"][0]).then_inc(ld_small, 16)
            for m in range(2):
                copy_out(f"sbq{m}", two(sbT[:, 2 * m:2 * m + 2, :]))
            for m in range(2):
                copy_out(f"sbk{m}", two(sbT[:, 4 + 2 * m:6 + 2 * m, :]))
            for tt in range(TT):
                copy_out(f"sbv{tt}", vtok[:, tt, DIL_W:DIL_W + SB_W])

            def sb_exp(h):
                act.wait_ge(sb_na, h + 1)
                act.activation(sbw[:, 2 + h % 2, :], sbw[:, h % 2, :], ACT.Exp).then_inc(sb_e, 1)
                act.wait_ge(sb_e, h + 1)
                act.activation(sbw[:, h % 2, :], sbw[:, 2 + h % 2, :], ACT.Ln, bias=1.0).then_inc(sb_ln, 1)

            def sb_weights(h):
                act.wait_ge(sb_l, h + 1)
                act.activation(sbw[:, 4 + h % 2, :], sbw[:, 8 + h % 2, :], ACT.Exp).then_inc(sb_w, 1)

            def sb_copy(p):
                copy_out(f"sbo{p}", ybT[:, p * T:(p + 1) * T], ps[un.bank(f"sbo{p}")][:, 0:T])

            dil = [("qk00", 0, 0), ("qk01", 1, 0), ("qk10", 0, 1), ("qk11", 1, 1), ("qk20", 0, 2), ("qk21", 1, 2),
                   ("va00", 0, 3), ("va01", 1, 3)]
            for h in range(SB_H + 2):
                if h < len(dil):
                    n, tt, c = dil[h]
                    dst = qk[:, tt, c * CW:(c + 1) * CW] if c < 3 else vtok[:, tt, 0:CW]
                    copy_out(n, dst)
                elif h == len(dil):
                    copy_out("va1", vtok[:, :, CW:DIL_W], ps[un.bank("va1")][:, :].rearrange("p (t n) -> p t n", t=TT))
                if h < SB_H:
                    sb_exp(h)
                if 1 <= h <= SB_H:
                    sb_weights(h - 1)
                if h >= 2 and h % 2 == 1:
                    sb_copy((h - 2) // 2)
            for u in range(6):
                copy_out(f"qkT{u}", two(qkT[:, 2 * u:2 * u + 2, :]))

            def gate_copy(n):
                copy_out(f"g{n}", two(gates[:, 2 * n:2 * n + 2, :]))

            for i in range(SLOTS):
                act.wait_ge(dl_max, i + 1)
                act.activation(prob[:, 0:NG * P], prob[:, 0:NG * P], ACT.Exp, bias=small[:, 26:27], scale=SCALE,
                               accum_out=small[:, 28:29]).then_inc(dl_exp, 1)
                act.activation(prob[:, NG * P:], prob[:, NG * P:], ACT.Exp, bias=small[:, 27:28], scale=SCALE,
                               accum_out=small[:, 29:30]).then_inc(dl_exp, 1)
                gate_copy(2 * i)
                for g in range(NG):
                    copy_out(f"pT{i}{g}", probT[:, g, :], ps[un.bank(f"pT{i}{g}")][:, 0:TRI])
                gate_copy(2 * i + 1)
                if i % 2:
                    p = i // 2
                    copy_out(f"dlo{p}", yaT[:, p * T:(p + 1) * T], ps[un.bank(f"dlo{p}")][:, 0:T])
            un.wait_read(act, "g7")
            for q in range(4):
                act.activation(two(gates[:, 4 * q:4 * q + 4, :]), two(gates[:, 4 * q:4 * q + 4, :]),
                               ACT.Sigmoid).then_inc(sig_ready, 1)
            ada_rows(range(4, 10), grow)
            copy_out("grow1a", grow[:, 0:512])
            copy_out("grow1b", grow[:, 512:D])
            for tt in range(TT):
                for dh in range(2):
                    un.wait_full(act, f"y{tt}{dh}")
                root_mean_square(psum[:, 2 * tt * 512:(2 * tt + 2) * 512], tt, 38, junk(tt))
                if tt == 1:
                    ada_rows(range(10, 11), row2)
                act.wait_ge(x1_ready, 2 * tt + 2)
                root_mean_square(x3[:, tt, :], tt, 42, junk(tt))
            ada_rows(range(11, 12), row2)
            copy_out("lpart", lpT, ps[2][:, 0:T])
            act.wait_ge(lmax_ready, 1)
            for tt in range(TT):
                act.activation(lg[:, 1, tt * E:(tt + 1) * E], lg[:, 0, tt * E:(tt + 1) * E], ACT.Exp,
                               bias=small[:, 50 + tt:51 + tt]).then_inc(lexp_ready, 1)
            for tt in range(TT):
                for hf in range(2):
                    copy_out(f"hb{tt}{hf}", h2[:, tt, hf * 512:(hf + 1) * 512])
            act.wait_ge(x1_ready, 4)
            copy_out("grow2a", grow[:, 0:512])
            copy_out("grow2b", grow[:, 512:D])
            copy_out("gateT", gT[0:E, :], ps[un.bank("gateT")][0:E, 0:T])

            def rows_out(b, q, first, end):
                return act.activation(XT[:, 2 * q:2 * q + 2, first:end],
                                      ps[b][:, :].rearrange("p (i t) -> p i t", i=2)[:, :, 0:end - first], ACT.Copy)

            act.wait_ge(cls_ready, 1)
            for q in range(4):
                act.wait_ge(xg_full, q + 1)
                rows_out(4 + q, q, 0, P).then_inc(xg_read, 1)
            act.wait_ge(gt_zero, 1)
            with act.Fori(0, E) as e:
                cls = act.value_load(cls_i[0:1, ds(e, 1)])

                def body(k):
                    passes = PASSES[k]
                    n_p = len(passes)
                    n = passes[-1][1] + P // passes[-1][0]
                    act.wait_ge(gt_full, e + 1)
                    for p, (G, _) in enumerate(passes):
                        for g in range(G):
                            r = slice(g * P // G, (g + 1) * P // G)
                            ins = act.activation(GT[:, p, :] if G == 1 else GTg[G][r, g, :],
                                                 ps[6][r, p * T:(p + 1) * T], ACT.Copy)
                    ins.then_inc(gt_read, 1)
                    if n_p == 2:
                        for q in range(4):
                            act.wait_ge(xe_full, 4 * e + q + 1)
                            rows_out(XE_BANK[q], q, P, n).then_inc(xe_read, 1)
                    else:
                        act.wait_ge(xe_full, 4 * e + 4)
                        act.sem_inc(xe_read, 4)
                    for j in range(4 * n_p):
                        h = CW // 2 // passes[j % n_p][0]
                        act.wait_ge(g_ready, 8 * e + j + 1)
                        act.activation(xw[:, 4 + j % 2, 0:h], xw[:, j % 2, 0:h], ACT.Sigmoid,
                                       scale=ALPHA).then_inc(sg_ready, 1)
                    for q in range(4):
                        act.wait_ge(xg_full, 4 * e + q + 5)
                        rows_out(XG_BANK[n_p - 1][q], q, 0, P).then_inc(xg_read, 1)
                    if n_p == 1:
                        act.wait_ge(sg_ready, 8 * e + 4)
                        act.sem_inc(sg_ready, 4)

                by_class(act, cls, body)

            act.wait_ge(acc_done, E)
            for tt in range(TT):
                root_mean_square(psum[:, 2 * tt * 512:(2 * tt + 2) * 512], tt, 46, junk(tt))

        @block.vector
        def _(v):
            n_chain = [0]

            def link(ins):
                n_chain[0] += 1
                ins.then_inc(chain, 1)
                v.wait_ge(chain, n_chain[0])

            def rstd(dst, n):
                v.wait_ge(rms_ready, 2 * n)
                link(v.reciprocal(dst, dst))

            un.wait_full(v, "rows")
            ins = v.tensor_copy(cols[:, :], ps[7][:, 0:R_N])
            ins.then_inc(bank_free[7], 1)
            un.wait_read(v, "rows")
            rstd(small[:, 18:20], 1)
            for tt in range(TT):
                ins = v.tensor_scalar(xn3[:, tt, :], x3[:, tt, :], small[:, 18 + tt:19 + tt], None, ALU.mult)
            link(ins)
            v.sem_inc(xn_ready, 1)
            v.wait_ge(ec_ready, 1)
            link(v.tensor_scalar(small[:, 8:16], small[:, 8:16], 1.0, None, ALU.add))
            link(v.reciprocal(small[:, 8:16], small[:, 8:16]))
            link(v.tensor_tensor(small[:, 0:8], small[:, 8:16], cols[:, R_C:R_C + KT], ALU.mult))
            v.tensor_copy(silu_rep[:, :].rearrange("p (k r) -> p k r", k=KT),
                          small[:, 0:8].rearrange("p (k r) -> p k r", r=1).broadcast_to([P, KT, 32])
                          ).then_inc(silu_ready, 1)
            v.wait_ge(ld_pos, 16 * TT)
            v.wait_ge(ld_cst, 16)
            n = TT * HALF
            link(v.tensor_copy(small[:, 20:22], pos_i[:, :]))
            ang, turns, arg = rope[:, 0:n], rope[:, n:2 * n], rope[:, 2 * n:4 * n]
            for tt in range(TT):
                ins = v.tensor_scalar(ang[:, tt * HALF:(tt + 1) * HALF], cst[:, C_FREQ:C_FREQ + HALF],
                                      small[:, 20 + tt:21 + tt], None, ALU.mult)
            link(ins)
            c1, c2, c3 = two_pi_parts()
            magic = 1.5 * 2.0 ** 23
            for q, (quarter, add) in enumerate(((0.0, 0.0), (0.25, float(np.pi / 2)))):
                to = arg[:, q * n:(q + 1) * n]
                link(v.tensor_scalar(turns, ang, float(1 / (2 * np.pi)), quarter, ALU.mult, ALU.add))
                link(v.tensor_scalar(turns, turns, magic, None, ALU.add))
                link(v.tensor_scalar(turns, turns, magic, None, ALU.subtract))
                link(v.scalar_tensor_tensor(out=to, in0=turns, scalar=-c1, in1=ang, op0=ALU.mult, op1=ALU.add))
                link(v.scalar_tensor_tensor(out=to, in0=turns, scalar=-c2, in1=to, op0=ALU.mult, op1=ALU.add))
                link(v.scalar_tensor_tensor(out=to, in0=turns, scalar=-c3, in1=to, op0=ALU.mult, op1=ALU.add))
                link(v.tensor_scalar(to, to, add, 3.1415925, ALU.add, ALU.min))
                link(v.tensor_scalar(to, to, -3.1415925, None, ALU.max))
            v.sem_inc(ang_ready, 1)

            def mod_part(unit, m0, m1):
                un.wait_full(v, unit)
                ins = v.tensor_tensor(mod[:, m0:m1], ps[un.bank(unit)][:, 0:m1 - m0], cols[:, m0:m1], ALU.add)
                ins.then_inc(bank_free[un.bank(unit)], 1)
                un.wait_read(v, unit)

            def scale_cols(dst, m0, gain):
                link(v.scalar_tensor_tensor(out=small[:, dst:dst + KT], in0=mod[:, m0:m0 + KT], scalar=1.0,
                                            in1=cols[:, R_G + gain * KT:R_G + (gain + 1) * KT],
                                            op0=ALU.add, op1=ALU.mult))

            mod_part("ada_a", 0, 16)
            scale_cols(64, 8, 0)
            for q in range(4):
                un.wait_full(v, f"hT{q}")
                for i in range(2):
                    k = 2 * q + i
                    ins = v.tensor_scalar(hT3[:, k, :], ps[q][:, i * T:(i + 1) * T], small[:, 64 + k:65 + k],
                                          mod[:, k:k + 1], ALU.mult, ALU.add)
                ins.then_inc(bank_free[q], 1)

            def blocks(ap):
                return ap[:, 0:P], ap[:, T:TRI]

            def sb_first(h):
                un.wait_full(v, f"z{h}")
                z = ps[un.bank(f"z{h}")][:, 0:TRI]
                if h >= 2:
                    v.wait_ge(sb_w, h - 1)
                zs = sbw[:, 8 + h % 2, :]
                v.tensor_scalar(zs, z, SCALE, None, ALU.mult).then_inc(bank_free[un.bank(f"z{h}")], 1)
                un.wait_read(v, f"z{h}")
                v.scalar_tensor_tensor(out=sbw[:, h % 2, :], in0=zs, scalar=-1.0, in1=zs, op0=ALU.mult,
                                       op1=ALU.min).then_inc(sb_na, 1)
                link(v.tensor_scalar(sbw[:, 6 + h % 2, :], zs, 0.0, None, ALU.max))

            def sb_second(h):
                v.wait_ge(sb_ln, h + 1)
                s = sbw[:, 6 + h % 2, :]
                link(v.tensor_tensor(s, s, sbw[:, h % 2, :], ALU.add))
                for d_ in blocks(s):
                    ins = v.tensor_tensor(d_, d_, cst[:, C_ST:C_ST + P], ALU.mult)
                link(ins)
                v.sem_inc(sb_sp, 1)

            def sb_third(h):
                un.wait_full(v, f"c{h}")
                L = sbw[:, 8 + h % 2, :]
                ins = v.tensor_tensor(L, L, ps[un.bank(f"c{h}")][:, 0:TRI], ALU.subtract)
                ins.then_inc(bank_free[un.bank(f"c{h}")], 1)
                un.wait_read(v, f"c{h}")
                for d_ in blocks(L):
                    ins = v.tensor_tensor(d_, d_, cst[:, C_NG:C_NG + P], ALU.add)
                link(ins)
                v.sem_inc(sb_l, 1)

            for h in range(SB_H + 1):
                if h < SB_H:
                    sb_first(h)
                if h >= 1:
                    sb_third(h - 1)
                if h < SB_H:
                    sb_second(h)

            v.wait_ge(rope_ready, 1)
            un.wait_read(v, "qk20")
            un.wait_read(v, "qk21")
            nh = 2 * NG * SLOTS
            for tt in range(TT):
                q4 = qk[:, tt, :].rearrange("p (h d) -> p h d", h=nh)
                t1, t2 = q4[:, :, 0:HALF], q4[:, :, HALF:2 * HALF]
                sin = rope[:, 4 * n + tt * HALF:4 * n + (tt + 1) * HALF]
                cos = rope[:, 5 * n + tt * HALF:5 * n + (tt + 1) * HALF]
                sin = sin.rearrange("p (o d) -> p o d", o=1).broadcast_to([P, nh, HALF])
                cos = cos.rearrange("p (o d) -> p o d", o=1).broadcast_to([P, nh, HALF])
                w = [xn[:, k * nh * HALF:(k + 1) * nh * HALF].rearrange("p (h d) -> p h d", h=nh) for k in range(4)]
                v.tensor_tensor(w[0], t1, cos, ALU.mult)
                v.tensor_tensor(w[1], t2, sin, ALU.mult)
                v.tensor_tensor(w[2], t2, cos, ALU.mult)
                link(v.tensor_tensor(w[3], t1, sin, ALU.mult))
                v.tensor_tensor(t1, w[0], w[1], ALU.subtract)
                link(v.tensor_tensor(t2, w[2], w[3], ALU.add))
            v.sem_inc(rot_done, 1)

            for i in range(SLOTS):
                if i > 0:
                    for g in range(NG):
                        un.wait_read(v, f"pT{i - 1}{g}")
                c = C_MASK
                un.wait_full(v, f"s{i}0")
                ins = v.tensor_tensor_reduce(out=prob[:, 0:TRI], in0=ps[2][:, 0:TRI], in1=cst[:, c:c + TRI],
                                             scale=1.0, scalar=-3e38, op0=ALU.add, op1=ALU.max,
                                             accum_out=small[:, 24:25])
                ins.then_inc(bank_free[2], 1)
                un.wait_full(v, f"s{i}1")
                ins = v.tensor_tensor_reduce(out=prob[:, TRI:TRI + 2 * T], in0=ps[3][:, :],
                                             in1=cst[:, c + TRI:c + TRI + 2 * T], scale=1.0, scalar=-3e38,
                                             op0=ALU.add, op1=ALU.max, accum_out=small[:, 30:31])
                ins.then_inc(bank_free[3], 1)
                un.wait_read(v, f"s{i}1")
                un.wait_full(v, f"s{i}2")
                ins = v.tensor_tensor_reduce(out=prob[:, TRI + 2 * T:TRI + 3 * T], in0=ps[4][:, 0:T],
                                             in1=cst[:, c + TRI + 2 * T:c + TRI + 3 * T], scale=1.0,
                                             scalar=small[:, 30:31], op0=ALU.add, op1=ALU.max,
                                             accum_out=small[:, 25:26])
                ins.then_inc(bank_free[4], 1)
                un.wait_read(v, f"s{i}0")
                un.wait_read(v, f"s{i}2")
                link(v.tensor_scalar(small[:, 26:28], small[:, 24:26], -SCALE, None, ALU.mult))
                v.sem_inc(dl_max, 1)
                v.wait_ge(dl_exp, 2 * (i + 1))
                link(v.reciprocal(small[:, 22:24], small[:, 28:30]))
                v.tensor_scalar(prob[:, 0:TRI], prob[:, 0:TRI], small[:, 22:23], None, ALU.mult)
                link(v.tensor_scalar(prob[:, TRI:], prob[:, TRI:], small[:, 23:24], None, ALU.mult))
                v.sem_inc(dl_p, 1)

            v.wait_ge(sig_ready, 4)
            for m in range(KT):
                un.wait_full(v, f"br{m}")
                b = ps[un.bank(f"br{m}")]
                v.tensor_tensor(brw[:, 2 * (m % 2), :], b[:, 0:T], gates[:, m, :], ALU.mult)
                ins = v.tensor_tensor(brw[:, 2 * (m % 2) + 1, :], b[:, T:2 * T], gates[:, KT + m, :], ALU.mult)
                ins.then_inc(bank_free[un.bank(f"br{m}")], 1)
                un.wait_read(v, f"br{m}")
                ins = v.tensor_tensor(merged[:, m, :], brw[:, 2 * (m % 2), :], brw[:, 2 * (m % 2) + 1, :], ALU.add)
            link(ins)
            v.sem_inc(merged_ready, 1)

            def diagonals(dst, m0, gain, wait=None):
                link(v.tensor_tensor(small[:, 80:88], mod[:, m0:m0 + KT],
                                     cols[:, R_G + gain * KT:R_G + (gain + 1) * KT], ALU.mult))
                for k in range(KT):
                    ins = v.tensor_scalar(dst[:, k * P:(k + 1) * P], ident, small[:, 80 + k:81 + k], None, ALU.mult)
                link(ins)
                v.sem_inc(diag_ready, 1)

            mod_part("ada_b", 16, 40)
            un.wait_full(v, "g7")
            diagonals(diag1, 16, 1)
            scale_cols(72, 32, 2)

            un.wait_read(v, "grow1a")
            un.wait_read(v, "grow1b")
            for tt in range(TT):
                v.wait_ge(rms_ready, 3 + 2 * tt)
                link(v.reciprocal(small[:, 38 + tt:39 + tt], small[:, 38 + tt:39 + tt]))
                for dh in range(2):
                    n_ = f"y{tt}{dh}"
                    w = xn3[:, tt, dh * 512:(dh + 1) * 512]
                    ins = v.scalar_tensor_tensor(out=w, in0=ps[un.bank(n_)][:, :], scalar=small[:, 38 + tt:39 + tt],
                                                 in1=grow[:, dh * 512:(dh + 1) * 512], op0=ALU.mult, op1=ALU.mult)
                    ins.then_inc(bank_free[un.bank(n_)], 1)
                    un.wait_read(v, n_)
                    r = x3[:, tt, dh * 512:(dh + 1) * 512]
                    link(v.tensor_tensor(r, r, w, ALU.add))
                    v.sem_inc(x1_ready, 1)
                v.wait_ge(rms_ready, 4 + 2 * tt)
                link(v.reciprocal(small[:, 42 + tt:43 + tt], small[:, 42 + tt:43 + tt]))
                v.tensor_scalar(xn3[:, tt, :], x3[:, tt, :], small[:, 42 + tt:43 + tt], None,
                                ALU.mult).then_inc(x1n_ready, 1)
            for q in range(4):
                un.wait_full(v, f"h2T{q}")
                for i in range(2):
                    k = 2 * q + i
                    ins = v.tensor_scalar(hT3[:, k, :], ps[4 + q][:, i * T:(i + 1) * T], small[:, 72 + k:73 + k],
                                          mod[:, 24 + k:25 + k], ALU.mult, ALU.add)
                ins.then_inc(bank_free[4 + q], 1)

            mod_part("ada_c", 40, 48)
            diagonals(diag2, 40, 3)

            un.wait_full(v, "logit")
            logit, expl, sel, rest = lg[:, 0, :], lg[:, 1, :], lg[:, 2, :], lg[:, 3, :]
            ins = v.tensor_copy(logit, ps[3][:, 0:TT * E])
            ins.then_inc(bank_free[3], 1)
            un.wait_read(v, "logit")
            for tt in range(TT):
                ins = v.max(top[:, tt, :], logit[:, tt * E:(tt + 1) * E])
            link(ins)
            link(v.tensor_scalar(small[:, 50:52], top[:, :, 0:1].rearrange("p a b -> p (a b)"), -1.0, None, ALU.mult))
            v.sem_inc(lmax_ready, 1)
            link(v.memset(top[:, :, TOPK:8], 3e38))
            for tt in range(TT):
                ins = v.match_replace(out=rest[:, tt * E:(tt + 1) * E], in_to_replace=top[:, tt, :],
                                      in_values=logit[:, tt * E:(tt + 1) * E], imm_value=-3e38)
            link(ins)
            link(v.tensor_tensor(sel, rest, logit, ALU.not_equal))
            v.sem_inc(sel_ready, 1)
            v.wait_ge(lexp_ready, 2)
            link(v.tensor_tensor(expl, expl, sel, ALU.mult))
            link(v.tensor_reduce(small[:, 52:54], expl.rearrange("p (t e) -> p t e", t=TT), AX_X, ALU.add))
            link(v.reciprocal(small[:, 54:56], small[:, 52:54]))
            link(v.memset(arena[:, 14336:14336 + 4 * (E + 1)], 0.0))
            link(v.memset(posm2, 0.0))
            for tt in range(TT):
                ins = v.tensor_scalar(gate[:, tt, 0:E], expl[:, tt * E:(tt + 1) * E], small[:, 54 + tt:55 + tt], None,
                                      ALU.mult)
            link(ins)
            v.sem_inc(gate_ready, 1)
            un.wait_full(v, "rank")
            for tt in range(TT):
                ins = v.tensor_tensor(lg[:, 4, tt * E:(tt + 1) * E], ps[1][:, tt * E:(tt + 1) * E],
                                      sel[:, tt * E:(tt + 1) * E], ALU.mult)
            ins = v.tensor_copy(lg[:, 5, 0:E], ps[1][:, 2 * E:3 * E])
            ins.then_inc(bank_free[1], 1)
            un.wait_read(v, "rank")
            for tt in range(TT):
                v.tensor_scalar(posm[:, tt, 0:E], lg[:, 4, tt * E:(tt + 1) * E], -1.0, None, ALU.add)
                v.tensor_scalar(posm2[:, tt, 0:E], lg[:, 4, tt * E:(tt + 1) * E], -1.0 - P, None, ALU.add)
            link(v.memset(lg[:, 6, 0:E + 1], 0.0))
            for least in CLASS_FROM:
                link(v.scalar_tensor_tensor(out=lg[:, 6, 0:E], in0=lg[:, 5, 0:E], scalar=least - 0.5,
                                            in1=lg[:, 6, 0:E], op0=ALU.is_ge, op1=ALU.add))
            v.tensor_copy(cls_i[:, :], lg[:, 6, 0:E + 1]).then_inc(cls_ready, 1)


            def one_hot(e, cls):
                for tt in range(TT):
                    ins = v.tensor_scalar(S[:, tt, :], iota, posm[:, tt, ds(e, 1)], None, ALU.is_equal)

                def gated(k):
                    for p, (G, t0) in enumerate(PASSES[k]):
                        slots = cst[:, {1: C_IOTA, 2: C_I64, 4: C_I32}[G]:][:, 0:P]
                        for tt in range(TT):
                            ins = v.tensor_scalar(Sg[:, p, tt * P:(tt + 1) * P], slots,
                                                  (posm2 if t0 else posm)[:, tt, ds(e, 1)],
                                                  gate[:, tt, ds(e, 1)], ALU.is_equal, ALU.mult)
                    ins.then_inc(s_ready, 1)

                by_class(v, cls, gated)

            v.wait_ge(cls_ready, 1)
            one_hot(0, v.value_load(cls_i[0:1, 0:1]))
            un.wait_full(v, "hb11")
            v.memset(hT[:, 0:6 * T], 0.0).then_inc(gt_zero, 1)
            v.wait_ge(ld_small, 64)
            with v.Fori(0, E) as e:
                cls = v.value_load(cls_i[0:1, ds(e, 1)])
                v.wait_ge(xg_full, 4 * e + 1)
                v.tensor_copy(pick, ident[:, ds(e * 4, 4)].rearrange("p (c m) -> p c m", m=1).broadcast_to(
                    [P, 4, P])).then_inc(pick_ready, 1)
                v.wait_ge(xg_full, 4 * e + 4)
                v.wait_ge(gt_full, e + 1)
                v.wait_ge(xe_full, 4 * e + 4)
                one_hot(e + 1, v.value_load(cls_i[0:1, ds(e + 1, 1)]))

                def body(k):
                    passes = PASSES[k]
                    n_p = len(passes)

                    def clamped(j):
                        c, p = j // n_p, j % n_p
                        last = p == n_p - 1
                        W = CW // passes[p][0]
                        if j >= 2:
                            v.wait_ge(act_ready, 8 * e + j - 1)
                        v.wait_ge(up_full if last else part_full, e * (4 if last else 8) + c + 1)
                        b = ps[(4 if last else 6) + c % 2][:, 0:W].rearrange("p (n two) -> p two n", two=2)
                        v.tensor_scalar(xw[:, j % 2, 0:W // 2], b[:, 0, :], LIMIT, None, ALU.min).then_inc(g_ready, 1)
                        v.tensor_scalar(xw[:, 2 + j % 2, 0:W // 2], b[:, 1, :], LIMIT, -LIMIT, ALU.min,
                                        ALU.max).then_inc(up_read if last else part_read, 1)

                    def finish(j):
                        c, p = j // n_p, j % n_p
                        h = CW // 2 // passes[p][0]
                        v.wait_ge(sg_ready, 8 * e + j + 1)
                        v.tensor_tensor(xw[:, 6 + j % 2, 0:h], xw[:, j % 2, 0:h], xw[:, 4 + j % 2, 0:h],
                                        ALU.mult).then_inc(m_ready, 1)
                        v.wait_ge(m_ready, 8 * e + j + 1)
                        to = hid[:, p, c // 2 * 2 * h:(c // 2 + 1) * 2 * h].rearrange("p (q c f) -> p q c f", c=2, f=64)
                        v.scalar_tensor_tensor(out=to[:, :, c % 2, :],
                                               in0=xw[:, 2 + j % 2, 0:h].rearrange("p (q f) -> p q f", f=64), scalar=1.0,
                                               in1=xw[:, 6 + j % 2, 0:h].rearrange("p (q f) -> p q f", f=64),
                                               op0=ALU.add, op1=ALU.mult).then_inc(act_ready, 1)

                    for j in range(4 * n_p + 1):
                        if j < 4 * n_p:
                            clamped(j)
                        if j >= 1:
                            finish(j - 1)
                    if n_p == 1:
                        v.wait_ge(act_ready, 8 * e + 4)
                        for s_ in (g_ready, m_ready, act_ready):
                            v.sem_inc(s_, 4)
                    for p, (G, _) in enumerate(passes):
                        last = p == n_p - 1
                        M, Q = P // G, SUB // G
                        for u in range(2):
                            v.wait_ge(at_full if last else part_full, e * (2 if last else 8) + u + (1 if last else 5))
                            v.tensor_copy(
                                hidT[:, p, u * 4 * M:(u + 1) * 4 * M].rearrange("p (g q t) -> p q g t", g=G, q=Q),
                                ps[at_bank(n_p, last, u)][:, 0:Q * P].rearrange("p (q g t) -> p q g t", q=Q, g=G)
                            ).then_inc(at_read if last else part_read, 1)
                    for d in range(2):
                        for p, (G, _) in enumerate(passes):
                            last = p == n_p - 1
                            W = CW // G
                            v.wait_ge(dn_full if last else part_full, e * (2 if last else 8) + d + (1 if last else 7))
                            v.tensor_copy(Y[:, p, d * W:(d + 1) * W], ps[(4 if last else 6) + d][:, 0:W]).then_inc(
                                dn_read if last else part_read, 1)
                    if n_p == 1:
                        v.sem_inc(part_read, 8)

                by_class(v, cls, body)

            rstd(small[:, 46:48], 4)
            un.wait_read(v, "grow2a")
            un.wait_read(v, "grow2b")
            for tt in range(TT):
                for dh in range(2):
                    w = xn3[:, tt, dh * 512:(dh + 1) * 512]
                    link(v.scalar_tensor_tensor(out=w, in0=ps[2 * tt + dh][:, :], scalar=small[:, 46 + tt:47 + tt],
                                                in1=grow[:, dh * 512:(dh + 1) * 512], op0=ALU.mult, op1=ALU.mult))
                    v.tensor_tensor(w, w, x3[:, tt, dh * 512:(dh + 1) * 512], ALU.add).then_inc(out_ready, 1)


_OUT = (1, T, D)


def kernel(**inputs):
    import concourse.bacc as _bacc
    from concourse.bass_utils import run_bass_kernel_spmd as _run

    nc = _bacc.Bacc("TRN2", target_bir_lowering=False, num_devices=1)
    arrays, a = {}, {}
    for name, value in list(inputs.items()) + [("cst", constants())]:
        v = np.ascontiguousarray(value)
        arrays[f"in_{name}"] = v
        a[name] = nc.dram_tensor(f"in_{name}", v.shape, mybir.dt.from_np(v.dtype), kind="ExternalInput").ap()
    out = nc.dram_tensor("out_0", _OUT, F32, kind="ExternalOutput").ap()
    layer_kernel(nc, a, out)
    r = _run(nc, [arrays], core_ids=[0])
    return r.results[0]["out_0"]
```
